# Optimizing a Trainium2 kernel written in Bass

```python
import math
import jax, jax.numpy as jnp
from jax import lax
import numpy as np

D_MODEL = 1024
BATCH = 1
SEQ = 256
DEPTH = 1

POOL_WINDOWS = (2, 4, 8, 16)
POOL_GROUPS = len(POOL_WINDOWS)
POOL_GROUP_DIM = D_MODEL // 8
POOL_WIDTH = POOL_GROUPS * POOL_GROUP_DIM
DN_HEAD_DIM = 128
DN_HEADS = D_MODEL // 128
DN_WIDTH = DN_HEADS * DN_HEAD_DIM
CONV_WIDTH = 4
CHUNK = 64
FFN_HIDDEN = ((8 * D_MODEL // 3) + 127) // 128 * 128
N_SUBLAYERS = 3
RMS_EPS = 1e-6
L2_EPS = 1e-6
MIX_IN_SIZES = (POOL_WIDTH, DN_WIDTH, DN_WIDTH, DN_WIDTH, DN_WIDTH, DN_HEADS, DN_HEADS, D_MODEL, D_MODEL)
MIX_IN_WIDTH = int(sum(MIX_IN_SIZES))
MIX_IN_SPLITS = tuple(int(s) for s in np.cumsum(MIX_IN_SIZES)[:-1])


def rms_norm(x, g):
    xf = x.astype(jnp.float32)
    xf = xf * lax.rsqrt(jnp.mean(xf * xf, axis=-1, keepdims=True) + RMS_EPS)
    return (xf * g.astype(jnp.float32)).astype(x.dtype)

def l2_normalize(x):
    return x * lax.rsqrt(jnp.sum(x * x, axis=-1, keepdims=True) + L2_EPS)

def modulate(h, shift, scale):
    return h * (1.0 + scale[:, None, :]) + shift[:, None, :]

def swiglu(h, w_in, w_out):
    gate, up = jnp.split(h @ w_in, 2, axis=-1)
    return (jax.nn.silu(gate) * up) @ w_out

def causal_depthwise_conv(x, w):
    C = x.shape[-1]
    return lax.conv_general_dilated(
        x, w[:, None, :].astype(x.dtype), window_strides=(1,),
        padding=[(CONV_WIDTH - 1, 0)],
        dimension_numbers=('NWC', 'WIO', 'NWC'), feature_group_count=C)

def multiscale_pool(xp):
    T = xp.shape[1]
    xf = xp.astype(jnp.float32)
    cs = jnp.cumsum(xf, axis=1)
    pos = jnp.arange(1, T + 1, dtype=jnp.float32)[:, None]
    outs = []
    for gi, w in enumerate(POOL_WINDOWS):
        sl = slice(gi * POOL_GROUP_DIM, (gi + 1) * POOL_GROUP_DIM)
        c_g = cs[..., sl]
        lagged = jnp.pad(c_g, ((0, 0), (w, 0), (0, 0)))[:, :T]
        mean = (c_g - lagged) / jnp.minimum(pos, float(w))
        outs.append(mean - xf[..., sl])
    return jnp.stack(outs, axis=2).astype(xp.dtype)

def gated_delta_rule_chunked(q, k, v, g, beta):
    B, T, H, K = q.shape
    V = v.shape[-1]
    N = T // CHUNK

    def to_chunks(a):
        a = a.reshape((B, N, CHUNK, H) + a.shape[3:])
        return jnp.moveaxis(a, (1, 3), (0, 2))

    qc, kc, vc, bc = to_chunks(q), to_chunks(k), to_chunks(v), to_chunks(beta)
    gc = jnp.cumsum(to_chunks(g), axis=-1)
    causal = jnp.tril(jnp.ones((CHUNK, CHUNK), dtype=bool))
    strict = jnp.tril(jnp.ones((CHUNK, CHUNK), dtype=bool), -1)
    decay = jnp.exp(jnp.where(causal, gc[..., :, None] - gc[..., None, :], -jnp.inf))
    kk = jnp.einsum('nbhik,nbhjk->nbhij', kc, kc)
    a_mat = jnp.where(strict, bc[..., :, None] * kk * decay, 0.0)
    eye = jnp.eye(CHUNK, dtype=q.dtype)
    rhs = jnp.concatenate([bc[..., None] * vc, (bc * jnp.exp(gc))[..., None] * kc], axis=-1)
    sol = lax.linalg.triangular_solve(a_mat + eye, rhs, left_side=True, lower=True,
                                      unit_diagonal=True)
    u, w = sol[..., :V], sol[..., V:]
    qk = jnp.where(causal, jnp.einsum('nbhik,nbhjk->nbhij', qc, kc) * decay, 0.0)
    q_dec = qc * jnp.exp(gc)[..., None]
    g_last = gc[..., -1]
    k_dec = kc * jnp.exp(g_last[..., None] - gc)[..., None]

    def step(S, xs):
        q_i, qk_i, u_i, w_i, k_i, gl_i = xs
        v_new = u_i - jnp.einsum('bhck,bhkv->bhcv', w_i, S)
        o_i = jnp.einsum('bhck,bhkv->bhcv', q_i, S) + jnp.einsum('bhij,bhjv->bhiv', qk_i, v_new)
        S = S * jnp.exp(gl_i)[..., None, None] + jnp.einsum('bhck,bhcv->bhkv', k_i, v_new)
        return S, o_i

    S0 = jnp.zeros((B, H, K, V), dtype=q.dtype)
    _, o = lax.scan(step, S0, (q_dec, qk, u, w, k_dec, g_last))
    return jnp.moveaxis(o, (0, 2), (1, 3)).reshape(B, T, H, V)

def token_mixer(h, mix_w_in, conv_w, a_log, dt_bias, dn_norm_g, pool_w, pool_scale,
                pool_proj, dn_proj, mix_w_out):
    B, T, _ = h.shape
    proj = h @ mix_w_in
    xp, q, k, v, z, b_raw, a_raw, g_pool, g_dn = jnp.split(proj, MIX_IN_SPLITS, axis=-1)

    pooled = multiscale_pool(xp)
    ya = jnp.einsum('btgc,gcd->btgd', pooled, pool_w).reshape(B, T, POOL_WIDTH) * pool_scale
    ya = ya @ pool_proj

    qkv = jax.nn.silu(causal_depthwise_conv(jnp.concatenate([q, k, v], axis=-1), conv_w))
    qkv = qkv.astype(jnp.float32).reshape(B, T, 3, DN_HEADS, DN_HEAD_DIM)
    qh = l2_normalize(qkv[:, :, 0]) * (DN_HEAD_DIM ** -0.5)
    kh = l2_normalize(qkv[:, :, 1])
    vh = qkv[:, :, 2]
    beta = jax.nn.sigmoid(b_raw.astype(jnp.float32))
    g = -jnp.exp(a_log.astype(jnp.float32)) * jax.nn.softplus(
        a_raw.astype(jnp.float32) + dt_bias.astype(jnp.float32))
    o = gated_delta_rule_chunked(qh, kh, vh, g, beta)
    o = rms_norm(o, dn_norm_g).astype(h.dtype).reshape(B, T, DN_WIDTH) * jax.nn.silu(z)
    yb = o @ dn_proj

    merged = jax.nn.sigmoid(g_pool) * ya + jax.nn.sigmoid(g_dn) * yb
    return merged @ mix_w_out

def first_inputs(seed: int = 0) -> dict:
    key = jax.random.key(seed)
    ks = jax.random.split(key, 20)
    D, L, F = D_MODEL, DEPTH, FFN_HIDDEN

    def nrm(k, shape, fan_in):
        return jax.random.normal(k, shape, jnp.float32) * fan_in ** -0.5

    x = jax.random.normal(ks[0], (BATCH, SEQ, D), jnp.float32)
    c = jax.random.normal(ks[1], (BATCH, D), jnp.float32)
    ada_w = 0.5 * nrm(ks[2], (L, D, N_SUBLAYERS * 3 * D), D)
    ada_b = 0.01 * jax.random.normal(ks[3], (L, N_SUBLAYERS * 3 * D), jnp.float32)
    norm_g = 1.0 + 0.05 * jax.random.normal(ks[4], (L, N_SUBLAYERS, D), jnp.float32)
    ffn1_w_in = nrm(ks[5], (L, D, 2 * F), D)
    ffn1_w_out = nrm(ks[6], (L, F, D), F)
    ffn2_w_in = nrm(ks[7], (L, D, 2 * F), D)
    ffn2_w_out = nrm(ks[8], (L, F, D), F)
    mix_w_in = nrm(ks[9], (L, D, MIX_IN_WIDTH), D)
    conv_w = nrm(ks[10], (L, CONV_WIDTH, 3 * DN_WIDTH), CONV_WIDTH)
    a_log = jnp.log(jax.random.uniform(ks[11], (L, DN_HEADS), jnp.float32, minval=1.0, maxval=16.0))
    dt = jnp.exp(jax.random.uniform(ks[12], (L, DN_HEADS), jnp.float32,
                                    minval=math.log(1e-3), maxval=math.log(1e-1)))
    dt_bias = dt + jnp.log(-jnp.expm1(-dt))
    dn_norm_g = 1.0 + 0.05 * jax.random.normal(ks[13], (L, DN_HEAD_DIM), jnp.float32)
    pool_w = nrm(ks[14], (L, POOL_GROUPS, POOL_GROUP_DIM, POOL_GROUP_DIM), POOL_GROUP_DIM)
    pool_scale = 1.0 + 0.1 * jax.random.normal(ks[15], (L, POOL_WIDTH), jnp.float32)
    pool_proj = nrm(ks[16], (L, POOL_WIDTH, D), POOL_WIDTH)
    dn_proj = nrm(ks[17], (L, DN_WIDTH, D), DN_WIDTH)
    mix_w_out = nrm(ks[18], (L, D, D), D)
    final_g = 1.0 + 0.05 * jax.random.normal(ks[19], (D,), jnp.float32)
    return {"x": x, "c": c, "ada_w": ada_w, "ada_b": ada_b, "norm_g": norm_g,
            "ffn1_w_in": ffn1_w_in, "ffn1_w_out": ffn1_w_out,
            "ffn2_w_in": ffn2_w_in, "ffn2_w_out": ffn2_w_out,
            "mix_w_in": mix_w_in, "conv_w": conv_w, "a_log": a_log, "dt_bias": dt_bias,
            "dn_norm_g": dn_norm_g, "pool_w": pool_w, "pool_scale": pool_scale,
            "pool_proj": pool_proj, "dn_proj": dn_proj, "mix_w_out": mix_w_out,
            "final_g": final_g}

def first_block(x, c, ada_w, ada_b, norm_g, ffn1_w_in, ffn1_w_out, ffn2_w_in, ffn2_w_out,
              mix_w_in, conv_w, a_log, dt_bias, dn_norm_g, pool_w, pool_scale, pool_proj,
              dn_proj, mix_w_out, final_g):
    B = x.shape[0]
    for l in range(DEPTH):
        mod = (jax.nn.silu(c) @ ada_w[l] + ada_b[l]).reshape(B, N_SUBLAYERS, 3, D_MODEL)
        shift, scale, gate = mod[:, :, 0], mod[:, :, 1], mod[:, :, 2]

        h = modulate(rms_norm(x, norm_g[l, 0]), shift[:, 0], scale[:, 0])
        x = x + 0.5 * gate[:, 0, None, :] * swiglu(h, ffn1_w_in[l], ffn1_w_out[l])

        h = modulate(rms_norm(x, norm_g[l, 1]), shift[:, 1], scale[:, 1])
        x = x + gate[:, 1, None, :] * token_mixer(
            h, mix_w_in[l], conv_w[l], a_log[l], dt_bias[l], dn_norm_g[l], pool_w[l],
            pool_scale[l], pool_proj[l], dn_proj[l], mix_w_out[l])

        h = modulate(rms_norm(x, norm_g[l, 2]), shift[:, 2], scale[:, 2])
        x = x + 0.5 * gate[:, 2, None, :] * swiglu(h, ffn2_w_in[l], ffn2_w_out[l])
    return rms_norm(x, final_g)


DEPTH_2 = 2

N_ATTN_HEADS = 8
ATTN_HEAD_DIM = 64
ATTN_WIDTH = N_ATTN_HEADS * ATTN_HEAD_DIM
MOBA_BLOCK = 256
MOBA_TOPK = 3
Q_CHUNK = 16
CONV_WIDTH_2 = 512
CONV_K = 3
N_BRANCH = 2
SPLIT_SIZES = (ATTN_WIDTH, ATTN_WIDTH, ATTN_WIDTH, CONV_WIDTH_2, CONV_WIDTH_2, CONV_WIDTH_2, D_MODEL, D_MODEL)
IN_COLS = sum(SPLIT_SIZES)
SPLIT_POINTS = tuple(int(s) for s in np.cumsum(SPLIT_SIZES)[:-1])
PEER_HEADS = 8
PEER_NKEYS = 128
PEER_EXPERTS = PEER_NKEYS * PEER_NKEYS
PEER_DKEY = 256
PEER_HALF = PEER_DKEY // 2
PEER_TOPK = 16
PEER_TOK_CHUNK = 128

NORM_EPS = 1e-6
MASK_VALUE = -1e30


def rmsnorm(x, g):
    xf = x.astype(jnp.float32)
    y = xf * lax.rsqrt(jnp.mean(xf * xf, axis=-1, keepdims=True) + NORM_EPS)
    return (y * g.astype(jnp.float32)).astype(x.dtype)

def alibi_slopes(n):
    return jnp.asarray(np.array([2.0 ** (-8.0 * (h + 1) / n) for h in range(n)], dtype=np.float32))

def moba_attention(q, k, v, slopes):
    B, S, H, hd = q.shape
    nb = -(-S // MOBA_BLOCK)
    pad = nb * MOBA_BLOCK - S
    ksel = min(MOBA_TOPK, nb - 1)
    scale = hd ** -0.5
    q = q.transpose(0, 2, 1, 3)
    k = jnp.pad(k.transpose(0, 2, 1, 3), ((0, 0), (0, 0), (0, pad), (0, 0)))
    v = jnp.pad(v.transpose(0, 2, 1, 3), ((0, 0), (0, 0), (0, pad), (0, 0)))
    kb = k.reshape(B, H, nb, MOBA_BLOCK, hd)
    vb = v.reshape(B, H, nb, MOBA_BLOCK, hd)
    qblk = jnp.arange(S, dtype=jnp.int32) // MOBA_BLOCK
    nc = S // Q_CHUNK

    def chunks(a):
        return jnp.moveaxis(a.reshape(B, H, nc, Q_CHUNK, *a.shape[3:]), 2, 0)

    xs = {"q": chunks(q), "start": jnp.arange(nc, dtype=jnp.int32) * Q_CHUNK}
    if ksel > 0:
        kmean = jnp.mean(kb.astype(jnp.float32), axis=3)
        gate = jnp.einsum("bhtd,bhnd->bhtn", q.astype(jnp.float32), kmean)
        past = jnp.arange(nb, dtype=jnp.int32)[None, :] < qblk[:, None]
        gate = jnp.where(past, gate, MASK_VALUE)
        _, idx = lax.top_k(gate, ksel)
        valid = idx < qblk[:, None]
        xs["idx"] = chunks(idx)
        xs["valid"] = chunks(valid)
    bi = jnp.arange(B)[:, None, None, None]
    hi = jnp.arange(H)[None, :, None, None]
    offs = jnp.arange(MOBA_BLOCK, dtype=jnp.int32)

    def body(xc):
        qc = xc["q"]
        start = xc["start"]
        pos_q = start + jnp.arange(Q_CHUNK, dtype=jnp.int32)
        own = start // MOBA_BLOCK
        k_own = lax.dynamic_index_in_dim(kb, own, axis=2, keepdims=False)
        v_own = lax.dynamic_index_in_dim(vb, own, axis=2, keepdims=False)
        d_own = pos_q[:, None] - (own * MOBA_BLOCK + offs)[None, :]
        s_own = (jnp.einsum("bhtd,bhsd->bhts", qc, k_own).astype(jnp.float32) * scale
                 - slopes[:, None, None] * d_own.astype(jnp.float32))
        s_own = jnp.where(d_own >= 0, s_own, MASK_VALUE)
        if ksel == 0:
            p = jax.nn.softmax(s_own, axis=-1).astype(v.dtype)
            return jnp.einsum("bhts,bhsd->bhtd", p, v_own)
        idxc = xc["idx"]
        validc = xc["valid"]
        k_g = kb[bi, hi, idxc]
        v_g = vb[bi, hi, idxc]
        pos_sel = idxc[..., None] * MOBA_BLOCK + offs
        d_sel = pos_q[None, None, :, None, None] - pos_sel
        s_sel = (jnp.einsum("bhtd,bhtjsd->bhtjs", qc, k_g).astype(jnp.float32) * scale
                 - slopes[None, :, None, None, None] * d_sel.astype(jnp.float32))
        s_sel = jnp.where(validc[..., None], s_sel, MASK_VALUE)
        s_all = jnp.concatenate([s_sel.reshape(B, H, Q_CHUNK, ksel * MOBA_BLOCK), s_own], axis=-1)
        p = jax.nn.softmax(s_all, axis=-1).astype(v.dtype)
        p_sel = p[..., : ksel * MOBA_BLOCK].reshape(B, H, Q_CHUNK, ksel, MOBA_BLOCK)
        p_own = p[..., ksel * MOBA_BLOCK:]
        return (jnp.einsum("bhts,bhsd->bhtd", p_own, v_own)
                + jnp.einsum("bhtjs,bhtjsd->bhtd", p_sel, v_g))

    out = lax.map(body, xs)
    return out.transpose(1, 0, 3, 2, 4).reshape(B, S, H * hd)

def gated_short_conv(b_gate, c_gate, h, w_conv):
    z = c_gate * h
    y = lax.conv_general_dilated(z, w_conv[:, None, :], window_strides=(1,),
                                 padding=[(CONV_K - 1, 0)],
                                 dimension_numbers=("NWC", "WIO", "NWC"),
                                 feature_group_count=CONV_WIDTH_2)
    return b_gate * y

def peer(h, w_query, sub_keys, expert_u, expert_v):
    B, S, D = h.shape
    T = B * S
    hf = h.reshape(T, D)
    q = (hf @ w_query).reshape(T, PEER_HEADS, 2, PEER_HALF)
    scores = jnp.einsum("thpd,hpnd->thpn", q, sub_keys).astype(jnp.float32)
    top_v, top_i = lax.top_k(scores, PEER_TOPK)
    cand_v = top_v[:, :, 0, :, None] + top_v[:, :, 1, None, :]
    cand_i = top_i[:, :, 0, :, None] * PEER_NKEYS + top_i[:, :, 1, None, :]
    cand_v = cand_v.reshape(T, PEER_HEADS, PEER_TOPK * PEER_TOPK)
    cand_i = cand_i.reshape(T, PEER_HEADS, PEER_TOPK * PEER_TOPK)
    best_v, best_pos = lax.top_k(cand_v, PEER_TOPK)
    expert_idx = jnp.take_along_axis(cand_i, best_pos, axis=-1)
    gates = jax.nn.softmax(best_v, axis=-1).astype(h.dtype)
    nc = T // PEER_TOK_CHUNK
    xs = {"h": hf.reshape(nc, PEER_TOK_CHUNK, D),
          "idx": expert_idx.reshape(nc, PEER_TOK_CHUNK, PEER_HEADS, PEER_TOPK),
          "g": gates.reshape(nc, PEER_TOK_CHUNK, PEER_HEADS, PEER_TOPK)}

    def body(xc):
        u = jnp.take(expert_u, xc["idx"], axis=0)
        vv = jnp.take(expert_v, xc["idx"], axis=0)
        a = jax.nn.gelu(jnp.einsum("td,thkd->thk", xc["h"], u))
        return jnp.einsum("thk,thkd->td", xc["g"] * a, vv)

    return lax.map(body, xs).reshape(B, S, D)

def second_inputs(seed: int = 0) -> dict:
    key = jax.random.key(seed)
    ks = jax.random.split(key, 16)
    L, D = DEPTH_2, D_MODEL

    def nrm(k, shape, s):
        return jax.random.normal(k, shape, jnp.float32) * s

    return {
        "x": nrm(ks[0], (BATCH, SEQ, D), 1.0),
        "c": nrm(ks[1], (BATCH, D), 1.0),
        "norm1_g": 1.0 + nrm(ks[2], (L, D), 0.02),
        "norm2_g": 1.0 + nrm(ks[3], (L, D), 0.02),
        "w_ada": nrm(ks[4], (L, D, 6 * D), 0.5 * D ** -0.5),
        "b_ada": nrm(ks[5], (L, 6 * D), 0.02),
        "w_in": nrm(ks[6], (L, D, IN_COLS), D ** -0.5),
        "conv_w": nrm(ks[7], (L, CONV_K, CONV_WIDTH_2), CONV_K ** -0.5),
        "w_attn_proj": nrm(ks[8], (L, ATTN_WIDTH, D), ATTN_WIDTH ** -0.5),
        "w_conv_proj": nrm(ks[9], (L, CONV_WIDTH_2, D), CONV_WIDTH_2 ** -0.5),
        "w_out": nrm(ks[10], (L, D, D), D ** -0.5),
        "w_query": nrm(ks[11], (L, D, PEER_HEADS * PEER_DKEY), D ** -0.5),
        "sub_keys": nrm(ks[12], (L, PEER_HEADS, 2, PEER_NKEYS, PEER_HALF), PEER_HALF ** -0.5),
        "expert_u": nrm(ks[13], (L, PEER_EXPERTS, D), D ** -0.5),
        "expert_v": nrm(ks[14], (L, PEER_EXPERTS, D), PEER_HEADS ** -0.5),
        "final_g": 1.0 + nrm(ks[15], (D,), 0.02),
    }

def second_block(x, c, norm1_g, norm2_g, w_ada, b_ada, w_in, conv_w, w_attn_proj, w_conv_proj,
              w_out, w_query, sub_keys, expert_u, expert_v, final_g):
    B, S, D = x.shape
    slopes = alibi_slopes(N_ATTN_HEADS)
    for l in range(DEPTH_2):
        ada = (c @ w_ada[l] + b_ada[l])[:, None, :]
        sh1, sc1, g1, sh2, sc2, g2 = jnp.split(ada, 6, axis=-1)
        h = rmsnorm(x, norm1_g[l]) * (1.0 + sc1) + sh1
        proj = h @ w_in[l]
        q, k, v, b_gate, c_gate, hc, gate_a, gate_c = jnp.split(proj, SPLIT_POINTS, axis=-1)
        ya = moba_attention(q.reshape(B, S, N_ATTN_HEADS, ATTN_HEAD_DIM),
                            k.reshape(B, S, N_ATTN_HEADS, ATTN_HEAD_DIM),
                            v.reshape(B, S, N_ATTN_HEADS, ATTN_HEAD_DIM), slopes)
        yc = gated_short_conv(b_gate, c_gate, hc, conv_w[l])
        merged = (jax.nn.sigmoid(gate_a) * (ya @ w_attn_proj[l])
                  + jax.nn.sigmoid(gate_c) * (yc @ w_conv_proj[l]))
        x = x + g1 * (merged @ w_out[l])
        h = rmsnorm(x, norm2_g[l]) * (1.0 + sc2) + sh2
        x = x + g2 * peer(h, w_query[l], sub_keys[l], expert_u[l], expert_v[l])
    return rmsnorm(x, final_g)


def setup_inputs(seed=0):
    out = dict(first_inputs(seed))
    for name, value in second_inputs(seed + 1).items():
        if name != "x":
            out[name + "_2"] = value
    return out


def reference(
    x, c, ada_w, ada_b, norm_g, ffn1_w_in, ffn1_w_out, ffn2_w_in, ffn2_w_out, mix_w_in, conv_w,
    a_log, dt_bias, dn_norm_g, pool_w, pool_scale, pool_proj, dn_proj, mix_w_out, final_g, c_2,
    norm1_g_2, norm2_g_2, w_ada_2, b_ada_2, w_in_2, conv_w_2, w_attn_proj_2, w_conv_proj_2,
    w_out_2, w_query_2, sub_keys_2, expert_u_2, expert_v_2, final_g_2,
):
    x = first_block(
        x, c, ada_w, ada_b, norm_g, ffn1_w_in, ffn1_w_out, ffn2_w_in, ffn2_w_out, mix_w_in,
        conv_w, a_log, dt_bias, dn_norm_g, pool_w, pool_scale, pool_proj, dn_proj, mix_w_out,
        final_g,
    )
    return second_block(
        x, c_2, norm1_g_2, norm2_g_2, w_ada_2, b_ada_2, w_in_2, conv_w_2, w_attn_proj_2,
        w_conv_proj_2, w_out_2, w_query_2, sub_keys_2, expert_u_2, expert_v_2, final_g_2,
    )


_drawn_inputs = setup_inputs


def setup_inputs(seed=0):
    import zlib

    import numpy as np

    out = dict(_drawn_inputs(seed))
    spreads = {}
    factors = {'ada_b': 2.9, 'dn_norm_g': 3.818, 'norm2_g_2': 2.827, 'final_g_2': 2.902}
    for name, (base, spread) in spreads.items():
        noise = np.random.default_rng([zlib.crc32(name.encode()), seed]).standard_normal(out[name].shape)
        drawn = base * np.exp(spread * noise) if base else spread * noise
        out[name] = __import__('jax').numpy.asarray(drawn.astype(out[name].dtype))
    for name, factor in factors.items():
        out[name] = (out[name] * factor).astype(out[name].dtype)
    return out
```

```python
from contextlib import ExitStack

import numpy as np

import concourse.bass as bass
from concourse import mybir

ALU = mybir.AluOpType
ACT = mybir.ActivationFunctionType
F32 = mybir.dt.float32
F32R = mybir.dt.float32r
BF16 = mybir.dt.bfloat16
U32 = mybir.dt.uint32
AX = mybir.AxisListType.X

P = 128
T = 256
TT = T // P
D = 1024
DT = D // P
FFN = 2816
FT = FFN // P
POOL_WINDOWS = (2, 4, 8, 16)
NPOOL = len(POOL_WINDOWS)
PADP = 16
HEADS = 8
CONV = 4
CONV2 = 3
LEVELS = 7
AH, AHD = 8, 64
LAYERS = 2
NKEYS = 128
TOPK = 16
PAIRS = HEADS * TOPK
NEG = -1e30

UNIT = 1024
RING = 4
N_ADA1, N_ADA2 = 72, 48
U_ADA = 0
U_FFN1 = U_ADA + N_ADA1 + LAYERS * N_ADA2
N_FFN = 3 * FT
U_MIX = U_FFN1 + N_FFN
N_MIX = 52
U_POOLP = U_MIX + N_MIX
U_DNP = U_POOLP + 4
U_MIXO = U_DNP + 8
U_FFN2 = U_MIXO + 8
U_L2 = U_FFN2 + N_FFN
O_QK, O_V, O_REST, O_AP, O_CP, O_OUT, O_WQ, O_SK, O_PEER = 0, 8, 12, 40, 44, 48, 56, 72, 74
N_L2 = O_PEER + 2 * NKEYS
N_UNITS = U_L2 + LAYERS * N_L2
N_BLOCKS = U_FFN1 // 8
assert N_UNITS % RING == 0

_COLS = {}


def _layout():
    at = 0
    for name, n in (("c", 8), ("c2", 8), ("ada_b", N_ADA1), ("b_ada2", LAYERS * N_ADA2), ("norm_g", 24),
                    ("final_g", 8), ("conv_w", CONV * 24), ("pool_scale", 4), ("dn_g", 1), ("a_log", 8),
                    ("dt_bias", 8), ("n1g2", 16), ("n2g2", 16), ("conv_w2", LAYERS * CONV2 * 4), ("final_g2", 8)):
        _COLS[name] = (at, n)
        at += n
    return at


N_PAR = _layout()

_K1 = {}


def _layout1():
    at = 0
    for name, n in (("ident", 128), ("ones", 128), ("iota", 128), ("dist", TT * T), ("onecol", 31),
                    ("iota16", 16), ("eps", 1), ("qk_scale", 1), ("qk_eps", 1)):
        _K1[name] = (at, n)
        at += n
    return at


N_K1 = _layout1()
_K2 = {}


def _layout2():
    at = 0
    for name, n in (("upto", 128), ("future", 128), ("levels", LEVELS * 128), ("inv_count", NPOOL * T),
                    ("select", 16 * 128)):
        _K2[name] = (at, n)
        at += n
    return at


N_K2 = _layout2()
N_SMALLW = 8 * 16 + NPOOL * 128
ARENA = T * NKEYS
K2_AT = ARENA - N_K2 - N_SMALLW
EXTRA = 3328


def build(nc, weights, params, const1, const2, smallw, out):
    with ExitStack() as ctx:
        def sb(name, shape, dt=F32):
            return ctx.enter_context(nc.sbuf_tensor(name, shape, dt))

        sems = {}

        def sem(name):
            if name not in sems:
                sems[name] = ctx.enter_context(nc.semaphore(name))
            return sems[name]

        ring = sb("ring", [P, RING, UNIT])
        x_t = sb("x_t", [P, DT, T])
        w_hi = sb("w_hi", [P, 2, UNIT], F32R)
        w_lo = sb("w_lo", [P, 2, UNIT], F32R)
        h_hi = sb("h_hi", [P, DT, T], F32R)
        h_lo = sb("h_lo", [P, DT, T], F32R)
        act_hi = sb("act_hi", [P, 2, T], F32R)
        act_lo = sb("act_lo", [P, 2, T], F32R)
        arena = sb("arena", [P, ARENA])
        extra = sb("extra", [P, EXTRA])
        par = sb("par", [P, N_PAR])
        k1 = sb("k1", [P, N_K1])
        mod = sb("mod", [P, N_ADA1 + LAYERS * N_ADA2])
        nscale = sb("nscale", [P, 7 * 8])
        half_gate = sb("half_gate", [P, 16])
        sc = sb("sc", [P, 8])
        zrow = sb("zrow", [1, P], BF16)
        acc = ctx.enter_context(nc.psum_tensor("acc", [P, 4, 512], F32))
        st = ctx.enter_context(nc.psum_tensor("st", [P, 4, 512], F32))
        acc_t = acc[:, :, :].rearrange("p b (u t) -> p (b u) t", u=2)

        def pc(name, i=0, n=None):
            at, size = _COLS[name]
            return par[:, at + i:at + i + (size - i if n is None else n)]

        def kc(name):
            at, n = _K1[name]
            return k1[:, at:at + n]

        def k2c(name):
            at, n = _K2[name]
            return arena[:, K2_AT + at:K2_AT + at + n]

        def ar(at, *shape, base=None):
            n = int(np.prod(shape))
            v = (arena if base is None else base)[:, at:at + n]
            if len(shape) == 2:
                v = v.rearrange("p (a b) -> p a b", b=shape[1])
            elif len(shape) == 3:
                v = v.rearrange("p (a b c) -> p a b c", b=shape[1], c=shape[2])
            return v

        ident, ones = kc("ident"), kc("ones")
        upto, future = k2c("upto"), k2c("future")
        level_mask = k2c("levels").rearrange("p (l i) -> p l i", l=LEVELS)
        inv_count = k2c("inv_count").rearrange("p (g t) -> p g t", g=NPOOL)
        select = k2c("select").rearrange("p (h i) -> p h i", h=16)
        sw_at = K2_AT + N_K2
        w_ba = arena[:, sw_at:sw_at + 128].rearrange("p (k n) -> p k n", n=16)
        w_pool = arena[:, sw_at + 128:sw_at + N_SMALLW].rearrange("p (g n) -> p g n", g=NPOOL)
        dist = kc("dist")

        gate_s = ar(0, 2, T)
        act = ar(2 * T, 2, T)
        part = ar(0, 4, UNIT)
        diag = ar(4 * UNIT, 8, P)
        nh = ar(23816, DT, T)
        std = ar(0, T, base=extra)
        rstd = ar(T, T, base=extra)

        qkv_raw = ar(0, 24, T + 3)
        qkv = ar(6216, 24, T)
        xp = ar(12360, NPOOL, PADP + T)
        pool_a = ar(13448, NPOOL, PADP + T)
        pool_b = ar(14536, NPOOL, PADP + T)
        pooled = ar(15624, NPOOL, T)
        z_s = ar(17672, 8, T)
        g_pool = ar(19720, 8, T)
        g_dn = ar(21768, 8, T)
        merged = ar(23816, 8, T)
        sq_qk = ar(0, 16, T)
        x_s = ar(0, 16, P)
        a_t = ar(2048, 16, P)
        qk_m = ar(4096, 16, P)
        bv = ar(12360, 16, P)
        k_dec = ar(14408, 8, P)
        q_dec = ar(15432, 8, P)
        s1 = ar(16456, 8, P)
        v_new = ar(10312, 16, P)
        resid = ar(2048, 8, P)
        d_m = ar(19720, 16, P)
        d_t = ar(0, 16, P, base=extra)
        off_t = [ar(6216, 16, P), ar(10312, 16, P)]
        o_t = ar(0, 8, T)
        sq_o = ar(0, 8, T, base=extra)
        small = 25864
        rn = ar(small, T)
        rn_s = ar(small + 256, T)
        rows = ar(small + 512, 512)
        ba_b = ar(small + 1024, 2, 8)
        ba_g = ar(small + 1040, 2, 8)
        sp1 = ar(small + 1056, 2, 8)
        sp2 = ar(small + 1072, 2, 8)
        sp3 = ar(small + 1088, 2, 8)
        neg_a = ar(small + 1104, 8)
        g_col = ar(small + 1120, 2, 8)
        g_end = ar(small + 1136, 8)
        k_sc = ar(small + 1144, 8)
        nbe = ar(small + 1152, 8)
        assert small + 1160 <= K2_AT
        dec = [ar(2048 + T * b, T, base=extra) for b in range(2)]
        tmp = [ar(2560 + T * b, T, base=extra) for b in range(2)]
        egb = [ar(3072 + P * b, P, base=extra) for b in range(2)]

        qk2 = ar(0, 8, T)
        v2 = ar(2048, 2, 512)
        bch = ar(3072, 12, T)
        ga2 = ar(6144, 8, T)
        gc2 = ar(8192, 8, T)
        zc = ar(10240, 4, T + 2)
        yc = ar(11272, 4, T)
        s_b = [ar(12296, 2, T), ar(12808, 2, T)]
        p_b = [ar(13320, 2, T), ar(13832, 2, T)]
        pt_b = [ar(14344, 384), ar(14728, 384)]
        vt = ar(15112, 4, T)
        mrg2 = ar(16136, 8, T)
        stat = ar(18184, 8, 8)

        qq = ar(0, 16, T)
        scores = ar(4096, 32, NKEYS)
        tv = ar(8192, 32, TOPK)
        ti = ar(8704, 32 * TOPK).bitcast(U32).rearrange("p (a b) -> p a b", b=TOPK)
        tif = ar(9216, 32, TOPK)
        cand = ar(9728, 16, TOPK * TOPK)
        best = ar(13824, 16, TOPK)
        bpos = ar(14080, 16 * TOPK).bitcast(U32).rearrange("p (a b) -> p a b", b=TOPK)
        pos_u = ar(14336, 2 * 256).bitcast(U32).rearrange("p (a b) -> p a b", b=256)
        pos_f = ar(14848, 2, 256)
        hot = ar(15360, 2, PAIRS * TOPK)
        hot2 = ar(19456, 2, PAIRS * TOPK)
        sel3 = ar(23552, 3, 256)
        ge_ = ar(24320, 256)
        gsum = ar(24576, 16)
        ginv = ar(24592, 16)
        gates = arena[:, :].rearrange("p (n t) -> p n t", t=T)
        selt = ar(512, 3, T, base=extra)
        hot_l = ar(1280, 2, 512, base=extra)
        hot_r = ar(2304, 2, 512, base=extra)
        gelu = ar(1280, 2, T, base=extra)
        gated = ar(1792, 2, T, base=extra)

        landed = [sem(f"landed{s}") for s in range(RING)]
        hi_ready = sem("w_hi_ready")
        taken = sem("w_taken")
        used = sem("weights_used")

        def nth(u):
            return u - U_FFN1 + 1

        def landed_count(u, i=None, per=0):
            assert per % RING == 0
            n = 16 * (u // RING + 1)
            return n if i is None else i * (16 * (per // RING)) + n

        def plus(i, per, n):
            return n if i is None else i * per + n
        stage_done = sem("stage_done")

        def stage(eng, n):
            eng.drain().then_inc(stage_done, 1)
            eng.wait_ge(stage_done, 4 * n)

        def linker(eng, name):
            chain = sem(name)
            count = [0]

            def link(ins):
                ins.then_inc(chain, 1)
                count[0] += 1
                eng.wait_ge(chain, count[0])
            return link

        ST = {}
        for name in ("ada", "ffn0", "mix_proj", "mix_pool", "mix_norm", "mix_heads", "mix_solve", "mix_state", "mix_o",
                     "mix_out", "ffn1", "final1"):
            ST[name] = len(ST) + 1
        for l in range(LAYERS):
            for name in ("proj", "attn", "out", "wq", "topk", "gates", "peer"):
                ST[f"{name}{l}"] = len(ST) + 1

        def shift1(s):
            return mod[:, 24 * s:24 * s + 8]

        def scale1(s):
            return mod[:, 24 * s + 8:24 * s + 16]

        def gate1(s):
            return mod[:, 24 * s + 16:24 * s + 24]

        def mod2(l, k):
            at = N_ADA1 + N_ADA2 * l + 8 * k
            return mod[:, at:at + 8]

        block = ctx.enter_context(nc.Block())

        @block.sync
        def _(sp):
            for s in range(RING):
                sp.dma_start(ring[:, s, :], weights[s]).then_inc(landed[s], 16)
            with sp.Fori(1, N_UNITS // RING) as i:
                for s in range(RING):
                    sp.wait_ge(taken, i * RING + (s + 1 - RING))
                    sp.dma_start(ring[:, s, :],
                                 weights[bass.ds(i * RING + s, 1), :, :].rearrange("a p n -> p (a n)"))\
                      .then_inc(landed[s], 16)

        @block.scalar
        def _(eng):
            link = linker(eng, "act_chain")
            nc_a = nc.scalar
            eng.dma_start(k1[:, :], const1).then_inc(sem("k1_in"), 16)
            eng.dma_start(arena[:, K2_AT:K2_AT + N_K2], const2).then_inc(sem("k2_in"), 16)
            eng.dma_start(arena[:, sw_at:sw_at + N_SMALLW], smallw).then_inc(sem("sw_in"), 16)

            def hi(u, i=None, per=0):
                eng.wait_ge(landed[u % RING], landed_count(u, i, per))
                if u >= U_FFN1 + 2:
                    eng.wait_ge(used, plus(i, per, nth(u - 2)))
                nc_a.activation(w_hi[:, u % 2, :], ring[:, u % RING, :], ACT.Copy).then_inc(hi_ready, 1)

            def step(u, i=None, per=0):
                if u + 2 < N_UNITS:
                    hi(u + 2, i, per)
                else:
                    eng.wait_ge(used, nth(u))

            def steps(u, n):
                for k in range(n):
                    step(u + k)

            def split(name, before, src, n):
                for half in range(2):
                    t = slice(half * n // 2, (half + 1) * n // 2)
                    eng.wait_ge(sem(name + "_full"), before + half + 1)
                    nc_a.activation(h_hi[:, t, :], src[:, t, :], ACT.Copy).then_inc(sem(name + "_hi"), 1)

            def norm(n, m=None):
                eng.wait_ge(sem("sumsq"), n + 1)
                nc_a.activation(std, st[:, 3, 0:T], ACT.Sqrt, scale=1.0 / D, bias=kc("eps")).then_inc(sem("std"), 1)
                if m is not None:
                    split("norm", 2 * m, nh, DT)

            eng.wait_ge(sem("par_in"), 16)
            eng.wait_ge(sem("k1_in"), 16)
            nc_a.activation(sc[:, :], pc("c"), ACT.Silu).then_inc(sem("silu_c"), 1)
            hi(U_FFN1)
            hi(U_FFN1 + 1)
            stage(eng, ST["ada"])

            def ffn(f):
                norm((0, 2)[f], (0, 2)[f])
                base = (U_FFN1, U_FFN2)[f]

                def silu(b):
                    nc_a.activation(gate_s[:, b, :], st[:, b, 0:T], ACT.Silu).then_inc(sem("silu_gate"), 1)

                def upper(j, i=None):
                    eng.wait_ge(sem("act"), plus(i, 4, FT * f + j + 1))
                    nc_a.activation(act_hi[:, j % 2, :], act[:, j % 2, :], ACT.Copy).then_inc(sem("act_hi"), 1)

                def body(j, i=None, per=0):
                    step(base + 2 + 3 * j, i, per)
                    silu((j + 1) % 2)
                    step(base + 3 + 3 * j, i, per)
                    step(base + 4 + 3 * j, i, per)
                    upper(j + 1, i)

                step(base)
                silu(0)
                step(base + 1)
                upper(0)
                body(0)
                with eng.Fori(0, (FT - 2) // 4) as i:
                    for j in range(4):
                        body(1 + j, i, 12)
                step(base + N_FFN - 1)

            ffn(0)
            stage(eng, ST["ffn0"])

            norm(1, 1)
            for p in range(14):
                steps(U_MIX + 2 * p, 2)
                src = st[:, p % 4, :].rearrange("p (u t) -> p u t", u=2)
                if p < 2:
                    dst = xp[:, 2 * p:2 * p + 2, PADP:PADP + T]
                else:
                    dst = qkv_raw[:, 2 * (p - 2):2 * (p - 1), 3:3 + T]
                nc_a.activation(dst, src, ACT.Copy).then_inc(sem("proj_out"), 1)
                if p >= 4:
                    m = p - 4
                    eng.wait_ge(sem("conv"), m + 1)
                    nc_a.activation(qkv[:, 2 * m:2 * m + 2, :], qkv[:, 2 * m:2 * m + 2, :], ACT.Silu)\
                        .then_inc(sem("qkv_silu"), 1)
            for p in range(14, 26):
                steps(U_MIX + 2 * p, 2)
                if p < 16:
                    m = p - 4
                    eng.wait_ge(sem("conv"), m + 1)
                    nc_a.activation(qkv[:, 2 * m:2 * m + 2, :], qkv[:, 2 * m:2 * m + 2, :], ACT.Silu)\
                        .then_inc(sem("qkv_silu"), 1)
                m = p - 14
                dst = (z_s, g_pool, g_dn)[m // 4][:, 2 * (m % 4):2 * (m % 4) + 2, :]
                src = st[:, p % 4, :].rearrange("p (u t) -> p u t", u=2)
                nc_a.activation(dst, src, ACT.Silu if m < 4 else ACT.Sigmoid).then_inc(sem("proj_out"), 1)
            eng.wait_ge(sem("ba_psum"), 1)
            ba_ps = acc[:, 0, 0:32].rearrange("p (c n) -> p c n", n=16)
            nc_a.activation(ba_b, ba_ps[:, :, 0:8], ACT.Sigmoid).then_inc(sem("beta"), 1)
            link(nc_a.activation(neg_a, pc("a_log"), ACT.Exp))
            eng.wait_ge(sem("a_in"), 1)
            link(nc_a.activation(sp2, sp1, ACT.Abs))
            link(nc_a.activation(sp2, sp2, ACT.Exp, scale=-1.0))
            nc_a.activation(sp3, sp2, ACT.Ln, bias=1.0).then_inc(sem("ln1p"), 1)
            stage(eng, ST["mix_proj"])
            eng.wait_ge(sem("pool_mm"), 1)
            for g in range(NPOOL):
                nc_a.activation(h_hi[:, g, :], st[:, g // 2, (g % 2) * T:(g % 2) * T + T], ACT.Copy,
                                scale=pc("pool_scale", g, 1)).then_inc(sem("ya0_hi"), 1)
            steps(U_POOLP, 4)
            stage(eng, ST["mix_pool"])

            eng.wait_ge(sem("sum_qk"), 1)
            nc_a.activation(rn_s[0:16, :], st[0:16, 0, 0:T], ACT.Sqrt, scale=kc("qk_scale")[0:16, :],
                            bias=kc("qk_eps")[0:16, :]).then_inc(sem("std_qk"), 1)
            stage(eng, ST["mix_norm"])

            for h in range(HEADS):
                b = h % 2
                eng.wait_ge(sem("dec_arg"), h + 1)
                nc_a.activation(dec[b], dec[b], ACT.Exp).then_inc(sem("dec"), 1)
                nc_a.activation(egb[b], st[:, b, 128:256], ACT.Exp).then_inc(sem("dec"), 1)
            eng.wait_ge(sem("k_arg"), 1)
            link(nc_a.activation(k_sc, k_sc, ACT.Exp))
            link(nc_a.activation(nbe, g_col[:, 1, :], ACT.Exp))
            for q in range(6):
                eng.wait_ge(sem("tok_t"), q + 1)
                for j in range(4):
                    n = 4 * q + j
                    src = acc[:, q % 4, j * 128:(j + 1) * 128]
                    if n < 16:
                        ins = nc_a.activation(bv[:, n, :], src, ACT.Copy, scale=ba_b[:, n // 8, n % 8:n % 8 + 1])
                    else:
                        ins = nc_a.activation(k_dec[:, n - 16, :], src, ACT.Copy, scale=k_sc[:, n - 16:n - 15])
                ins.then_inc(sem("tok_out"), 1)
            stage(eng, ST["mix_heads"])

            for lv in range(LEVELS):
                for g in range(4):
                    eng.wait_ge(sem("lv_x"), 4 * lv + g + 1)
                    nc_a.activation(x_s[:, 4 * g:4 * g + 4, :], st[:, g, :].rearrange("p (a b) -> p a b", b=128),
                                    ACT.Copy).then_inc(sem("lv_xs"), 1)
            stage(eng, ST["mix_solve"])

            def out_of(dst, src, name):
                nc_a.activation(dst, src.rearrange("p (a b) -> p a b", b=128), ACT.Copy).then_inc(sem(name), 1)

            for g in range(2):
                eng.wait_ge(sem("vn0_psum"), g + 1)
                out_of(v_new[:, 4 * g:4 * g + 4, :], acc[:, g, :], "vn0")
            for g in range(2):
                eng.wait_ge(sem("s1_psum"), g + 1)
                out_of(s1[:, 4 * g:4 * g + 4, :], acc[:, 2 + g, :], "s1")
            for g in range(2):
                eng.wait_ge(sem("vn1_psum"), g + 1)
                out_of(v_new[:, 8 + 4 * g:12 + 4 * g, :], acc[:, g, :], "vn1")
            for m in range(4):
                eng.wait_ge(sem("o_psum"), m + 1)
                nc_a.activation(o_t[:, 2 * m:2 * m + 2, :], st[:, m, :].rearrange("p (u t) -> p u t", u=2),
                                ACT.Copy).then_inc(sem("o_t"), 1)
            stage(eng, ST["mix_state"])
            eng.wait_ge(sem("sum_o"), 1)
            nc_a.activation(rn_s[0:8, :], st[0:8, 0, 0:T], ACT.Sqrt, scale=1.0 / P, bias=kc("eps")[0:8, :])\
                .then_inc(sem("std_o"), 1)
            split("o", 0, o_t, 8)
            stage(eng, ST["mix_o"])
            steps(U_DNP, 8)
            split("merged", 0, merged, 8)
            steps(U_MIXO, 8)
            stage(eng, ST["mix_out"])

            ffn(1)
            stage(eng, ST["ffn1"])
            norm(3)
            stage(eng, ST["final1"])

            for l in range(LAYERS):
                U = U_L2 + N_L2 * l
                norm(4 + 2 * l, 3 + 2 * l)
                for p in range(20):
                    steps(U + O_QK + 2 * p, 2)
                    src = st[:, p % 4, :].rearrange("p (u t) -> p u t", u=2)
                    if p < 4:
                        dst = qk2[:, 2 * p:2 * p + 2, :]
                    elif p < 6:
                        dst = vt[:, 2 * p - 8:2 * p - 6, :]
                    elif p < 12:
                        dst = bch[:, 2 * p - 12:2 * p - 10, :]
                    else:
                        dst = (ga2, gc2)[(p - 12) // 4][:, 2 * ((p - 12) % 4):2 * ((p - 12) % 4) + 2, :]
                    nc_a.activation(dst, src, ACT.Copy if p < 12 else ACT.Sigmoid).then_inc(sem("proj2"), 1)
                stage(eng, ST[f"proj{l}"])

                eng.wait_ge(sem("v_tok"), l + 1)
                nc_a.activation(v2, acc[:, 0:2, :], ACT.Copy).then_inc(sem("v2"), 1)
                for h in range(AH):
                    b = h % 2
                    n = AH * l + h
                    eng.wait_ge(sem("smax"), n + 1)
                    for q in range(2):
                        nc_a.activation(p_b[b][:, q, :], s_b[b][:, q, :], ACT.Exp, scale=AHD ** -0.5,
                                        bias=stat[:, b, 2 + q:3 + q], accum_out=stat[:, b, 4 + q:5 + q])\
                            .then_inc(sem("pexp"), 1)
                    eng.wait_ge(sem("pt_psum"), n + 1)
                    nc_a.activation(pt_b[b], acc[:, b, 0:384], ACT.Copy).then_inc(sem("pt"), 1)
                for m in range(2):
                    eng.wait_ge(sem("pv"), 8 * l + 4 * m + 4)
                    nc_a.activation(h_hi[:, 2 * m:2 * m + 2, :], acc[:, 2 + m, :].rearrange("p (u t) -> p u t", u=2),
                                    ACT.Copy).then_inc(sem("y_hi"), 1)
                eng.wait_ge(sem("yc_full"), l + 1)
                nc_a.activation(h_hi[:, 4:8, :], yc, ACT.Copy).then_inc(sem("yc_hi"), 1)
                stage(eng, ST[f"attn{l}"])
                steps(U + O_AP, 8)
                split("mrg2", 2 * l, mrg2, 8)
                steps(U + O_OUT, 8)
                stage(eng, ST[f"out{l}"])

                norm(5 + 2 * l, 4 + 2 * l)
                for p in range(8):
                    steps(U + O_WQ + 2 * p, 2)
                    nc_a.activation(qq[:, 2 * p:2 * p + 2, :], st[:, p % 4, :].rearrange("p (u t) -> p u t", u=2),
                                    ACT.Copy).then_inc(sem("qq"), 1)
                for u in range(2):
                    for t in range(TT):
                        for half in range(2):
                            if (t, half) == (1, 1):
                                step(U + O_SK + u)
                            else:
                                eng.wait_ge(sem("sk"), 6 * l + 3 * u + 2 * t + half + 1)
                            nc_a.activation(scores[:, 16 * t + 8 * u + 4 * half:16 * t + 8 * u + 4 * half + 4, :],
                                            acc[:, 2 * t + half, :].rearrange("p (a b) -> p a b", b=128), ACT.Copy)\
                                .then_inc(sem("scores"), 1)
                stage(eng, ST[f"wq{l}"])
                eng.wait_ge(sem("best_c"), l + 1)
                nc_a.activation(ge_, ge_, ACT.Exp).then_inc(sem("gexp"), 1)
                eng.wait_ge(sem("sel_psum"), l + 1)
                nc_a.activation(selt, st[:, 0:2, :].rearrange("p a b -> p (a b)")[:, 0:3 * T]
                                .rearrange("p (k t) -> p k t", k=3), ACT.Copy).then_inc(sem("selt"), 1)
                stage(eng, ST[f"topk{l}"])
                with eng.Fori(0, T // 8) as i:
                    for b in range(2):
                        eng.wait_ge(sem("g_psum"), i * 2 + (64 * l + b + 1))
                        nc_a.activation(gates[:, :, bass.ds(i * 8 + 4 * b, 4)].rearrange("p n t -> p t n"),
                                        st[:, b, :].rearrange("p (t n) -> p t n", t=4), ACT.Copy)\
                            .then_inc(sem("g_out"), 1)
                stage(eng, ST[f"gates{l}"])
                base = U + O_PEER

                def gelu_of(b):
                    nc_a.activation(gelu[:, b, :], st[:, b, 0:T], ACT.Gelu_apprx_tanh).then_inc(sem("gelu"), 1)

                def upper(j, i=None):
                    eng.wait_ge(sem("gated"), plus(i, 2, NKEYS * l + j + 1))
                    nc_a.activation(act_hi[:, j % 2, :], gated[:, j % 2, :], ACT.Copy).then_inc(sem("gated_hi"), 1)

                def body(j, i=None, per=0):
                    step(base + 1 + 2 * j, i, per)
                    gelu_of((j + 1) % 2)
                    step(base + 2 + 2 * j, i, per)
                    upper(j + 1, i)

                step(base)
                gelu_of(0)
                upper(0)
                body(0)
                with eng.Fori(0, NKEYS // 2 - 2) as i:
                    for j in range(2):
                        body(1 + j, i, 4)
                for j in range(NKEYS - 3, NKEYS - 1):
                    body(j)
                step(base + 2 * NKEYS - 1)
                stage(eng, ST[f"peer{l}"])
            norm(8)

        @block.vector
        def _(eng):
            link = linker(eng, "dve_chain")
            v = nc.vector
            v.memset(zrow[:, :], 0.0).then_inc(sem("zrow"), 1)

            def lo(u, i=None, per=0):
                eng.wait_ge(hi_ready, plus(i, per, nth(u)))
                v.tensor_tensor(w_lo[:, u % 2, :], ring[:, u % RING, :], w_hi[:, u % 2, :], ALU.subtract)\
                    .then_inc(taken, 1)

            def step(u, i=None, per=0):
                if u + 2 < N_UNITS:
                    lo(u + 2, i, per)
                else:
                    eng.wait_ge(used, nth(u))

            def steps(u, n):
                for k in range(n):
                    step(u + k)

            def split(name, before, src, n, at=0):
                for half in range(2):
                    t = slice(half * n // 2, (half + 1) * n // 2)
                    eng.wait_ge(sem(name + "_hi"), before + half + 1)
                    v.tensor_tensor(h_lo[:, t, :], src[:, t, :], h_hi[:, t, :], ALU.subtract)\
                        .then_inc(sem(name + "_lo"), 1)

            def norm(n, a, b, dst, m=None):
                v.tensor_tensor(nh, x_t[:, :, :], x_t[:, :, :], ALU.mult).then_inc(sem("sq"), 1)
                eng.wait_ge(sem("std"), n + 1)
                link(v.reciprocal(rstd, std))
                for t in range(DT):
                    ins = v.scalar_tensor_tensor(out=dst[:, t, :], in0=x_t[:, t, :], scalar=a[:, t:t + 1], in1=rstd,
                                                 op0=ALU.mult, op1=ALU.mult)
                if b is None:
                    ins.then_inc(sem("normed"), 1)
                    return
                link(ins)
                for t in range(DT):
                    ins = v.tensor_scalar(dst[:, t, :], dst[:, t, :], b[:, t:t + 1], None, ALU.add)
                    if t % 4 == 3:
                        ins.then_inc(sem("norm_full"), 1)
                split("norm", 2 * m, nh, DT)

            eng.wait_ge(sem("par_in"), 16)
            eng.wait_ge(sem("silu_c"), 1)
            eng.wait_ge(sem("k1_in"), 16)

            def on_diagonal(q, i=None):
                b = q % 2
                eng.wait_ge(sem("ada_psum"), plus(i, 2, q + 1))
                v.tensor_tensor(diag, st[:, 2 * b:2 * b + 2, :].rearrange("p b (u n) -> p (b u) n", n=P),
                                ident.unsqueeze(1).to_broadcast([P, 8, P]), ALU.mult).then_inc(sem("ada_diag"), 1)
                eng.wait_ge(sem("ada_diag"), plus(i, 2, q + 1))
                dst = mod[:, 8 * q:8 * q + 8] if i is None else mod[:, bass.ds(i * 16 + 8 * q, 8)]
                v.tensor_reduce(dst, diag, AX, ALU.add).then_inc(sem("ada_mod"), 1)
                eng.wait_ge(sem("ada_mod"), plus(i, 2, q + 1))

            def ada_block(q, vec, i=None):
                for k in range(8):
                    u = 8 * q + k
                    dst = part[:, 2 * (q % 2) + k % 2, :]
                    eng.wait_ge(landed[u % RING], landed_count(u, i, 16))
                    if k < 2:
                        ins = v.tensor_scalar(dst, ring[:, u % RING, :], vec[:, k:k + 1], None, ALU.mult)
                    else:
                        eng.wait_ge(taken, plus(i, 16, u - 1))
                        ins = v.scalar_tensor_tensor(out=dst, in0=ring[:, u % RING, :], scalar=vec[:, k:k + 1],
                                                     in1=dst, op0=ALU.mult, op1=ALU.add)
                    ins.then_inc(taken, 1)
                    if k == 3 and q > 0:
                        on_diagonal(q - 1, i)

            ada_block(0, sc)
            with eng.Fori(0, (N_ADA1 // 8 - 1) // 2) as i:
                for b in range(2):
                    ada_block(1 + b, sc, i)
            with eng.Fori(0, LAYERS * N_ADA2 // 16) as i:
                for b in range(2):
                    ada_block(N_ADA1 // 8 + b, pc("c2"), i)
            on_diagonal(N_BLOCKS - 1)
            link(v.tensor_tensor(mod[:, :], mod[:, :], pc("ada_b", 0, 8 * N_BLOCKS), ALU.add))
            for s in range(3):
                v.scalar_tensor_tensor(out=nscale[:, 8 * s:8 * s + 8], in0=scale1(s), scalar=1.0,
                                       in1=pc("norm_g", 8 * s, 8), op0=ALU.add, op1=ALU.mult)
            for l in range(LAYERS):
                for k, g in ((0, "n1g2"), (1, "n2g2")):
                    at = 24 + 16 * l + 8 * k
                    v.scalar_tensor_tensor(out=nscale[:, at:at + 8], in0=mod2(l, 3 * k + 1), scalar=1.0,
                                           in1=pc(g, 8 * l, 8), op0=ALU.add, op1=ALU.mult)
            for f in range(2):
                ins = v.tensor_scalar(half_gate[:, 8 * f:8 * f + 8], gate1(2 * f), 0.5, None, ALU.mult)
            link(ins)
            lo(U_FFN1)
            lo(U_FFN1 + 1)
            eng.wait_ge(sem("x_in"), 16)
            stage(eng, ST["ada"])

            def add_to_x(gate):
                for t in range(DT):
                    ins = v.scalar_tensor_tensor(out=x_t[:, t, :], in0=acc_t[:, t, :], scalar=gate[:, t:t + 1],
                                                 in1=x_t[:, t, :], op0=ALU.mult, op1=ALU.add)
                link(ins)

            def ffn(f):
                norm((0, 2)[f], nscale[:, 16 * f:16 * f + 8], shift1(2 * f), nh, (0, 2)[f])
                base = (U_FFN1, U_FFN2)[f]

                def mult(j, i=None):
                    eng.wait_ge(sem("silu_gate"), plus(i, 4, FT * f + j + 1))
                    b = j % 2
                    v.tensor_tensor(act[:, b, :], gate_s[:, b, :], st[:, 2 + b, 0:T], ALU.mult).then_inc(sem("act"), 1)

                def lower(j, i=None):
                    eng.wait_ge(sem("act_hi"), plus(i, 4, FT * f + j + 1))
                    b = j % 2
                    v.tensor_tensor(act_lo[:, b, :], act[:, b, :], act_hi[:, b, :], ALU.subtract)\
                        .then_inc(sem("act_lo"), 1)

                def body(j, i=None, per=0):
                    step(base + 2 + 3 * j, i, per)
                    step(base + 3 + 3 * j, i, per)
                    mult(j + 1, i)
                    step(base + 4 + 3 * j, i, per)
                    lower(j + 1, i)

                step(base)
                step(base + 1)
                mult(0)
                lower(0)
                body(0)
                with eng.Fori(0, (FT - 2) // 4) as i:
                    for j in range(4):
                        body(1 + j, i, 12)
                step(base + N_FFN - 1)
                add_to_x(half_gate[:, 8 * f:8 * f + 8])

            ffn(0)
            stage(eng, ST["ffn0"])

            norm(1, nscale[:, 8:16], shift1(1), nh, 1)
            v.memset(qkv_raw[:, :, 0:3], 0.0).then_inc(sem("pad"), 1)
            eng.wait_ge(sem("pad"), 1)

            def conv(m):
                eng.wait_ge(sem("proj_out"), m + 3)
                for j in range(CONV):
                    for t in (2 * m, 2 * m + 1):
                        w = pc("conv_w", 24 * j + t, 1)
                        if j == 0:
                            ins = v.tensor_scalar(qkv[:, t, :], qkv_raw[:, t, 0:T], w, None, ALU.mult)
                        else:
                            ins = v.scalar_tensor_tensor(out=qkv[:, t, :], in0=qkv_raw[:, t, j:j + T], scalar=w,
                                                         in1=qkv[:, t, :], op0=ALU.mult, op1=ALU.add)
                    if j < CONV - 1:
                        link(ins)
                ins.then_inc(sem("conv"), 1)

            for p in range(26):
                steps(U_MIX + 2 * p, 2)
                if 3 <= p < 15:
                    conv(p - 3)
            eng.wait_ge(sem("ba_psum"), 1)
            ba_ps = acc[:, 0, 0:32].rearrange("p (c n) -> p c n", n=16)
            eng.wait_ge(sem("beta"), 1)
            v.tensor_tensor(sp1, ba_ps[:, :, 8:16], pc("dt_bias").unsqueeze(1).to_broadcast([P, 2, 8]), ALU.add)\
                .then_inc(sem("a_in"), 1)
            eng.wait_ge(sem("ln1p"), 1)
            link(v.scalar_tensor_tensor(out=sp1, in0=sp1, scalar=0.0, in1=sp3, op0=ALU.max, op1=ALU.add))
            link(v.scalar_tensor_tensor(out=ba_g, in0=sp1, scalar=-1.0,
                                        in1=neg_a.unsqueeze(1).to_broadcast([P, 2, 8]), op0=ALU.mult, op1=ALU.mult))
            stage(eng, ST["mix_proj"])

            eng.wait_ge(sem("pool_mm"), 1)
            for g in range(NPOOL):
                eng.wait_ge(sem("ya0_hi"), 2 * (g // 2) + 2)
                v.scalar_tensor_tensor(out=h_lo[:, g, :], in0=st[:, g // 2, (g % 2) * T:(g % 2) * T + T],
                                       scalar=pc("pool_scale", g, 1), in1=h_hi[:, g, :], op0=ALU.mult,
                                       op1=ALU.subtract).then_inc(sem("ya0_lo"), 1)
            v.tensor_tensor(sq_qk, qkv[:, 0:16, :], qkv[:, 0:16, :], ALU.mult).then_inc(sem("sq_qk"), 1)
            steps(U_POOLP, 4)
            link(v.tensor_tensor(merged, acc_t, g_pool, ALU.mult))
            stage(eng, ST["mix_pool"])

            eng.wait_ge(sem("std_qk"), 1)
            v.reciprocal(rn[0:16, :], rn_s[0:16, :]).then_inc(sem("rn"), 1)
            eng.wait_ge(sem("g_rows"), 1)
            v.tensor_copy(rows[0:8, :], st[0:8, 1, :]).then_inc(sem("rows"), 1)
            v.tensor_copy(g_col, st[:, 2, 0:16].rearrange("p (c n) -> p c n", n=8)).then_inc(sem("rows"), 1)
            for m in range(8):
                eng.wait_ge(sem("rn_b"), m + 1)
                v.tensor_tensor(qkv[:, 2 * m:2 * m + 2, :], qkv[:, 2 * m:2 * m + 2, :],
                                acc[:, m % 4, :].rearrange("p (u t) -> p u t", u=2), ALU.mult)\
                    .then_inc(sem("qk_n"), 1)
            stage(eng, ST["mix_norm"])

            for h in range(HEADS):
                b = h % 2
                eng.wait_ge(sem("bc"), h + 1)
                dec3 = dec[b].rearrange("p (c i) -> p c i", c=2)
                tmp3 = tmp[b].rearrange("p (c i) -> p c i", c=2)
                v.tensor_copy(g_end[:, h:h + 1], st[:, b, 127:128])
                for c in range(2):
                    ins = v.scalar_tensor_tensor(out=dec3[:, c, :], in0=st[:, b, c * 128:(c + 1) * 128],
                                                 scalar=g_col[:, c, h:h + 1], in1=future,
                                                 op0=ALU.subtract, op1=ALU.add)
                ins.then_inc(sem("dec_arg"), 1)
                eng.wait_ge(sem("dec"), 2 * h + 2)
                eng.wait_ge(sem("kkqk"), h + 1)
                kk = st[:, 2 + b, 0:256].rearrange("p (c i) -> p c i", c=2)
                qk = st[:, 2 + b, 256:512].rearrange("p (c i) -> p c i", c=2)
                link(v.tensor_tensor(tmp3, kk, dec3, ALU.mult))
                both = a_t.rearrange("p (c h) i -> p c h i", c=2)[:, :, h, :]
                v.tensor_tensor(both, tmp3, st[:, b, 256:512].rearrange("p (c i) -> p c i", c=2), ALU.mult)
                v.tensor_tensor(qk_m.rearrange("p (c h) i -> p c h i", c=2)[:, :, h, :], qk, dec3, ALU.mult)
                v.tensor_tensor(q_dec[:, h, :], qkv[:, h, 128:256], egb[b], ALU.mult).then_inc(sem("head"), 1)
            eng.wait_ge(sem("head"), HEADS)
            v.tensor_tensor(k_sc, g_end, g_col[:, 0, :], ALU.subtract).then_inc(sem("k_arg"), 1)
            v.tensor_copy(d_m, ident.unsqueeze(1).to_broadcast([P, 16, P]))
            v.tensor_copy(d_t, ident.unsqueeze(1).to_broadcast([P, 16, P]))
            stage(eng, ST["mix_heads"])

            for lv in range(LEVELS):
                for g in range(4):
                    eng.wait_ge(sem("lv_dx"), 4 * lv + g + 1)
                    b = 2 * (g % 2)
                    sl = slice(4 * g, 4 * g + 4)
                    v.tensor_tensor(d_m[:, sl, :], d_m[:, sl, :], acc[:, b, :].rearrange("p (a b) -> p a b", b=128),
                                    ALU.subtract)
                    v.tensor_tensor(d_t[:, sl, :], d_t[:, sl, :],
                                    acc[:, b + 1, :].rearrange("p (a b) -> p a b", b=128),
                                    ALU.subtract).then_inc(sem("lv_d"), 1)
            link(v.scalar_tensor_tensor(out=nbe, in0=nbe, scalar=-1.0, in1=ba_b[:, 1, :], op0=ALU.mult, op1=ALU.mult))
            stage(eng, ST["mix_solve"])

            for h in range(HEADS):
                if h % 4 == 0:
                    eng.wait_ge(sem("ks1_psum"), h // 4 + 1)
                ins = v.scalar_tensor_tensor(out=resid[:, h, :], in0=st[:, h // 4, (h % 4) * 128:(h % 4) * 128 + 128],
                                             scalar=nbe[:, h:h + 1], in1=bv[:, 8 + h, :], op0=ALU.mult, op1=ALU.add)
                if h % 4 == 3:
                    ins.then_inc(sem("resid"), 1)
            eng.wait_ge(sem("o_t"), 4)
            v.tensor_tensor(sq_o, o_t, o_t, ALU.mult).then_inc(sem("sq_o"), 1)
            stage(eng, ST["mix_state"])
            eng.wait_ge(sem("std_o"), 1)
            v.reciprocal(rn[0:8, :], rn_s[0:8, :]).then_inc(sem("rn_o"), 1)
            for m in range(4):
                eng.wait_ge(sem("rno_b"), m + 1)
                o2 = o_t[:, 2 * m:2 * m + 2, :]
                link(v.scalar_tensor_tensor(out=o2, in0=o2, scalar=pc("dn_g"),
                                            in1=acc[:, m, :].rearrange("p (u t) -> p u t", u=2),
                                            op0=ALU.mult, op1=ALU.mult))
                ins = v.tensor_tensor(o2, o2, z_s[:, 2 * m:2 * m + 2, :], ALU.mult)
                if m % 2 == 1:
                    ins.then_inc(sem("o_full"), 1)
            split("o", 0, o_t, 8)
            stage(eng, ST["mix_o"])
            steps(U_DNP, 8)
            for half in range(2):
                t = slice(4 * half, 4 * half + 4)
                link(v.tensor_tensor(g_dn[:, t, :], acc_t[:, t, :], g_dn[:, t, :], ALU.mult))
                v.tensor_tensor(merged[:, t, :], merged[:, t, :], g_dn[:, t, :], ALU.add)\
                    .then_inc(sem("merged_full"), 1)
            split("merged", 0, merged, 8)
            steps(U_MIXO, 8)
            add_to_x(gate1(1))
            stage(eng, ST["mix_out"])

            ffn(1)
            stage(eng, ST["ffn1"])
            norm(3, pc("final_g"), None, x_t)
            stage(eng, ST["final1"])

            for l in range(LAYERS):
                U = U_L2 + N_L2 * l
                norm(4 + 2 * l, nscale[:, 24 + 16 * l:32 + 16 * l], mod2(l, 0), nh, 3 + 2 * l)
                steps(U + O_QK, 40)
                stage(eng, ST[f"proj{l}"])
                for h in range(AH):
                    b = h % 2
                    n = AH * l + h
                    eng.wait_ge(sem("s_psum"), n + 1)
                    link(v.scalar_tensor_tensor(out=s_b[b], in0=dist.rearrange("p (q s) -> p q s", q=2),
                                                scalar=-(2.0 ** (-8.0 * (h + 1) / AH)) * AHD ** 0.5,
                                                in1=st[:, b, :].rearrange("p (q s) -> p q s", q=2),
                                                op0=ALU.mult, op1=ALU.add))
                    link(v.tensor_reduce(stat[:, b, 0:2], s_b[b], AX, ALU.max))
                    v.tensor_scalar(stat[:, b, 2:4], stat[:, b, 0:2], -(AHD ** -0.5), None, ALU.mult)\
                        .then_inc(sem("smax"), 1)
                    eng.wait_ge(sem("pexp"), 2 * n + 2)
                    link(v.reciprocal(stat[:, b, 6:8], stat[:, b, 4:6]))
                    for q in range(2):
                        ins = v.tensor_scalar(p_b[b][:, q, :], p_b[b][:, q, :], stat[:, b, 6 + q:7 + q], None, ALU.mult)
                    ins.then_inc(sem("p"), 1)
                eng.wait_ge(sem("zc"), l + 1)
                for j in range(CONV2):
                    for t in range(4):
                        w = pc("conv_w2", (l * CONV2 + j) * 4 + t, 1)
                        if j == 0:
                            ins = v.tensor_scalar(yc[:, t, :], zc[:, t, 0:T], w, None, ALU.mult)
                        else:
                            ins = v.scalar_tensor_tensor(out=yc[:, t, :], in0=zc[:, t, j:j + T], scalar=w,
                                                         in1=yc[:, t, :], op0=ALU.mult, op1=ALU.add)
                    link(ins)
                v.tensor_tensor(yc, yc, bch[:, 0:4, :], ALU.mult).then_inc(sem("yc_full"), 1)
                for m in range(2):
                    eng.wait_ge(sem("y_hi"), 2 * l + m + 1)
                    v.tensor_tensor(h_lo[:, 2 * m:2 * m + 2, :], acc[:, 2 + m, :].rearrange("p (u t) -> p u t", u=2),
                                    h_hi[:, 2 * m:2 * m + 2, :], ALU.subtract)
                eng.wait_ge(sem("yc_hi"), l + 1)
                v.tensor_tensor(h_lo[:, 4:8, :], yc, h_hi[:, 4:8, :], ALU.subtract)
                stage(eng, ST[f"attn{l}"])
                steps(U + O_AP, 4)
                v.tensor_tensor(mrg2, acc_t, ga2, ALU.mult).then_inc(sem("acc_free"), 1)
                steps(U + O_CP, 4)
                v.tensor_tensor(gc2, acc_t, gc2, ALU.mult).then_inc(sem("acc_free"), 1)
                eng.wait_ge(sem("acc_free"), 2 * l + 2)
                for half in range(2):
                    t = slice(4 * half, 4 * half + 4)
                    v.tensor_tensor(mrg2[:, t, :], mrg2[:, t, :], gc2[:, t, :], ALU.add).then_inc(sem("mrg2_full"), 1)
                split("mrg2", 2 * l, mrg2, 8)
                steps(U + O_OUT, 8)
                add_to_x(mod2(l, 2))
                stage(eng, ST[f"out{l}"])

                norm(5 + 2 * l, nscale[:, 32 + 16 * l:40 + 16 * l], mod2(l, 3), nh, 4 + 2 * l)
                steps(U + O_WQ, 18)
                stage(eng, ST[f"wq{l}"])

                def top16(src, vals, places, n):
                    for half in range(2):
                        lo = 8 * half
                        for k in range(n):
                            ins = v.max(vals[:, k, lo:lo + 8], src[:, k, :])
                        link(ins)
                        for k in range(n):
                            ins = v.max_index(places[:, k, lo:lo + 8], vals[:, k, lo:lo + 8], src[:, k, :])
                        link(ins)
                        if half == 0:
                            for k in range(n):
                                ins = v.match_replace(src[:, k, :], vals[:, k, lo:lo + 8], src[:, k, :],
                                                      -3.4028234e38)
                            link(ins)

                top16(scores, tv, ti, 32)
                link(v.tensor_copy(tif, ti))
                tv5 = tv.rearrange("p (g s) k -> p g s k", s=2)
                for t in range(TT):
                    g = slice(8 * t, 8 * t + 8)
                    ins = v.tensor_tensor(cand[:, g, :].rearrange("p g (a b) -> p g a b", b=TOPK),
                                          tv5[:, g, 0, :].unsqueeze(3).to_broadcast([P, 8, TOPK, TOPK]),
                                          tv5[:, g, 1, :].unsqueeze(2).to_broadcast([P, 8, TOPK, TOPK]), ALU.add)
                link(ins)
                top16(cand, best, bpos, 16)
                v.tensor_tensor(ge_.rearrange("p (g k) -> p g k", k=TOPK), best,
                                best[:, :, 0:1].to_broadcast([P, 16, TOPK]), ALU.subtract).then_inc(sem("best_c"), 1)
                bp = bpos.rearrange("p a b -> p (a b)")
                v.tensor_single_scalar(pos_u[:, 0, :], bp, 4, ALU.logical_shift_right)
                link(v.tensor_single_scalar(pos_u[:, 1, :], bp, 15, ALU.bitwise_and))
                link(v.tensor_copy(pos_f, pos_u))
                tif5 = tif.rearrange("p (g s) k -> p g s k", s=2)
                iota16 = kc("iota16")
                for t in range(TT):
                    for s in range(2):
                        hv = hot[:, s, :].rearrange("p (n a) -> p n a", a=TOPK)
                        link(v.tensor_tensor(hv, pos_f[:, s, 128 * t:128 * t + 128].unsqueeze(2)
                                             .to_broadcast([P, PAIRS, TOPK]),
                                             iota16.unsqueeze(1).to_broadcast([P, PAIRS, TOPK]), ALU.is_equal))
                        link(v.tensor_tensor(hot2[:, s, :].rearrange("p (g k a) -> p g k a", k=TOPK, a=TOPK),
                                             hot[:, s, :].rearrange("p (g k a) -> p g k a", k=TOPK, a=TOPK),
                                             tif5[:, 8 * t:8 * t + 8, s, :].unsqueeze(2)
                                             .to_broadcast([P, 8, TOPK, TOPK]), ALU.mult))
                        link(v.tensor_reduce(sel3[:, s, 128 * t:128 * t + 128],
                                             hot2[:, s, :].rearrange("p (n a) -> p n a", a=TOPK), AX, ALU.add))
                eng.wait_ge(sem("gexp"), l + 1)
                ge3 = ge_.rearrange("p (g k) -> p g k", k=TOPK)
                link(v.tensor_reduce(gsum, ge3, AX, ALU.add))
                link(v.reciprocal(ginv, gsum))
                v.tensor_tensor(sel3[:, 2, :].rearrange("p (g k) -> p g k", k=TOPK), ge3,
                                ginv.unsqueeze(2).to_broadcast([P, 16, TOPK]), ALU.mult).then_inc(sem("sel3"), 1)
                stage(eng, ST[f"topk{l}"])
                def hot_rows(b, i=0):
                    for k in range(4):
                        at = i * 8 + (4 * b + k)
                        v.tensor_scalar(hot_l[:, b, 128 * k:128 * k + 128], kc("iota"),
                                        selt[:, 0, bass.ds(at, 1)], None, ALU.is_equal)
                        ins = v.tensor_scalar(hot_r[:, b, 128 * k:128 * k + 128], kc("iota"),
                                              selt[:, 1, bass.ds(at, 1)], selt[:, 2, bass.ds(at, 1)],
                                              ALU.is_equal, ALU.mult)
                    ins.then_inc(sem("hot"), 1)

                for b in range(2):
                    hot_rows(b)
                with eng.Fori(1, T // 8) as i:
                    for b in range(2):
                        eng.wait_ge(sem("g_psum"), i * 2 + (64 * l + b - 1))
                        hot_rows(b, i)
                stage(eng, ST[f"gates{l}"])
                base = U + O_PEER

                def mult(j, i=None):
                    eng.wait_ge(sem("gelu"), plus(i, 2, NKEYS * l + j + 1))
                    b = j % 2
                    g_ = gates[:, j, :] if i is None else gates[:, bass.ds(i * 2 + j, 1), :]\
                        .rearrange("p a t -> p (a t)")
                    v.tensor_tensor(gated[:, b, :], gelu[:, b, :], g_, ALU.mult).then_inc(sem("gated"), 1)

                def lower(j, i=None):
                    eng.wait_ge(sem("gated_hi"), plus(i, 2, NKEYS * l + j + 1))
                    b = j % 2
                    v.tensor_tensor(act_lo[:, b, :], gated[:, b, :], act_hi[:, b, :], ALU.subtract)\
                        .then_inc(sem("gated_lo"), 1)

                def body(j, i=None, per=0):
                    step(base + 1 + 2 * j, i, per)
                    mult(j + 1, i)
                    step(base + 2 + 2 * j, i, per)
                    lower(j + 1, i)

                step(base)
                mult(0)
                lower(0)
                body(0)
                with eng.Fori(0, NKEYS // 2 - 2) as i:
                    for j in range(2):
                        body(1 + j, i, 4)
                for j in range(NKEYS - 3, NKEYS - 1):
                    body(j)
                step(base + 2 * NKEYS - 1)
                add_to_x(mod2(l, 5))
                stage(eng, ST[f"peer{l}"])
            norm(8, pc("final_g2"), None, nh)

        @block.gpsimd
        def _(eng):
            link = linker(eng, "pool_chain")
            g = nc.gpsimd
            eng.dma_start(par[:, :], params[:, 0:N_PAR]).then_inc(sem("par_in"), 16)
            eng.dma_start(x_t[:, :, :].rearrange("p a t -> p (a t)"), params[:, N_PAR:N_PAR + DT * T])\
               .then_inc(sem("x_in"), 16)
            stage(eng, ST["ada"])
            stage(eng, ST["ffn0"])
            for buf in (xp, pool_a, pool_b):
                ins = g.memset(buf[:, :, 0:PADP], 0.0)
            link(ins)
            eng.wait_ge(sem("proj_out"), 2)
            src = xp
            for k in range(NPOOL):
                dst = (pool_a, pool_b)[k % 2]
                w = 1 << k
                link(g.tensor_tensor(dst[:, k:NPOOL, PADP:PADP + T], src[:, k:NPOOL, PADP:PADP + T],
                                     src[:, k:NPOOL, PADP - w:PADP + T - w], ALU.add))
                src = dst
            eng.wait_ge(sem("k2_in"), 16)
            for k in range(NPOOL):
                ins = g.tensor_tensor(pooled[:, k, :], (pool_a, pool_b)[k % 2][:, k, PADP:PADP + T],
                                      inv_count[:, k, :], ALU.mult)
            link(ins)
            g.tensor_tensor(pooled, pooled, xp[:, :, PADP:PADP + T], ALU.subtract).then_inc(sem("pooled"), 1)
            stage(eng, ST["mix_proj"])
            stage(eng, ST["mix_pool"])
            stage(eng, ST["mix_norm"])
            stage(eng, ST["mix_heads"])
            for lv in range(LEVELS):
                if lv >= 2:
                    eng.wait_ge(sem("lv_x"), 4 * (lv - 1))
                g.tensor_tensor(off_t[lv % 2], a_t, level_mask[:, lv, :].unsqueeze(1).to_broadcast([P, 16, P]),
                                ALU.mult).then_inc(sem("lv_off"), 1)
            for name in ("mix_solve", "mix_state", "mix_o", "mix_out", "ffn1", "final1"):
                stage(eng, ST[name])
            for l in range(LAYERS):
                stage(eng, ST[f"proj{l}"])
                link(g.memset(zc[:, :, 0:2], 0.0))
                g.tensor_tensor(zc[:, :, 2:2 + T], bch[:, 4:8, :], bch[:, 8:12, :], ALU.mult).then_inc(sem("zc"), 1)
                for name in ("attn", "out", "wq", "topk"):
                    stage(eng, ST[f"{name}{l}"])
                stage(eng, ST[f"gates{l}"])
                stage(eng, ST[f"peer{l}"])
            eng.wait_ge(sem("normed"), 2)
            eng.dma_start(out, nh.rearrange("p a t -> p (a t)")).then_inc(sem("out"), 16)
            eng.wait_ge(sem("out"), 16)

        @block.tensor
        def _(eng):
            mm = nc.tensor.matmul

            def product(u, dst, hi_t, lo_t, i=None, per=0, first=False, last=False, shared=False):
                eng.wait_ge(hi_ready, plus(i, per, nth(u)))
                for t in range(DT):
                    w = w_hi[:, u % 2, t * P:(t + 1) * P]
                    start = first and (t == 0 if shared else t % 2 == 0)
                    mm(dst(t), w, hi_t(t), start=start, stop=False, skip_group_check=True)
                    mm(dst(t), w, lo_t(t), start=False, stop=False, skip_group_check=True)
                eng.wait_ge(taken, plus(i, per, u + 1))
                for t in range(DT):
                    ins = mm(dst(t), w_lo[:, u % 2, t * P:(t + 1) * P], hi_t(t), start=False,
                             stop=last and (t == DT - 1 or not shared), skip_group_check=True)
                ins.then_inc(used, 1)

            def norm(m=None):
                n = norm_count[0]
                norm_count[0] += 1
                eng.wait_ge(sem("sq"), n + 1)
                for t in range(DT):
                    ins = mm(st[:, 3, 0:T], ones, nh[:, t, :], start=t == 0, stop=t == DT - 1)
                ins.then_inc(sem("sumsq"), 1)
                if m is not None:
                    eng.wait_ge(sem("norm_lo"), 2 * m + 2)

            norm_count = [0]

            def ada_total(q, i=None):
                b = q % 2
                eng.wait_ge(taken, plus(i, 16, 8 * q + 8))
                if q >= 2:
                    eng.wait_ge(sem("ada_diag"), plus(i, 2, q - 1))
                for half in range(2):
                    for k in range(2):
                        ins = mm(st[:, 2 * b + half, :], ones, part[:, 2 * b + k, half * 512:half * 512 + 512],
                                 start=k == 0, stop=k == 1)
                ins.then_inc(sem("ada_psum"), 1)

            eng.wait_ge(sem("k1_in"), 16)
            ada_total(0)
            ada_total(1)
            ada_total(2)
            with eng.Fori(0, (N_BLOCKS - 3) // 2) as i:
                for b in range(2):
                    ada_total(3 + b, i)
            eng.wait_ge(sem("zrow"), 1)
            stage(eng, ST["ada"])

            def clear_acc():
                for b in range(4):
                    mm(acc[:, b, :], zrow[0:1, :], zrow[0:1, :].unsqueeze(1).to_broadcast([1, 4, P]), start=True, stop=False,
                       skip_group_check=True)

            def accumulate(u, b, i=None, per=0, last=False):
                product(u, lambda t: acc_t[:, t, :], lambda t: act_hi[:, b, :], lambda t: act_lo[:, b, :],
                        i, per, last=last)

            def tile(dst, u, i=None, per=0):
                product(u, lambda t: dst, lambda t: h_hi[:, t, :], lambda t: h_lo[:, t, :], i, per,
                        first=True, last=True, shared=True)

            def ffn(f):
                norm((0, 2)[f])
                clear_acc()
                base = (U_FFN1, U_FFN2)[f]

                def up(u, j, i=None, per=0):
                    tile(st[:, j, 0:T], u, i, per)
                    tile(st[:, 2 + j, 0:T], u + 1, i, per)

                def body(j, i=None, per=0):
                    up(base + 2 + 3 * j, (j + 1) % 2, i, per)
                    eng.wait_ge(sem("act_lo"), plus(i, 4, FT * f + j + 1))
                    accumulate(base + 4 + 3 * j, j % 2, i, per)

                up(base, 0)
                body(0)
                with eng.Fori(0, (FT - 2) // 4) as i:
                    for j in range(4):
                        body(1 + j, i, 12)
                eng.wait_ge(sem("act_lo"), FT * f + FT)
                accumulate(base + N_FFN - 1, (FT - 1) % 2, last=True)

            ffn(0)
            stage(eng, ST["ffn0"])

            def pairs(base, n, sem_name, before):
                for p in range(n):
                    if p >= 4:
                        eng.wait_ge(sem(sem_name), before + p - 3)
                    for k in range(2):
                        tile(st[:, p % 4, k * T:(k + 1) * T], base + 2 * p + k)

            norm(1)
            pairs(U_MIX, 26, "proj_out", 0)
            eng.wait_ge(sem("sw_in"), 16)
            for t in range(TT):
                for k in range(DT):
                    ins = mm(acc[:, 0, 16 * t:16 * t + 16], nh[:, k, t * P:(t + 1) * P], w_ba[:, k, :],
                             start=k == 0, stop=k == DT - 1)
            ins.then_inc(sem("ba_psum"), 1)
            stage(eng, ST["mix_proj"])

            def kmajor(base, n, at=0, waits=None):
                for k in range(n):
                    if waits is not None:
                        eng.wait_ge(*waits(k))
                    product(base + k, lambda t: acc_t[:, t, :], lambda t: h_hi[:, at + k, :],
                            lambda t: h_lo[:, at + k, :], first=k == 0, last=k == n - 1)

            eng.wait_ge(sem("pooled"), 1)
            for k in range(NPOOL):
                ins = mm(st[:, k // 2, (k % 2) * T:(k % 2) * T + T], w_pool[:, k, :], pooled[:, k, :],
                         start=True, stop=True)
            ins.then_inc(sem("pool_mm"), 1)
            kmajor(U_POOLP, 4, waits=lambda k: (sem("ya0_lo"), k + 1))
            stage(eng, ST["mix_pool"])

            eng.wait_ge(sem("sq_qk"), 1)
            eng.wait_ge(sem("k2_in"), 16)
            onecol = kc("onecol")
            for h in range(16):
                ins = mm(st[0:16, 0, 0:T], onecol[:, 15 - h:31 - h], sq_qk[:, h, :], start=h == 0, stop=h == 15)
            ins.then_inc(sem("sum_qk"), 1)
            for c in range(2):
                mm(st[0:8, 1, c * P:(c + 1) * P], ba_g[:, c, :], upto, start=True, stop=True)
                mm(st[0:8, 1, T + c * P:T + (c + 1) * P], ba_b[:, c, :], ident, start=True, stop=True)
            for c in range(2):
                ins = mm(st[:, 2, 8 * c:8 * c + 8], upto, ba_g[:, c, :], start=True, stop=True)
            ins.then_inc(sem("g_rows"), 1)
            eng.wait_ge(sem("rn"), 1)
            for m in range(8):
                if m >= 4:
                    eng.wait_ge(sem("qk_n"), m - 3)
                for k in range(2):
                    ins = mm(acc[:, m % 4, k * T:(k + 1) * T], select[0:16, 2 * m + k, :], rn[0:16, :],
                             start=True, stop=True)
                ins.then_inc(sem("rn_b"), 1)
            stage(eng, ST["mix_norm"])

            for h in range(HEADS):
                b = h % 2
                if h >= 2:
                    eng.wait_ge(sem("head"), h - 1)
                mm(st[:, b, :], select[0:8, h, :], rows[0:8, :], start=True, stop=True).then_inc(sem("bc"), 1)
                for c in range(2):
                    ck = slice(c * P, (c + 1) * P)
                    mm(st[:, 2 + b, c * P:(c + 1) * P], qkv[:, 8 + h, ck], qkv[:, 8 + h, ck], start=True, stop=True)
                    ins = mm(st[:, 2 + b, T + c * P:T + (c + 1) * P], qkv[:, 8 + h, ck], qkv[:, h, ck],
                             start=True, stop=True)
                ins.then_inc(sem("kkqk"), 1)
            for q in range(6):
                if q >= 4:
                    eng.wait_ge(sem("tok_out"), q - 3)
                for j in range(4):
                    n = 4 * q + j
                    src = qkv[:, 16 + n % 8, (n // 8) * P:(n // 8 + 1) * P] if n < 16 else qkv[:, 8 + n - 16, 0:P]
                    ins = nc.tensor.transpose(acc[:, q % 4, j * P:(j + 1) * P], src, ident)
                ins.then_inc(sem("tok_t"), 1)
            stage(eng, ST["mix_heads"])

            for lv in range(LEVELS):
                eng.wait_ge(sem("lv_off"), lv + 1)
                for g in range(4):
                    if lv >= 1:
                        eng.wait_ge(sem("lv_d"), 4 * (lv - 1) + g + 1)
                    for k in range(4):
                        ins = mm(st[:, g, k * P:(k + 1) * P], off_t[lv % 2][:, 4 * g + k, :], d_m[:, 4 * g + k, :],
                                 start=True, stop=True)
                    ins.then_inc(sem("lv_x"), 1)
                for g in range(4):
                    b = 2 * (g % 2)
                    if 4 * lv + g >= 2:
                        eng.wait_ge(sem("lv_d"), 4 * lv + g - 1)
                    eng.wait_ge(sem("lv_xs"), 4 * lv + g + 1)
                    for k in range(4):
                        n = 4 * g + k
                        mm(acc[:, b, k * P:(k + 1) * P], d_t[:, n, :], x_s[:, n, :], start=True, stop=True)
                        ins = mm(acc[:, b + 1, k * P:(k + 1) * P], x_s[:, n, :], d_t[:, n, :], start=True, stop=True)
                    ins.then_inc(sem("lv_dx"), 1)
            stage(eng, ST["mix_solve"])

            def four(bank, g, name, lhs, rhs):
                for k in range(4):
                    h = 4 * g + k
                    ins = mm(bank[:, k * P:(k + 1) * P], lhs(h), rhs(h), start=True, stop=True)
                ins.then_inc(sem(name), 1)

            for g in range(2):
                four(acc[:, g, :], g, "vn0_psum", lambda h: d_t[:, h, :], lambda h: bv[:, h, :])
            for g in range(2):
                eng.wait_ge(sem("vn0"), g + 1)
                four(acc[:, 2 + g, :], g, "s1_psum", lambda h: k_dec[:, h, :], lambda h: v_new[:, h, :])
            for g in range(2):
                eng.wait_ge(sem("s1"), g + 1)
                four(st[:, g, :], g, "ks1_psum", lambda h: qkv[:, 8 + h, 128:256], lambda h: s1[:, h, :])
            for g in range(2):
                eng.wait_ge(sem("resid"), g + 1)
                four(acc[:, g, :], g, "vn1_psum", lambda h: d_t[:, 8 + h, :], lambda h: resid[:, h, :])
            for m in range(4):
                eng.wait_ge(sem("vn1"), m // 2 + 1)
                if m == 0:
                    eng.wait_ge(sem("resid"), 2)
                for k in range(2):
                    h = 2 * m + k
                    o = st[:, m, k * T:(k + 1) * T]
                    mm(o[:, 0:128], v_new[:, h, :], qk_m[:, h, :], start=True, stop=True)
                    mm(o[:, 128:256], v_new[:, 8 + h, :], qk_m[:, 8 + h, :], start=True, stop=False)
                    ins = mm(o[:, 128:256], s1[:, h, :], q_dec[:, h, :], start=False, stop=True)
                ins.then_inc(sem("o_psum"), 1)
            stage(eng, ST["mix_state"])
            eng.wait_ge(sem("sq_o"), 1)
            for h in range(8):
                ins = mm(st[0:8, 0, 0:T], onecol[:, 15 - h:23 - h], sq_o[:, h, :], start=h == 0, stop=h == 7)
            ins.then_inc(sem("sum_o"), 1)
            eng.wait_ge(sem("rn_o"), 1)
            for m in range(4):
                for k in range(2):
                    ins = mm(acc[:, m, k * T:(k + 1) * T], select[0:8, 2 * m + k, :], rn[0:8, :],
                             start=True, stop=True)
                ins.then_inc(sem("rno_b"), 1)
            stage(eng, ST["mix_o"])
            kmajor(U_DNP, 8, waits=lambda k: (sem("o_lo"), k // 4 + 1))
            kmajor(U_MIXO, 8, waits=lambda k: (sem("merged_lo"), k // 4 + 1))
            stage(eng, ST["mix_out"])

            ffn(1)
            stage(eng, ST["ffn1"])
            norm()
            stage(eng, ST["final1"])

            for l in range(LAYERS):
                U = U_L2 + N_L2 * l
                norm(3 + 2 * l)
                pairs(U + O_QK, 20, "proj2", 20 * l)
                stage(eng, ST[f"proj{l}"])

                def scores_of(h):
                    b, r = h % 2, slice(64 * (h % 2), 64 * (h % 2) + 64)
                    if h >= 2:
                        eng.wait_ge(sem("smax"), AH * l + h - 1)
                    for q in range(2):
                        ins = mm(st[:, b, q * T:(q + 1) * T], qk2[r, h // 2, q * P:(q + 1) * P],
                                 qk2[r, 4 + h // 2, :], start=True, stop=True)
                    ins.then_inc(sem("s_psum"), 1)

                def values_of(h):
                    b = h % 2
                    eng.wait_ge(sem("p"), AH * l + h + 1)
                    if h >= 2:
                        eng.wait_ge(sem("pt"), AH * l + h - 1)
                    nc.tensor.transpose(acc[:, b, 0:128], p_b[b][:, 0, 0:128], ident)
                    nc.tensor.transpose(acc[:, b, 128:256], p_b[b][:, 1, 0:128], ident)
                    nc.tensor.transpose(acc[:, b, 256:384], p_b[b][:, 1, 128:256], ident)\
                        .then_inc(sem("pt_psum"), 1)
                    eng.wait_ge(sem("pt"), AH * l + h + 1)
                    m = h // 2
                    o = acc[64 * b:64 * b + 64, 2 + m // 2, (m % 2) * T:(m % 2) * T + T]
                    mm(o[:, 0:128], v2[:, 0, 64 * h:64 * h + 64], pt_b[b][:, 0:128], start=True, stop=True)
                    mm(o[:, 128:256], v2[:, 0, 64 * h:64 * h + 64], pt_b[b][:, 128:256], start=True, stop=False)
                    mm(o[:, 128:256], v2[:, 1, 64 * h:64 * h + 64], pt_b[b][:, 256:384], start=False, stop=True)\
                        .then_inc(sem("pv"), 1)

                for t in range(TT):
                    for n in range(4):
                        ins = nc.tensor.transpose(acc[:, t, n * P:(n + 1) * P], vt[:, n, t * P:(t + 1) * P], ident)
                ins.then_inc(sem("v_tok"), 1)
                scores_of(0)
                eng.wait_ge(sem("v2"), l + 1)
                for h in range(AH):
                    if h + 1 < AH:
                        scores_of(h + 1)
                    values_of(h)
                stage(eng, ST[f"attn{l}"])
                kmajor(U + O_AP, 4)
                eng.wait_ge(sem("acc_free"), 2 * l + 1)
                kmajor(U + O_CP, 4, at=4)
                kmajor(U + O_OUT, 8, waits=lambda k: (sem("mrg2_lo"), 2 * l + k // 4 + 1))
                stage(eng, ST[f"out{l}"])

                norm(4 + 2 * l)
                pairs(U + O_WQ, 8, "qq", 8 * l)
                eng.wait_ge(sem("qq"), 8 * l + 8)
                for u in range(2):
                    n_u = U + O_SK + u
                    eng.wait_ge(taken, n_u + 1)
                    for t in range(TT):
                        for half in range(2):
                            if u == 1:
                                eng.wait_ge(sem("scores"), 8 * l + 2 * t + half + 1)
                            for k in range(4):
                                n = 4 * half + k
                                for part_ in (w_hi, w_lo):
                                    w = part_[:, n_u % 2, n * P:(n + 1) * P].bitcast(F32)
                                    ins = mm(acc[:, 2 * t + half, k * P:(k + 1) * P],
                                             qq[:, 8 * u + n, t * P:(t + 1) * P], w,
                                             start=part_ is w_hi, stop=part_ is w_lo)
                            ins.then_inc(used if (t, half) == (1, 1) else sem("sk"), 1)
                stage(eng, ST[f"wq{l}"])
                eng.wait_ge(sem("sel3"), l + 1)
                for k in range(3):
                    for t in range(TT):
                        at = k * T + t * P
                        ins = nc.tensor.transpose(st[:, at // 512, at % 512:at % 512 + P],
                                                  sel3[:, k, t * P:(t + 1) * P], ident)
                ins.then_inc(sem("sel_psum"), 1)
                stage(eng, ST[f"topk{l}"])

                def token_gates(b, i=0):
                    eng.wait_ge(sem("hot"), i * 2 + (64 * l + b + 1))
                    for k in range(4):
                        ins = mm(st[:, b, k * P:(k + 1) * P], hot_l[:, b, k * P:(k + 1) * P],
                                 hot_r[:, b, k * P:(k + 1) * P], start=True, stop=True)
                    ins.then_inc(sem("g_psum"), 1)

                for b in range(2):
                    token_gates(b)
                with eng.Fori(1, T // 8) as i:
                    for b in range(2):
                        eng.wait_ge(sem("g_out"), i * 2 + (64 * l + b - 1))
                        token_gates(b, i)
                stage(eng, ST[f"gates{l}"])

                base = U + O_PEER
                clear_acc()

                def body(j, i=None, per=0):
                    tile(st[:, (j + 1) % 2, 0:T], base + 1 + 2 * j, i, per)
                    eng.wait_ge(sem("gated_lo"), plus(i, 2, NKEYS * l + j + 1))
                    accumulate(base + 2 + 2 * j, j % 2, i, per)

                tile(st[:, 0, 0:T], base)
                body(0)
                with eng.Fori(0, NKEYS // 2 - 1) as i:
                    for j in range(2):
                        body(1 + j, i, 4)
                eng.wait_ge(sem("gated_lo"), NKEYS * l + NKEYS)
                accumulate(base + 2 * NKEYS - 1, (NKEYS - 1) % 2, last=True)
                stage(eng, ST[f"peer{l}"])
            norm()


def _columns(a):
    return np.asarray(a).reshape(-1, P).T


def _out_tiles(w):
    return w.reshape(8, P, -1, P).transpose(2, 1, 0, 3).reshape(-1, P, UNIT)


def _row_tiles(w):
    return w.reshape(-1, P, UNIT)


def _constants():
    f = np.arange(P)
    tok = np.arange(T)
    dist = tok[:, None] - tok[None, :]
    dist = np.where(dist >= 0, dist, -NEG).astype(np.float32).reshape(TT, P, T).transpose(1, 0, 2).reshape(P, -1)
    onecol = np.zeros((P, 31), np.float32)
    onecol[:, 15] = 1
    is_q = (f < HEADS)[:, None]
    one = np.ones((P, 1), np.float32)
    parts = dict(ident=np.eye(P), ones=np.ones((P, P)), iota=np.tile(f, (P, 1)), dist=dist, onecol=onecol,
                 iota16=np.tile(np.arange(16), (P, 1)), eps=one * 1e-6, qk_scale=np.where(is_q, 128.0, 1.0),
                 qk_eps=np.where(is_q, 128e-6, 1e-6))
    k1 = np.concatenate([parts[n] for n in _K1], 1).astype(np.float32)
    j, i = f[:, None], f[None, :]
    levels = [((j // (2 * b) == i // (2 * b)) & (j % (2 * b) < b) & (i % (2 * b) >= b)) for b in
              (1 << lv for lv in range(LEVELS))]
    inv = np.concatenate([1.0 / np.minimum(tok + 1, w) for w in POOL_WINDOWS])
    select = np.zeros((P, 16, P))
    for h in range(16):
        select[h, h] = 1
    parts = dict(upto=j <= i, future=np.where(j <= i, 0, NEG), levels=np.concatenate(levels, 1),
                 inv_count=np.tile(inv, (P, 1)), select=select.reshape(P, -1))
    k2 = np.concatenate([parts[n] for n in _K2], 1).astype(np.float32)
    return k1, k2


def _weights(a):
    w = np.empty((N_UNITS, P, UNIT), np.float32)

    def put(at, units):
        w[at:at + len(units)] = units

    put(U_ADA, a["ada_w"][0].reshape(8, P, -1, UNIT).transpose(2, 0, 1, 3).reshape(-1, P, UNIT))
    for l in range(LAYERS):
        put(U_ADA + N_ADA1 + l * N_ADA2,
            a["w_ada_2"][l].reshape(8, P, -1, UNIT).transpose(2, 0, 1, 3).reshape(-1, P, UNIT))
    for base, w_in, w_out in ((U_FFN1, "ffn1_w_in", "ffn1_w_out"), (U_FFN2, "ffn2_w_in", "ffn2_w_out")):
        up = _out_tiles(a[w_in][0])
        down = _row_tiles(a[w_out][0])
        w[base] = up[0]
        w[base + 1] = up[FT]
        w[base + 2:base + N_FFN - 1:3] = up[1:FT]
        w[base + 3:base + N_FFN - 1:3] = up[FT + 1:]
        w[base + 4:base + N_FFN - 1:3] = down[:FT - 1]
        w[base + N_FFN - 1] = down[FT - 1]
    m = a["mix_w_in"][0]
    ba = 512 + 4 * D
    put(U_MIX, _out_tiles(m[:, :ba]))
    put(U_MIX + 36, _out_tiles(m[:, ba + 16:]))
    small_ba = m[:, ba:ba + 16].reshape(8, P, 16).transpose(1, 0, 2).reshape(P, -1)
    pool_w = a["pool_w"][0].transpose(1, 0, 2).reshape(P, -1)
    put(U_POOLP, _row_tiles(a["pool_proj"][0]))
    put(U_DNP, _row_tiles(a["dn_proj"][0]))
    put(U_MIXO, _row_tiles(a["mix_w_out"][0]))
    for l in range(LAYERS):
        U = U_L2 + l * N_L2
        tiles = _out_tiles(a["w_in_2"][l])
        put(U + O_QK, tiles[0:8])
        put(U + O_V, tiles[8:12])
        put(U + O_REST, tiles[12:])
        put(U + O_AP, _row_tiles(a["w_attn_proj_2"][l]))
        put(U + O_CP, _row_tiles(a["w_conv_proj_2"][l]))
        put(U + O_OUT, _row_tiles(a["w_out_2"][l]))
        put(U + O_WQ, _out_tiles(a["w_query_2"][l]))
        keys = a["sub_keys_2"][l].reshape(16, NKEYS, P).transpose(2, 0, 1).reshape(P, 2, UNIT)
        put(U + O_SK, keys.transpose(1, 0, 2))
        u = a["expert_u_2"][l].reshape(NKEYS, NKEYS, 8, P).transpose(1, 3, 2, 0)
        v = a["expert_v_2"][l].reshape(NKEYS, NKEYS, D).transpose(1, 0, 2)
        base = U + O_PEER
        w[base] = u[0].reshape(P, UNIT)
        w[base + 1:base + 2 * NKEYS - 1:2] = u[1:].reshape(NKEYS - 1, P, UNIT)
        w[base + 2:base + 2 * NKEYS - 1:2] = v[:-1]
        w[base + 2 * NKEYS - 1] = v[-1]
    return w, np.concatenate([small_ba, pool_w], 1)


def kernel(**inputs):
    import concourse.bacc as bacc
    from concourse.bass_utils import run_bass_kernel_spmd

    a = {n: np.asarray(x) for n, x in inputs.items()}
    weights, smallw = _weights(a)

    def row(name):
        return np.broadcast_to(a[name].reshape(1, -1), (P, a[name].size))

    cols = dict(c=_columns(a["c"]), c2=_columns(a["c_2"]), ada_b=_columns(a["ada_b"]), b_ada2=_columns(a["b_ada_2"]),
                norm_g=_columns(a["norm_g"]), final_g=_columns(a["final_g"]), conv_w=_columns(a["conv_w"]),
                pool_scale=_columns(a["pool_scale"]), dn_g=_columns(a["dn_norm_g"]), a_log=row("a_log"),
                dt_bias=row("dt_bias"), n1g2=_columns(a["norm1_g_2"]), n2g2=_columns(a["norm2_g_2"]),
                conv_w2=_columns(a["conv_w_2"]), final_g2=_columns(a["final_g_2"]))
    x = a["x"][0].reshape(T, DT, P).transpose(2, 1, 0).reshape(P, -1)
    params = np.concatenate([cols[n] for n in _COLS] + [x], 1)
    k1, k2 = _constants()
    arrays = {"weights": weights, "params": params, "const1": k1, "const2": k2, "smallw": smallw}
    arrays = {n: np.ascontiguousarray(v, dtype=np.float32) for n, v in arrays.items()}

    nc = bacc.Bacc("TRN2", target_bir_lowering=False, num_devices=1)
    args = [nc.dram_tensor(n, v.shape, F32, kind="ExternalInput").ap() for n, v in arrays.items()]
    out = nc.dram_tensor("out", (P, DT * T), F32, kind="ExternalOutput").ap()
    build(nc, *args, out)
    r = run_bass_kernel_spmd(nc, [arrays], core_ids=[0])
    y = np.asarray(r.results[0]["out"])
    return y.reshape(P, DT, T).transpose(2, 1, 0).reshape(1, T, D)
```

```python
from contextlib import ExitStack

import numpy as np

import concourse.bass as bass
from concourse import mybir

ALU = mybir.AluOpType
ACT = mybir.ActivationFunctionType
F32 = mybir.dt.float32
F32R = mybir.dt.float32r
BF16 = mybir.dt.bfloat16
U32 = mybir.dt.uint32
AX = mybir.AxisListType.X

P = 128
T = 256
TT = T // P
D = 1024
DT = D // P
FFN = 2816
FT = FFN // P
POOL_WINDOWS = (2, 4, 8, 16)
NPOOL = len(POOL_WINDOWS)
PADP = 16
HEADS = 8
CONV = 4
CONV2 = 3
LEVELS = 7
AH, AHD = 8, 64
LAYERS = 2
NKEYS = 128
TOPK = 16
PAIRS = HEADS * TOPK
HALF = NKEYS // 2
GROUP = 8
TURNS = T // GROUP
assert 2 * TURNS == HALF and TURNS % 2 == 0
NEG = -1e30

UNIT = 1024
RING = 4
PACE = 960
N_ADA1, N_ADA2 = 72, 48
U_ADA = 0
U_FFN1 = U_ADA + N_ADA1 + LAYERS * N_ADA2
N_FFN = 3 * FT
U_MIX = U_FFN1 + N_FFN
N_MIX = 52
U_POOLP = U_MIX + N_MIX
U_DNP = U_POOLP + 4
U_MIXO = U_DNP + 8
U_FFN2 = U_MIXO + 8
U_L2 = U_FFN2 + N_FFN
O_QK, O_V, O_REST, O_AP, O_CP, O_OUT, O_WQ, O_SK, O_PEER = 0, 8, 12, 40, 44, 48, 56, 72, 74
N_L2 = O_PEER + 2 * NKEYS
N_UNITS = U_L2 + LAYERS * N_L2
N_BLOCKS = U_FFN1 // 8
assert N_UNITS % RING == 0

_COLS = {}


def _layout():
    at = 0
    for name, n in (("c", 8), ("c2", 8), ("ada_b", N_ADA1), ("b_ada2", LAYERS * N_ADA2), ("norm_g", 24),
                    ("final_g", 8), ("conv_w", CONV * 24), ("pool_scale", 4), ("dn_g", 1), ("a_log", 8),
                    ("dt_bias", 8), ("n1g2", 16), ("n2g2", 16), ("conv_w2", LAYERS * CONV2 * 4), ("final_g2", 8)):
        _COLS[name] = (at, n)
        at += n
    return at


N_PAR = _layout()

_K1 = {}


def _layout1():
    at = 0
    for name, n in (("ident", 128), ("ones", 128), ("iota", 128), ("dist", TT * T), ("onecol", 31),
                    ("iota16", 16), ("eps", 1), ("qk_scale", 1), ("qk_eps", 1)):
        _K1[name] = (at, n)
        at += n
    return at


N_K1 = _layout1()
_K2 = {}


def _layout2():
    at = 0
    for name, n in (("upto", 128), ("future", 128), ("levels", LEVELS * 128), ("inv_count", NPOOL * T),
                    ("select", 16 * 128)):
        _K2[name] = (at, n)
        at += n
    return at


N_K2 = _layout2()
N_SMALLW = 8 * 16 + NPOOL * 128
ARENA = T * NKEYS
K2_AT = ARENA - N_K2 - N_SMALLW
EXTRA = 3328


def build(nc, weights, params, const1, const2, smallw, out):
    with ExitStack() as ctx:
        def sb(name, shape, dt=F32):
            return ctx.enter_context(nc.sbuf_tensor(name, shape, dt))

        sems = {}

        def sem(name):
            if name not in sems:
                sems[name] = ctx.enter_context(nc.semaphore(name))
            return sems[name]

        ring = sb("ring", [P, RING, UNIT])
        x_t = sb("x_t", [P, DT, T])
        w_hi = sb("w_hi", [P, 2, UNIT], F32R)
        w_lo = sb("w_lo", [P, 2, UNIT], F32R)
        h_hi = sb("h_hi", [P, DT, T], F32R)
        h_lo = sb("h_lo", [P, DT, T], F32R)
        act_hi = sb("act_hi", [P, 2, T], F32R)
        act_lo = sb("act_lo", [P, 2, T], F32R)
        arena = sb("arena", [P, ARENA])
        extra = sb("extra", [P, EXTRA])
        par = sb("par", [P, N_PAR])
        k1 = sb("k1", [P, N_K1])
        mod = sb("mod", [P, N_ADA1 + LAYERS * N_ADA2])
        nscale = sb("nscale", [P, 7 * 8])
        half_gate = sb("half_gate", [P, 16])
        sc = sb("sc", [P, 8])
        zrow = sb("zrow", [1, P], BF16)
        acc = ctx.enter_context(nc.psum_tensor("acc", [P, 4, 512], F32))
        st = ctx.enter_context(nc.psum_tensor("st", [P, 4, 512], F32))
        acc_t = acc[:, :, :].rearrange("p b (u t) -> p (b u) t", u=2)

        def pc(name, i=0, n=None):
            at, size = _COLS[name]
            return par[:, at + i:at + i + (size - i if n is None else n)]

        def kc(name):
            at, n = _K1[name]
            return k1[:, at:at + n]

        def k2c(name):
            at, n = _K2[name]
            return arena[:, K2_AT + at:K2_AT + at + n]

        def ar(at, *shape, base=None):
            n = int(np.prod(shape))
            v = (arena if base is None else base)[:, at:at + n]
            if len(shape) == 2:
                v = v.rearrange("p (a b) -> p a b", b=shape[1])
            elif len(shape) == 3:
                v = v.rearrange("p (a b c) -> p a b c", b=shape[1], c=shape[2])
            return v

        ident, ones = kc("ident"), kc("ones")
        upto, future = k2c("upto"), k2c("future")
        level_mask = k2c("levels").rearrange("p (l i) -> p l i", l=LEVELS)
        inv_count = k2c("inv_count").rearrange("p (g t) -> p g t", g=NPOOL)
        select = k2c("select").rearrange("p (h i) -> p h i", h=16)
        sw_at = K2_AT + N_K2
        w_ba = arena[:, sw_at:sw_at + 128].rearrange("p (k n) -> p k n", n=16)
        w_pool = arena[:, sw_at + 128:sw_at + N_SMALLW].rearrange("p (g n) -> p g n", g=NPOOL)
        dist = kc("dist")

        gate_s = ar(0, 2, T)
        act = ar(2 * T, 2, T)
        part = ar(0, 4, UNIT)
        diag = ar(4 * UNIT, 8, P)
        nh = ar(23816, DT, T)
        std = ar(0, T, base=extra)
        rstd = ar(T, T, base=extra)

        qkv_raw = ar(0, 24, T + 3)
        qkv = ar(6216, 24, T)
        xp = ar(12360, NPOOL, PADP + T)
        pool_a = ar(13448, NPOOL, PADP + T)
        pool_b = ar(14536, NPOOL, PADP + T)
        pooled = ar(15624, NPOOL, T)
        z_s = ar(17672, 8, T)
        g_pool = ar(19720, 8, T)
        g_dn = ar(21768, 8, T)
        merged = ar(23816, 8, T)
        sq_qk = ar(0, 16, T)
        x_s = ar(0, 16, P)
        a_t = ar(2048, 16, P)
        qk_m = ar(4096, 16, P)
        bv = ar(12360, 16, P)
        k_dec = ar(14408, 8, P)
        q_dec = ar(15432, 8, P)
        s1 = ar(16456, 8, P)
        v_new = ar(10312, 16, P)
        resid = ar(2048, 8, P)
        d_m = ar(19720, 16, P)
        d_t = ar(0, 16, P, base=extra)
        off_t = [ar(6216, 16, P), ar(10312, 16, P)]
        o_t = ar(0, 8, T)
        sq_o = ar(0, 8, T, base=extra)
        small = 25864
        rn = ar(small, T)
        rn_s = ar(small + 256, T)
        rows = ar(small + 512, 512)
        ba_b = ar(small + 1024, 2, 8)
        ba_g = ar(small + 1040, 2, 8)
        sp1 = ar(small + 1056, 2, 8)
        sp2 = ar(small + 1072, 2, 8)
        sp3 = ar(small + 1088, 2, 8)
        neg_a = ar(small + 1104, 8)
        g_col = ar(small + 1120, 2, 8)
        g_end = ar(small + 1136, 8)
        k_sc = ar(small + 1144, 8)
        nbe = ar(small + 1152, 8)
        assert small + 1160 <= K2_AT
        dec = [ar(2048 + T * b, T, base=extra) for b in range(2)]
        tmp = [ar(2560 + T * b, T, base=extra) for b in range(2)]
        egb = [ar(3072 + P * b, P, base=extra) for b in range(2)]

        qk2 = ar(0, 8, T)
        v2 = ar(2048, 2, 512)
        bch = ar(3072, 12, T)
        ga2 = ar(6144, 8, T)
        gc2 = ar(8192, 8, T)
        zc = ar(10240, 4, T + 2)
        yc = ar(11272, 4, T)
        s_b = [ar(12296, 2, T), ar(12808, 2, T)]
        p_b = [ar(13320, 2, T), ar(13832, 2, T)]
        pt_b = [ar(14344, 384), ar(14728, 384)]
        vt = ar(15112, 4, T)
        mrg2 = ar(16136, 8, T)
        stat = ar(18184, 8, 8)

        experts = arena[:, :].rearrange("p (n t) -> p n t", t=T)
        half1 = ARENA // 2
        qq = ar(0, 16, T)
        scores = ar(half1, 32, NKEYS)
        cand = ar(half1, 16, TOPK * TOPK)
        tv = ar(half1 + 4096, 32, TOPK)
        ti = ar(half1 + 4608, 32 * TOPK).bitcast(U32).rearrange("p (a b) -> p a b", b=TOPK)
        tif = ar(half1 + 5120, 32, TOPK)
        best = ar(half1 + 5632, 16, TOPK)
        bpos = ar(half1 + 5888, 16 * TOPK).bitcast(U32).rearrange("p (a b) -> p a b", b=TOPK)
        pos_u = ar(half1 + 6144, 2 * 256).bitcast(U32).rearrange("p (a b) -> p a b", b=256)
        pos_f = ar(half1 + 6656, 2, 256)
        sel3 = ar(half1 + 7168, 3, 256)
        ge_ = ar(half1 + 7936, 256)
        gsum = ar(half1 + 8192, 16)
        ginv = ar(half1 + 8208, 16)
        hot = ar(half1 + 8224, 2, PAIRS * TOPK)
        selt = ar(512, 3, T, base=extra)
        hot_l = ar(1280, GROUP, NKEYS, base=extra)
        hot_r = ar(1280 + GROUP * NKEYS, GROUP, HALF, base=extra)

        landed = [sem(f"landed{s}") for s in range(RING)]
        hi_ready = sem("w_hi_ready")
        taken = sem("w_taken")
        used = sem("weights_used")

        def nth(u):
            return u - U_FFN1 + 1

        def landed_count(u, i=None, per=0):
            assert per % RING == 0
            n = 16 * (u // RING + 1)
            return n if i is None else i * (16 * (per // RING)) + n

        def plus(i, per, n):
            return n if i is None else i * per + n
        stage_done = sem("stage_done")

        def stage(eng, n):
            eng.drain().then_inc(stage_done, 1)
            eng.wait_ge(stage_done, 4 * n)

        def linker(eng, name):
            chain = sem(name)
            count = [0]

            def link(ins):
                ins.then_inc(chain, 1)
                count[0] += 1
                eng.wait_ge(chain, count[0])
            return link

        ST = {}
        for name in ("ada", "ffn0", "mix_proj", "mix_pool", "mix_norm", "mix_heads", "mix_solve", "mix_state", "mix_o",
                     "mix_out", "ffn1", "final1"):
            ST[name] = len(ST) + 1
        for l in range(LAYERS):
            for name in ("proj", "attn", "out", "wq", "peer_a", "peer_b", "peer_c", "peer_d"):
                ST[f"{name}{l}"] = len(ST) + 1

        def shift1(s):
            return mod[:, 24 * s:24 * s + 8]

        def scale1(s):
            return mod[:, 24 * s + 8:24 * s + 16]

        def gate1(s):
            return mod[:, 24 * s + 16:24 * s + 24]

        def mod2(l, k):
            at = N_ADA1 + N_ADA2 * l + 8 * k
            return mod[:, at:at + 8]

        block = ctx.enter_context(nc.Block())

        @block.sync
        def _(sp):
            for s in range(RING):
                sp.dma_start(ring[:, s, :], weights[s]).then_inc(landed[s], 16)
            with sp.Fori(1, N_UNITS // RING) as i:
                for s in range(RING):
                    sp.wait_ge(taken, i * RING + (s + 1 - RING))
                    sp.dma_start(ring[:, s, :],
                                 weights[bass.ds(i * RING + s, 1), :, :].rearrange("a p n -> p (a n)"))\
                      .then_inc(landed[s], 16)

        @block.scalar
        def _(eng):
            link = linker(eng, "act_chain")
            nc_a = nc.scalar
            eng.dma_start(k1[:, :], const1).then_inc(sem("k1_in"), 16)
            eng.dma_start(arena[:, K2_AT:K2_AT + N_K2], const2).then_inc(sem("k2_in"), 16)
            eng.dma_start(arena[:, sw_at:sw_at + N_SMALLW], smallw).then_inc(sem("sw_in"), 16)

            def hi(u, i=None, per=0):
                eng.wait_ge(landed[u % RING], landed_count(u, i, per))
                if u >= U_FFN1 + 2:
                    eng.wait_ge(used, plus(i, per, nth(u - 2)))
                nc_a.activation(w_hi[:, u % 2, :], ring[:, u % RING, :], ACT.Copy).then_inc(hi_ready, 1)

            def step(u, i=None, per=0):
                if u + 2 < N_UNITS:
                    hi(u + 2, i, per)
                else:
                    eng.wait_ge(used, nth(u))

            def steps(u, n):
                for k in range(n):
                    step(u + k)

            def split(name, before, src, n):
                for half in range(2):
                    t = slice(half * n // 2, (half + 1) * n // 2)
                    eng.wait_ge(sem(name + "_full"), before + half + 1)
                    nc_a.activation(h_hi[:, t, :], src[:, t, :], ACT.Copy).then_inc(sem(name + "_hi"), 1)

            def norm(n, m=None):
                eng.wait_ge(sem("sumsq"), n + 1)
                nc_a.activation(std, st[:, 3, 0:T], ACT.Sqrt, scale=1.0 / D, bias=kc("eps")).then_inc(sem("std"), 1)
                if m is not None:
                    split("norm", 2 * m, nh, DT)

            eng.wait_ge(sem("par_in"), 16)
            eng.wait_ge(sem("k1_in"), 16)
            nc_a.activation(sc[:, :], pc("c"), ACT.Silu).then_inc(sem("silu_c"), 1)
            hi(U_FFN1)
            hi(U_FFN1 + 1)
            stage(eng, ST["ada"])

            def ffn(f):
                norm((0, 2)[f], (0, 2)[f])
                base = (U_FFN1, U_FFN2)[f]

                def silu(b):
                    nc_a.activation(gate_s[:, b, :], st[:, b, 0:T], ACT.Silu).then_inc(sem("silu_gate"), 1)

                def upper(j, i=None):
                    eng.wait_ge(sem("act"), plus(i, 4, FT * f + j + 1))
                    nc_a.activation(act_hi[:, j % 2, :], act[:, j % 2, :], ACT.Copy).then_inc(sem("act_hi"), 1)

                def body(j, i=None, per=0):
                    silu((j + 1) % 2)
                    step(base + 3 + 3 * j, i, per)
                    upper(j + 1, i)
                    step(base + 4 + 3 * j, i, per)
                    step(base + 5 + 3 * j, i, per)

                step(base)
                silu(0)
                step(base + 1)
                upper(0)
                step(base + 2)
                body(0)
                with eng.Fori(0, (FT - 2) // 4) as i:
                    for j in range(4):
                        body(1 + j, i, 12)

            ffn(0)
            stage(eng, ST["ffn0"])

            norm(1, 1)
            for p in range(14):
                steps(U_MIX + 2 * p, 2)
                src = st[:, p % 4, :].rearrange("p (u t) -> p u t", u=2)
                if p < 2:
                    dst = xp[:, 2 * p:2 * p + 2, PADP:PADP + T]
                else:
                    dst = qkv_raw[:, 2 * (p - 2):2 * (p - 1), 3:3 + T]
                nc_a.activation(dst, src, ACT.Copy).then_inc(sem("proj_out"), 1)
                if p >= 4:
                    m = p - 4
                    eng.wait_ge(sem("conv"), m + 1)
                    nc_a.activation(qkv[:, 2 * m:2 * m + 2, :], qkv[:, 2 * m:2 * m + 2, :], ACT.Silu)\
                        .then_inc(sem("qkv_silu"), 1)
            for p in range(14, 26):
                steps(U_MIX + 2 * p, 2)
                if p < 16:
                    m = p - 4
                    eng.wait_ge(sem("conv"), m + 1)
                    nc_a.activation(qkv[:, 2 * m:2 * m + 2, :], qkv[:, 2 * m:2 * m + 2, :], ACT.Silu)\
                        .then_inc(sem("qkv_silu"), 1)
                m = p - 14
                dst = (z_s, g_pool, g_dn)[m // 4][:, 2 * (m % 4):2 * (m % 4) + 2, :]
                src = st[:, p % 4, :].rearrange("p (u t) -> p u t", u=2)
                nc_a.activation(dst, src, ACT.Silu if m < 4 else ACT.Sigmoid).then_inc(sem("proj_out"), 1)
            eng.wait_ge(sem("ba_psum"), 1)
            ba_ps = acc[:, 0, 0:32].rearrange("p (c n) -> p c n", n=16)
            nc_a.activation(ba_b, ba_ps[:, :, 0:8], ACT.Sigmoid).then_inc(sem("beta"), 1)
            link(nc_a.activation(neg_a, pc("a_log"), ACT.Exp))
            eng.wait_ge(sem("a_in"), 1)
            link(nc_a.activation(sp2, sp1, ACT.Abs))
            link(nc_a.activation(sp2, sp2, ACT.Exp, scale=-1.0))
            nc_a.activation(sp3, sp2, ACT.Ln, bias=1.0).then_inc(sem("ln1p"), 1)
            stage(eng, ST["mix_proj"])
            eng.wait_ge(sem("pool_mm"), 1)
            for g in range(NPOOL):
                nc_a.activation(h_hi[:, g, :], st[:, g // 2, (g % 2) * T:(g % 2) * T + T], ACT.Copy,
                                scale=pc("pool_scale", g, 1)).then_inc(sem("ya0_hi"), 1)
            steps(U_POOLP, 4)
            stage(eng, ST["mix_pool"])

            eng.wait_ge(sem("sum_qk"), 1)
            nc_a.activation(rn_s[0:16, :], st[0:16, 0, 0:T], ACT.Sqrt, scale=kc("qk_scale")[0:16, :],
                            bias=kc("qk_eps")[0:16, :]).then_inc(sem("std_qk"), 1)
            stage(eng, ST["mix_norm"])

            for h in range(HEADS):
                b = h % 2
                eng.wait_ge(sem("dec_arg"), h + 1)
                nc_a.activation(dec[b], dec[b], ACT.Exp).then_inc(sem("dec"), 1)
                nc_a.activation(egb[b], st[:, b, 128:256], ACT.Exp).then_inc(sem("dec"), 1)
            eng.wait_ge(sem("k_arg"), 1)
            link(nc_a.activation(k_sc, k_sc, ACT.Exp))
            link(nc_a.activation(nbe, g_col[:, 1, :], ACT.Exp))
            for q in range(6):
                eng.wait_ge(sem("tok_t"), q + 1)
                for j in range(4):
                    n = 4 * q + j
                    src = acc[:, q % 4, j * 128:(j + 1) * 128]
                    if n < 16:
                        ins = nc_a.activation(bv[:, n, :], src, ACT.Copy, scale=ba_b[:, n // 8, n % 8:n % 8 + 1])
                    else:
                        ins = nc_a.activation(k_dec[:, n - 16, :], src, ACT.Copy, scale=k_sc[:, n - 16:n - 15])
                ins.then_inc(sem("tok_out"), 1)
            stage(eng, ST["mix_heads"])

            for lv in range(LEVELS):
                for g in range(4):
                    eng.wait_ge(sem("lv_x"), 4 * lv + g + 1)
                    nc_a.activation(x_s[:, 4 * g:4 * g + 4, :], st[:, g, :].rearrange("p (a b) -> p a b", b=128),
                                    ACT.Copy).then_inc(sem("lv_xs"), 1)
            stage(eng, ST["mix_solve"])

            def out_of(dst, src, name):
                nc_a.activation(dst, src.rearrange("p (a b) -> p a b", b=128), ACT.Copy).then_inc(sem(name), 1)

            for g in range(2):
                eng.wait_ge(sem("vn0_psum"), g + 1)
                out_of(v_new[:, 4 * g:4 * g + 4, :], acc[:, g, :], "vn0")
            for g in range(2):
                eng.wait_ge(sem("s1_psum"), g + 1)
                out_of(s1[:, 4 * g:4 * g + 4, :], acc[:, 2 + g, :], "s1")
            for g in range(2):
                eng.wait_ge(sem("vn1_psum"), g + 1)
                out_of(v_new[:, 8 + 4 * g:12 + 4 * g, :], acc[:, g, :], "vn1")
            for m in range(4):
                eng.wait_ge(sem("o_psum"), m + 1)
                nc_a.activation(o_t[:, 2 * m:2 * m + 2, :], st[:, m, :].rearrange("p (u t) -> p u t", u=2),
                                ACT.Copy).then_inc(sem("o_t"), 1)
            stage(eng, ST["mix_state"])
            eng.wait_ge(sem("sum_o"), 1)
            nc_a.activation(rn_s[0:8, :], st[0:8, 0, 0:T], ACT.Sqrt, scale=1.0 / P, bias=kc("eps")[0:8, :])\
                .then_inc(sem("std_o"), 1)
            split("o", 0, o_t, 8)
            stage(eng, ST["mix_o"])
            steps(U_DNP, 8)
            split("merged", 0, merged, 8)
            steps(U_MIXO, 8)
            stage(eng, ST["mix_out"])

            ffn(1)
            stage(eng, ST["ffn1"])
            norm(3)
            stage(eng, ST["final1"])

            for l in range(LAYERS):
                U = U_L2 + N_L2 * l
                norm(4 + 2 * l, 3 + 2 * l)
                for p in range(20):
                    steps(U + O_QK + 2 * p, 2)
                    src = st[:, p % 4, :].rearrange("p (u t) -> p u t", u=2)
                    if p < 4:
                        dst = qk2[:, 2 * p:2 * p + 2, :]
                    elif p < 6:
                        dst = vt[:, 2 * p - 8:2 * p - 6, :]
                    elif p < 12:
                        dst = bch[:, 2 * p - 12:2 * p - 10, :]
                    else:
                        dst = (ga2, gc2)[(p - 12) // 4][:, 2 * ((p - 12) % 4):2 * ((p - 12) % 4) + 2, :]
                    nc_a.activation(dst, src, ACT.Copy if p < 12 else ACT.Sigmoid).then_inc(sem("proj2"), 1)
                stage(eng, ST[f"proj{l}"])

                eng.wait_ge(sem("v_tok"), l + 1)
                nc_a.activation(v2, acc[:, 0:2, :], ACT.Copy).then_inc(sem("v2"), 1)
                for h in range(AH):
                    b = h % 2
                    n = AH * l + h
                    eng.wait_ge(sem("smax"), n + 1)
                    for q in range(2):
                        nc_a.activation(p_b[b][:, q, :], s_b[b][:, q, :], ACT.Exp, scale=AHD ** -0.5,
                                        bias=stat[:, b, 2 + q:3 + q], accum_out=stat[:, b, 4 + q:5 + q])\
                            .then_inc(sem("pexp"), 1)
                    eng.wait_ge(sem("pt_psum"), n + 1)
                    nc_a.activation(pt_b[b], acc[:, b, 0:384], ACT.Copy).then_inc(sem("pt"), 1)
                for m in range(2):
                    eng.wait_ge(sem("pv"), 8 * l + 4 * m + 4)
                    nc_a.activation(h_hi[:, 2 * m:2 * m + 2, :], acc[:, 2 + m, :].rearrange("p (u t) -> p u t", u=2),
                                    ACT.Copy).then_inc(sem("y_hi"), 1)
                eng.wait_ge(sem("yc_full"), l + 1)
                nc_a.activation(h_hi[:, 4:8, :], yc, ACT.Copy).then_inc(sem("yc_hi"), 1)
                stage(eng, ST[f"attn{l}"])
                steps(U + O_AP, 8)
                split("mrg2", 2 * l, mrg2, 8)
                steps(U + O_OUT, 8)
                stage(eng, ST[f"out{l}"])

                norm(5 + 2 * l, 4 + 2 * l)
                for p in range(8):
                    steps(U + O_WQ + 2 * p, 2)
                    nc_a.activation(qq[:, 2 * p:2 * p + 2, :], st[:, p % 4, :].rearrange("p (u t) -> p u t", u=2),
                                    ACT.Copy).then_inc(sem("qq"), 1)
                for u in range(2):
                    for t in range(TT):
                        for half in range(2):
                            if (t, half) == (1, 1):
                                step(U + O_SK + u)
                            else:
                                eng.wait_ge(sem("sk"), 6 * l + 3 * u + 2 * t + half + 1)
                            nc_a.activation(scores[:, 16 * t + 8 * u + 4 * half:16 * t + 8 * u + 4 * half + 4, :],
                                            acc[:, 2 * t + half, :].rearrange("p (a b) -> p a b", b=128), ACT.Copy)\
                                .then_inc(sem("scores"), 1)
                stage(eng, ST[f"wq{l}"])
                base = U + O_PEER
                n_key = NKEYS * l

                def gelu_of(n, i=None):
                    dst = experts[:, n, :] if i is None else \
                        experts[:, bass.ds(i * 4 + n, 1), :].rearrange("p a t -> p (a t)")
                    nc_a.activation(dst, st[:, n % 2, 0:T], ACT.Gelu_apprx_tanh).then_inc(sem("gelu"), 1)

                def u_half(first):
                    step(base + first)
                    with eng.Fori(0, HALF // 4 - 1) as i:
                        for k in range(4):
                            gelu_of(first + k, i)
                            step(base + first + k + 1, i, 4)
                    for n in range(first + HALF - 4, first + HALF):
                        gelu_of(n)
                        if n + 1 < first + HALF:
                            step(base + n + 1)

                u_half(0)
                eng.wait_ge(sem("best_c"), l + 1)
                nc_a.activation(ge_, ge_, ACT.Exp).then_inc(sem("gexp"), 1)
                eng.wait_ge(sem("sel_psum"), l + 1)
                nc_a.activation(selt, st[:, 2:4, :].rearrange("p a b -> p (a b)")[:, 0:3 * T]
                                .rearrange("p (k t) -> p k t", k=3), ACT.Copy).then_inc(sem("selt"), 1)
                stage(eng, ST[f"peer_a{l}"])
                u_half(HALF)
                stage(eng, ST[f"peer_b{l}"])

                def upper(n, i=None):
                    src = experts[:, n, :] if i is None else \
                        experts[:, bass.ds(i * 4 + n, 1), :].rearrange("p a t -> p (a t)")
                    nc_a.activation(act_hi[:, n % 2, :], src, ACT.Copy).then_inc(sem("gated_hi"), 1)

                def v_half(first):
                    v_base = base + NKEYS
                    upper(first)
                    upper(first + 1)
                    with eng.Fori(0, HALF // 4 - 1) as i:
                        for k in range(4):
                            eng.wait_ge(used, plus(i, 4, nth(v_base + first + k)))
                            upper(first + k + 2, i)
                            step(v_base + first + k, i, 4)
                    for n in range(first + HALF - 4, first + HALF):
                        if n + 2 < first + HALF:
                            eng.wait_ge(used, nth(v_base + n))
                            upper(n + 2)
                        step(v_base + n)

                v_half(0)
                stage(eng, ST[f"peer_c{l}"])
                v_half(HALF)
                stage(eng, ST[f"peer_d{l}"])
            norm(8)

        @block.vector
        def _(eng):
            link = linker(eng, "dve_chain")
            v = nc.vector
            v.memset(zrow[:, :], 0.0).then_inc(sem("zrow"), 1)

            def lo(u, i=None, per=0):
                eng.wait_ge(hi_ready, plus(i, per, nth(u)))
                v.tensor_tensor(w_lo[:, u % 2, :], ring[:, u % RING, :], w_hi[:, u % 2, :], ALU.subtract)\
                    .then_inc(taken, 1)

            def step(u, i=None, per=0):
                if u + 2 < N_UNITS:
                    lo(u + 2, i, per)
                else:
                    eng.wait_ge(used, nth(u))

            def steps(u, n):
                for k in range(n):
                    step(u + k)

            def split(name, before, src, n, at=0):
                for half in range(2):
                    t = slice(half * n // 2, (half + 1) * n // 2)
                    eng.wait_ge(sem(name + "_hi"), before + half + 1)
                    v.tensor_tensor(h_lo[:, t, :], src[:, t, :], h_hi[:, t, :], ALU.subtract)\
                        .then_inc(sem(name + "_lo"), 1)

            def norm(n, a, b, dst, m=None):
                v.tensor_tensor(nh, x_t[:, :, :], x_t[:, :, :], ALU.mult).then_inc(sem("sq"), 1)
                eng.wait_ge(sem("std"), n + 1)
                link(v.reciprocal(rstd, std))
                for t in range(DT):
                    ins = v.scalar_tensor_tensor(out=dst[:, t, :], in0=x_t[:, t, :], scalar=a[:, t:t + 1], in1=rstd,
                                                 op0=ALU.mult, op1=ALU.mult)
                if b is None:
                    ins.then_inc(sem("normed"), 1)
                    return
                link(ins)
                for t in range(DT):
                    ins = v.tensor_scalar(dst[:, t, :], dst[:, t, :], b[:, t:t + 1], None, ALU.add)
                    if t % 4 == 3:
                        ins.then_inc(sem("norm_full"), 1)
                split("norm", 2 * m, nh, DT)

            eng.wait_ge(sem("par_in"), 16)
            eng.wait_ge(sem("silu_c"), 1)
            eng.wait_ge(sem("k1_in"), 16)

            def on_diagonal(q, i=None):
                b = q % 2
                eng.wait_ge(sem("ada_psum"), plus(i, 2, q + 1))
                v.tensor_tensor(diag, st[:, 2 * b:2 * b + 2, :].rearrange("p b (u n) -> p (b u) n", n=P),
                                ident.unsqueeze(1).to_broadcast([P, 8, P]), ALU.mult).then_inc(sem("ada_diag"), 1)
                eng.wait_ge(sem("ada_diag"), plus(i, 2, q + 1))
                dst = mod[:, 8 * q:8 * q + 8] if i is None else mod[:, bass.ds(i * 16 + 8 * q, 8)]
                v.tensor_reduce(dst, diag, AX, ALU.add).then_inc(sem("ada_mod"), 1)
                eng.wait_ge(sem("ada_mod"), plus(i, 2, q + 1))

            def ada_block(q, vec, i=None):
                for k in range(8):
                    u = 8 * q + k
                    dst = part[:, 2 * (q % 2) + k % 2, :]
                    eng.wait_ge(landed[u % RING], landed_count(u, i, 16))
                    if k < 2:
                        ins = v.tensor_scalar(dst, ring[:, u % RING, :], vec[:, k:k + 1], None, ALU.mult)
                    else:
                        eng.wait_ge(taken, plus(i, 16, u - 1))
                        ins = v.scalar_tensor_tensor(out=dst, in0=ring[:, u % RING, :], scalar=vec[:, k:k + 1],
                                                     in1=dst, op0=ALU.mult, op1=ALU.add)
                    ins.then_inc(taken, 1)
                    if k == 3 and q > 0:
                        on_diagonal(q - 1, i)

            ada_block(0, sc)
            with eng.Fori(0, (N_ADA1 // 8 - 1) // 2) as i:
                for b in range(2):
                    ada_block(1 + b, sc, i)
            with eng.Fori(0, LAYERS * N_ADA2 // 16) as i:
                for b in range(2):
                    ada_block(N_ADA1 // 8 + b, pc("c2"), i)
            on_diagonal(N_BLOCKS - 1)
            link(v.tensor_tensor(mod[:, :], mod[:, :], pc("ada_b", 0, 8 * N_BLOCKS), ALU.add))
            for s in range(3):
                v.scalar_tensor_tensor(out=nscale[:, 8 * s:8 * s + 8], in0=scale1(s), scalar=1.0,
                                       in1=pc("norm_g", 8 * s, 8), op0=ALU.add, op1=ALU.mult)
            for l in range(LAYERS):
                for k, g in ((0, "n1g2"), (1, "n2g2")):
                    at = 24 + 16 * l + 8 * k
                    v.scalar_tensor_tensor(out=nscale[:, at:at + 8], in0=mod2(l, 3 * k + 1), scalar=1.0,
                                           in1=pc(g, 8 * l, 8), op0=ALU.add, op1=ALU.mult)
            for f in range(2):
                ins = v.tensor_scalar(half_gate[:, 8 * f:8 * f + 8], gate1(2 * f), 0.5, None, ALU.mult)
            link(ins)
            lo(U_FFN1)
            lo(U_FFN1 + 1)
            eng.wait_ge(sem("x_in"), 16)
            stage(eng, ST["ada"])

            def add_to_x(gate):
                for t in range(DT):
                    ins = v.scalar_tensor_tensor(out=x_t[:, t, :], in0=acc_t[:, t, :], scalar=gate[:, t:t + 1],
                                                 in1=x_t[:, t, :], op0=ALU.mult, op1=ALU.add)
                link(ins)

            def ffn(f):
                norm((0, 2)[f], nscale[:, 16 * f:16 * f + 8], shift1(2 * f), nh, (0, 2)[f])
                base = (U_FFN1, U_FFN2)[f]

                def mult(j, i=None):
                    eng.wait_ge(sem("silu_gate"), plus(i, 4, FT * f + j + 1))
                    b = j % 2
                    v.tensor_tensor(act[:, b, :], gate_s[:, b, :], st[:, 2 + b, 0:T], ALU.mult).then_inc(sem("act"), 1)

                def lower(j, i=None):
                    eng.wait_ge(sem("act_hi"), plus(i, 4, FT * f + j + 1))
                    b = j % 2
                    v.tensor_tensor(act_lo[:, b, :], act[:, b, :], act_hi[:, b, :], ALU.subtract)\
                        .then_inc(sem("act_lo"), 1)

                def body(j, i=None, per=0):
                    step(base + 2 + 3 * j, i, per)
                    step(base + 3 + 3 * j, i, per)
                    mult(j + 1, i)
                    lower(j + 1, i)
                    step(base + 4 + 3 * j, i, per)

                step(base)
                step(base + 1)
                mult(0)
                lower(0)
                body(0)
                with eng.Fori(0, (FT - 2) // 4) as i:
                    for j in range(4):
                        body(1 + j, i, 12)
                step(base + N_FFN - 1)
                add_to_x(half_gate[:, 8 * f:8 * f + 8])

            ffn(0)
            stage(eng, ST["ffn0"])

            norm(1, nscale[:, 8:16], shift1(1), nh, 1)
            v.memset(qkv_raw[:, :, 0:3], 0.0).then_inc(sem("pad"), 1)
            eng.wait_ge(sem("pad"), 1)

            def conv(m):
                eng.wait_ge(sem("proj_out"), m + 3)
                for j in range(CONV):
                    for t in (2 * m, 2 * m + 1):
                        w = pc("conv_w", 24 * j + t, 1)
                        if j == 0:
                            ins = v.tensor_scalar(qkv[:, t, :], qkv_raw[:, t, 0:T], w, None, ALU.mult)
                        else:
                            ins = v.scalar_tensor_tensor(out=qkv[:, t, :], in0=qkv_raw[:, t, j:j + T], scalar=w,
                                                         in1=qkv[:, t, :], op0=ALU.mult, op1=ALU.add)
                    if j < CONV - 1:
                        link(ins)
                ins.then_inc(sem("conv"), 1)

            for p in range(26):
                steps(U_MIX + 2 * p, 2)
                if 3 <= p < 15:
                    conv(p - 3)
            eng.wait_ge(sem("ba_psum"), 1)
            ba_ps = acc[:, 0, 0:32].rearrange("p (c n) -> p c n", n=16)
            eng.wait_ge(sem("beta"), 1)
            v.tensor_tensor(sp1, ba_ps[:, :, 8:16], pc("dt_bias").unsqueeze(1).to_broadcast([P, 2, 8]), ALU.add)\
                .then_inc(sem("a_in"), 1)
            eng.wait_ge(sem("ln1p"), 1)
            link(v.scalar_tensor_tensor(out=sp1, in0=sp1, scalar=0.0, in1=sp3, op0=ALU.max, op1=ALU.add))
            link(v.scalar_tensor_tensor(out=ba_g, in0=sp1, scalar=-1.0,
                                        in1=neg_a.unsqueeze(1).to_broadcast([P, 2, 8]), op0=ALU.mult, op1=ALU.mult))
            stage(eng, ST["mix_proj"])

            eng.wait_ge(sem("pool_mm"), 1)
            for g in range(NPOOL):
                eng.wait_ge(sem("ya0_hi"), 2 * (g // 2) + 2)
                v.scalar_tensor_tensor(out=h_lo[:, g, :], in0=st[:, g // 2, (g % 2) * T:(g % 2) * T + T],
                                       scalar=pc("pool_scale", g, 1), in1=h_hi[:, g, :], op0=ALU.mult,
                                       op1=ALU.subtract).then_inc(sem("ya0_lo"), 1)
            v.tensor_tensor(sq_qk, qkv[:, 0:16, :], qkv[:, 0:16, :], ALU.mult).then_inc(sem("sq_qk"), 1)
            steps(U_POOLP, 4)
            link(v.tensor_tensor(merged, acc_t, g_pool, ALU.mult))
            stage(eng, ST["mix_pool"])

            eng.wait_ge(sem("std_qk"), 1)
            v.reciprocal(rn[0:16, :], rn_s[0:16, :]).then_inc(sem("rn"), 1)
            eng.wait_ge(sem("g_rows"), 1)
            v.tensor_copy(rows[0:8, :], st[0:8, 1, :]).then_inc(sem("rows"), 1)
            v.tensor_copy(g_col, st[:, 2, 0:16].rearrange("p (c n) -> p c n", n=8)).then_inc(sem("rows"), 1)
            for m in range(8):
                eng.wait_ge(sem("rn_b"), m + 1)
                v.tensor_tensor(qkv[:, 2 * m:2 * m + 2, :], qkv[:, 2 * m:2 * m + 2, :],
                                acc[:, m % 4, :].rearrange("p (u t) -> p u t", u=2), ALU.mult)\
                    .then_inc(sem("qk_n"), 1)
            stage(eng, ST["mix_norm"])

            for h in range(HEADS):
                b = h % 2
                eng.wait_ge(sem("bc"), h + 1)
                dec3 = dec[b].rearrange("p (c i) -> p c i", c=2)
                tmp3 = tmp[b].rearrange("p (c i) -> p c i", c=2)
                v.tensor_copy(g_end[:, h:h + 1], st[:, b, 127:128])
                for c in range(2):
                    ins = v.scalar_tensor_tensor(out=dec3[:, c, :], in0=st[:, b, c * 128:(c + 1) * 128],
                                                 scalar=g_col[:, c, h:h + 1], in1=future,
                                                 op0=ALU.subtract, op1=ALU.add)
                ins.then_inc(sem("dec_arg"), 1)
                eng.wait_ge(sem("dec"), 2 * h + 2)
                eng.wait_ge(sem("kkqk"), h + 1)
                kk = st[:, 2 + b, 0:256].rearrange("p (c i) -> p c i", c=2)
                qk = st[:, 2 + b, 256:512].rearrange("p (c i) -> p c i", c=2)
                link(v.tensor_tensor(tmp3, kk, dec3, ALU.mult))
                both = a_t.rearrange("p (c h) i -> p c h i", c=2)[:, :, h, :]
                v.tensor_tensor(both, tmp3, st[:, b, 256:512].rearrange("p (c i) -> p c i", c=2), ALU.mult)
                v.tensor_tensor(qk_m.rearrange("p (c h) i -> p c h i", c=2)[:, :, h, :], qk, dec3, ALU.mult)
                v.tensor_tensor(q_dec[:, h, :], qkv[:, h, 128:256], egb[b], ALU.mult).then_inc(sem("head"), 1)
            eng.wait_ge(sem("head"), HEADS)
            v.tensor_tensor(k_sc, g_end, g_col[:, 0, :], ALU.subtract).then_inc(sem("k_arg"), 1)
            v.tensor_copy(d_m, ident.unsqueeze(1).to_broadcast([P, 16, P]))
            v.tensor_copy(d_t, ident.unsqueeze(1).to_broadcast([P, 16, P]))
            stage(eng, ST["mix_heads"])

            for lv in range(LEVELS):
                for g in range(4):
                    eng.wait_ge(sem("lv_dx"), 4 * lv + g + 1)
                    b = 2 * (g % 2)
                    sl = slice(4 * g, 4 * g + 4)
                    v.tensor_tensor(d_m[:, sl, :], d_m[:, sl, :], acc[:, b, :].rearrange("p (a b) -> p a b", b=128),
                                    ALU.subtract)
                    v.tensor_tensor(d_t[:, sl, :], d_t[:, sl, :],
                                    acc[:, b + 1, :].rearrange("p (a b) -> p a b", b=128),
                                    ALU.subtract).then_inc(sem("lv_d"), 1)
            link(v.scalar_tensor_tensor(out=nbe, in0=nbe, scalar=-1.0, in1=ba_b[:, 1, :], op0=ALU.mult, op1=ALU.mult))
            stage(eng, ST["mix_solve"])

            for h in range(HEADS):
                if h % 4 == 0:
                    eng.wait_ge(sem("ks1_psum"), h // 4 + 1)
                ins = v.scalar_tensor_tensor(out=resid[:, h, :], in0=st[:, h // 4, (h % 4) * 128:(h % 4) * 128 + 128],
                                             scalar=nbe[:, h:h + 1], in1=bv[:, 8 + h, :], op0=ALU.mult, op1=ALU.add)
                if h % 4 == 3:
                    ins.then_inc(sem("resid"), 1)
            eng.wait_ge(sem("o_t"), 4)
            v.tensor_tensor(sq_o, o_t, o_t, ALU.mult).then_inc(sem("sq_o"), 1)
            stage(eng, ST["mix_state"])
            eng.wait_ge(sem("std_o"), 1)
            v.reciprocal(rn[0:8, :], rn_s[0:8, :]).then_inc(sem("rn_o"), 1)
            for m in range(4):
                eng.wait_ge(sem("rno_b"), m + 1)
                o2 = o_t[:, 2 * m:2 * m + 2, :]
                link(v.scalar_tensor_tensor(out=o2, in0=o2, scalar=pc("dn_g"),
                                            in1=acc[:, m, :].rearrange("p (u t) -> p u t", u=2),
                                            op0=ALU.mult, op1=ALU.mult))
                ins = v.tensor_tensor(o2, o2, z_s[:, 2 * m:2 * m + 2, :], ALU.mult)
                if m % 2 == 1:
                    ins.then_inc(sem("o_full"), 1)
            split("o", 0, o_t, 8)
            stage(eng, ST["mix_o"])
            steps(U_DNP, 8)
            for half in range(2):
                t = slice(4 * half, 4 * half + 4)
                link(v.tensor_tensor(g_dn[:, t, :], acc_t[:, t, :], g_dn[:, t, :], ALU.mult))
                v.tensor_tensor(merged[:, t, :], merged[:, t, :], g_dn[:, t, :], ALU.add)\
                    .then_inc(sem("merged_full"), 1)
            split("merged", 0, merged, 8)
            steps(U_MIXO, 8)
            add_to_x(gate1(1))
            stage(eng, ST["mix_out"])

            ffn(1)
            stage(eng, ST["ffn1"])
            norm(3, pc("final_g"), None, x_t)
            stage(eng, ST["final1"])

            for l in range(LAYERS):
                U = U_L2 + N_L2 * l
                norm(4 + 2 * l, nscale[:, 24 + 16 * l:32 + 16 * l], mod2(l, 0), nh, 3 + 2 * l)
                steps(U + O_QK, 40)
                stage(eng, ST[f"proj{l}"])
                for h in range(AH):
                    b = h % 2
                    n = AH * l + h
                    eng.wait_ge(sem("s_psum"), n + 1)
                    link(v.scalar_tensor_tensor(out=s_b[b], in0=dist.rearrange("p (q s) -> p q s", q=2),
                                                scalar=-(2.0 ** (-8.0 * (h + 1) / AH)) * AHD ** 0.5,
                                                in1=st[:, b, :].rearrange("p (q s) -> p q s", q=2),
                                                op0=ALU.mult, op1=ALU.add))
                    link(v.tensor_reduce(stat[:, b, 0:2], s_b[b], AX, ALU.max))
                    v.tensor_scalar(stat[:, b, 2:4], stat[:, b, 0:2], -(AHD ** -0.5), None, ALU.mult)\
                        .then_inc(sem("smax"), 1)
                    eng.wait_ge(sem("pexp"), 2 * n + 2)
                    link(v.reciprocal(stat[:, b, 6:8], stat[:, b, 4:6]))
                    for q in range(2):
                        ins = v.tensor_scalar(p_b[b][:, q, :], p_b[b][:, q, :], stat[:, b, 6 + q:7 + q], None, ALU.mult)
                    ins.then_inc(sem("p"), 1)
                eng.wait_ge(sem("zc"), l + 1)
                for j in range(CONV2):
                    for t in range(4):
                        w = pc("conv_w2", (l * CONV2 + j) * 4 + t, 1)
                        if j == 0:
                            ins = v.tensor_scalar(yc[:, t, :], zc[:, t, 0:T], w, None, ALU.mult)
                        else:
                            ins = v.scalar_tensor_tensor(out=yc[:, t, :], in0=zc[:, t, j:j + T], scalar=w,
                                                         in1=yc[:, t, :], op0=ALU.mult, op1=ALU.add)
                    link(ins)
                v.tensor_tensor(yc, yc, bch[:, 0:4, :], ALU.mult).then_inc(sem("yc_full"), 1)
                for m in range(2):
                    eng.wait_ge(sem("y_hi"), 2 * l + m + 1)
                    v.tensor_tensor(h_lo[:, 2 * m:2 * m + 2, :], acc[:, 2 + m, :].rearrange("p (u t) -> p u t", u=2),
                                    h_hi[:, 2 * m:2 * m + 2, :], ALU.subtract)
                eng.wait_ge(sem("yc_hi"), l + 1)
                v.tensor_tensor(h_lo[:, 4:8, :], yc, h_hi[:, 4:8, :], ALU.subtract)
                stage(eng, ST[f"attn{l}"])
                steps(U + O_AP, 4)
                v.tensor_tensor(mrg2, acc_t, ga2, ALU.mult).then_inc(sem("acc_free"), 1)
                steps(U + O_CP, 4)
                v.tensor_tensor(gc2, acc_t, gc2, ALU.mult).then_inc(sem("acc_free"), 1)
                eng.wait_ge(sem("acc_free"), 2 * l + 2)
                for half in range(2):
                    t = slice(4 * half, 4 * half + 4)
                    v.tensor_tensor(mrg2[:, t, :], mrg2[:, t, :], gc2[:, t, :], ALU.add).then_inc(sem("mrg2_full"), 1)
                split("mrg2", 2 * l, mrg2, 8)
                steps(U + O_OUT, 8)
                add_to_x(mod2(l, 2))
                stage(eng, ST[f"out{l}"])

                norm(5 + 2 * l, nscale[:, 32 + 16 * l:40 + 16 * l], mod2(l, 3), nh, 4 + 2 * l)
                steps(U + O_WQ, 18)
                stage(eng, ST[f"wq{l}"])
                base = U + O_PEER

                paced = {"work": 0, "units": 0}

                def pace(n):
                    paced["work"] += n
                    while paced["units"] < HALF and paced["work"] >= PACE * (paced["units"] + 1):
                        step(base + paced["units"])
                        paced["units"] += 1

                def top16(src, vals, places, n, width):
                    for half in range(2):
                        at = slice(8 * half, 8 * half + 8)
                        for k in range(n):
                            ins = v.max(vals[:, k, at], src[:, k, :])
                            pace(width)
                        link(ins)
                        for k in range(n):
                            ins = v.max_index(places[:, k, at], vals[:, k, at], src[:, k, :])
                            pace(width)
                        link(ins)
                        if half == 0:
                            for k in range(n):
                                ins = v.match_replace(src[:, k, :], vals[:, k, at], src[:, k, :], -3.4028234e38)
                                pace(width)
                            link(ins)

                top16(scores, tv, ti, 32, NKEYS)
                link(v.tensor_copy(tif, ti))
                tv5 = tv.rearrange("p (g s) k -> p g s k", s=2)
                for t in range(TT):
                    g = slice(8 * t, 8 * t + 8)
                    ins = v.tensor_tensor(cand[:, g, :].rearrange("p g (a b) -> p g a b", b=TOPK),
                                          tv5[:, g, 0, :].unsqueeze(3).to_broadcast([P, 8, TOPK, TOPK]),
                                          tv5[:, g, 1, :].unsqueeze(2).to_broadcast([P, 8, TOPK, TOPK]), ALU.add)
                    pace(8 * TOPK * TOPK)
                link(ins)
                top16(cand, best, bpos, 16, TOPK * TOPK)
                v.tensor_tensor(ge_.rearrange("p (g k) -> p g k", k=TOPK), best,
                                best[:, :, 0:1].to_broadcast([P, 16, TOPK]), ALU.subtract).then_inc(sem("best_c"), 1)
                bp = bpos.rearrange("p a b -> p (a b)")
                v.tensor_single_scalar(pos_u[:, 0, :], bp, 4, ALU.logical_shift_right)
                link(v.tensor_single_scalar(pos_u[:, 1, :], bp, 15, ALU.bitwise_and))
                link(v.tensor_copy(pos_f, pos_u))
                tif5 = tif.rearrange("p (g s) k -> p g s k", s=2)
                iota16 = kc("iota16")

                def one_hot(r):
                    t, s = r // 2, r % 2
                    v.tensor_tensor(hot[:, s, :].rearrange("p (n a) -> p n a", a=TOPK),
                                    pos_f[:, s, 128 * t:128 * t + 128].unsqueeze(2).to_broadcast([P, PAIRS, TOPK]),
                                    iota16.unsqueeze(1).to_broadcast([P, PAIRS, TOPK]), ALU.is_equal)                        .then_inc(sem("place"), 1)
                    pace(PAIRS * TOPK)

                def key_number(r):
                    t, s = r // 2, r % 2
                    eng.wait_ge(sem("place_key"), 4 * l + r + 1)
                    link(v.tensor_reduce(sel3[:, s, 128 * t:128 * t + 128],
                                         hot[:, s, :].rearrange("p (n a) -> p n a", a=TOPK), AX, ALU.add))
                    pace(PAIRS * TOPK)

                one_hot(0)
                one_hot(1)
                for r in range(4):
                    key_number(r)
                    if r + 2 < 4:
                        one_hot(r + 2)
                while paced["units"] < HALF:
                    pace(PACE)
                eng.wait_ge(sem("gexp"), l + 1)
                ge3 = ge_.rearrange("p (g k) -> p g k", k=TOPK)
                link(v.tensor_reduce(gsum, ge3, AX, ALU.add))
                link(v.reciprocal(ginv, gsum))
                v.tensor_tensor(sel3[:, 2, :].rearrange("p (g k) -> p g k", k=TOPK), ge3,
                                ginv.unsqueeze(2).to_broadcast([P, 16, TOPK]), ALU.mult).then_inc(sem("sel3"), 1)
                stage(eng, ST[f"peer_a{l}"])

                def build(half, g, i=None):
                    n = 2 * TURNS * l + TURNS * half + g
                    if g > 0:
                        eng.wait_ge(sem("g_psum"), plus(i, 2, n))
                    at = slice(GROUP * g, GROUP * g + GROUP) if i is None else                         bass.ds(i * (2 * GROUP) + GROUP * g, GROUP)
                    for k, dst, numbers in ((1, hot_r, kc("iota")[:, HALF * half:HALF * half + HALF]),
                                            (0, hot_l, kc("iota"))):
                        width = NKEYS if k == 0 else HALF
                        v.tensor_tensor(dst, selt[:, k, at].unsqueeze(2).to_broadcast([P, GROUP, width]),
                                        numbers.unsqueeze(1).to_broadcast([P, GROUP, width]), ALU.is_equal)                            .then_inc(sem("hot_l" if k == 0 else "hot_eq"), 1)

                def multiply(half, g, i=None):
                    n = 2 * TURNS * l + TURNS * half + g
                    eng.wait_ge(sem("g_psum"), plus(i, 2, n + 1))
                    at = slice(GROUP * g, GROUP * g + GROUP) if i is None else                         bass.ds(i * (2 * GROUP) + GROUP * g, GROUP)
                    here = experts[:, HALF * half:HALF * half + HALF, at].rearrange("p n t -> p t n")
                    v.tensor_tensor(here, here, st[:, 2 + g % 2, :].rearrange("p (t n) -> p t n", t=GROUP),
                                    ALU.mult).then_inc(sem("g_mult"), 1)

                def lower(n, i=None):
                    eng.wait_ge(sem("gated_hi"), plus(i, 4, NKEYS * l + n + 1))
                    src = experts[:, n, :] if i is None else                         experts[:, bass.ds(i * 4 + n, 1), :].rearrange("p a t -> p (a t)")
                    v.tensor_tensor(act_lo[:, n % 2, :], src, act_hi[:, n % 2, :], ALU.subtract)                        .then_inc(sem("gated_lo"), 1)

                def turns(half, turn):
                    turn(half, 0)
                    with eng.Fori(0, TURNS // 2 - 1) as i:
                        for g in range(2):
                            turn(half, 1 + g, i)
                    turn(half, TURNS - 1)
                    multiply(half, TURNS - 1)

                def u_turn(half, g, i=None):
                    u = base + HALF + 2 * g
                    step(u, i, 4)
                    build(half, g, i)
                    step(u + 1, i, 4)
                    if g > 0:
                        multiply(half, g - 1, i)

                def v_turn(half, g, i=None):
                    u = base + NKEYS + 2 * g
                    if g < TURNS - 1:
                        lower(2 * g + 2, i)
                    step(u, i, 4)
                    build(half, g, i)
                    if g < TURNS - 1:
                        lower(2 * g + 3, i)
                    step(u + 1, i, 4)
                    if g > 0:
                        multiply(half, g - 1, i)

                eng.wait_ge(sem("selt"), l + 1)
                turns(0, u_turn)
                stage(eng, ST[f"peer_b{l}"])
                lower(0)
                lower(1)
                turns(1, v_turn)
                stage(eng, ST[f"peer_c{l}"])
                v_base = base + NKEYS
                lower(HALF)
                lower(HALF + 1)
                with eng.Fori(0, HALF // 4 - 1) as i:
                    for k in range(4):
                        lower(HALF + k + 2, i)
                        step(v_base + HALF + k, i, 4)
                for n in range(NKEYS - 4, NKEYS):
                    if n + 2 < NKEYS:
                        lower(n + 2)
                    step(v_base + n)
                add_to_x(mod2(l, 5))
                stage(eng, ST[f"peer_d{l}"])
            norm(8, pc("final_g2"), None, nh)

        @block.gpsimd
        def _(eng):
            link = linker(eng, "pool_chain")
            g = nc.gpsimd
            eng.dma_start(par[:, :], params[:, 0:N_PAR]).then_inc(sem("par_in"), 16)
            eng.dma_start(x_t[:, :, :].rearrange("p a t -> p (a t)"), params[:, N_PAR:N_PAR + DT * T])\
               .then_inc(sem("x_in"), 16)
            stage(eng, ST["ada"])
            stage(eng, ST["ffn0"])
            for buf in (xp, pool_a, pool_b):
                ins = g.memset(buf[:, :, 0:PADP], 0.0)
            link(ins)
            eng.wait_ge(sem("proj_out"), 2)
            src = xp
            for k in range(NPOOL):
                dst = (pool_a, pool_b)[k % 2]
                w = 1 << k
                link(g.tensor_tensor(dst[:, k:NPOOL, PADP:PADP + T], src[:, k:NPOOL, PADP:PADP + T],
                                     src[:, k:NPOOL, PADP - w:PADP + T - w], ALU.add))
                src = dst
            eng.wait_ge(sem("k2_in"), 16)
            for k in range(NPOOL):
                ins = g.tensor_tensor(pooled[:, k, :], (pool_a, pool_b)[k % 2][:, k, PADP:PADP + T],
                                      inv_count[:, k, :], ALU.mult)
            link(ins)
            g.tensor_tensor(pooled, pooled, xp[:, :, PADP:PADP + T], ALU.subtract).then_inc(sem("pooled"), 1)
            stage(eng, ST["mix_proj"])
            stage(eng, ST["mix_pool"])
            stage(eng, ST["mix_norm"])
            stage(eng, ST["mix_heads"])
            for lv in range(LEVELS):
                if lv >= 2:
                    eng.wait_ge(sem("lv_x"), 4 * (lv - 1))
                g.tensor_tensor(off_t[lv % 2], a_t, level_mask[:, lv, :].unsqueeze(1).to_broadcast([P, 16, P]),
                                ALU.mult).then_inc(sem("lv_off"), 1)
            for name in ("mix_solve", "mix_state", "mix_o", "mix_out", "ffn1", "final1"):
                stage(eng, ST[name])
            for l in range(LAYERS):
                stage(eng, ST[f"proj{l}"])
                link(g.memset(zc[:, :, 0:2], 0.0))
                g.tensor_tensor(zc[:, :, 2:2 + T], bch[:, 4:8, :], bch[:, 8:12, :], ALU.mult).then_inc(sem("zc"), 1)
                for name in ("attn", "out", "wq"):
                    stage(eng, ST[f"{name}{l}"])
                tif5 = tif.rearrange("p (g s) k -> p g s k", s=2)
                for r in range(4):
                    t, s = r // 2, r % 2
                    eng.wait_ge(sem("place"), 4 * l + r + 1)
                    hv = hot[:, s, :].rearrange("p (g k a) -> p g k a", k=TOPK, a=TOPK)
                    g.tensor_tensor(hv, hv, tif5[:, 8 * t:8 * t + 8, s, :].unsqueeze(2)
                                    .to_broadcast([P, 8, TOPK, TOPK]), ALU.mult).then_inc(sem("place_key"), 1)
                stage(eng, ST[f"peer_a{l}"])

                def weigh(half, n, i=None):
                    eng.wait_ge(sem("hot_eq"), plus(i, 1, 2 * TURNS * l + TURNS * half + n + 1))
                    at = slice(GROUP * n, GROUP * n + GROUP) if i is None else bass.ds(i * GROUP + GROUP * n, GROUP)
                    g.tensor_tensor(hot_r, hot_r, selt[:, 2, at].unsqueeze(2).to_broadcast([P, GROUP, HALF]),
                                    ALU.mult).then_inc(sem("hot_r"), 1)

                for half in range(2):
                    with eng.Fori(0, TURNS) as i:
                        weigh(half, 0, i)
                    stage(eng, ST[("peer_b", "peer_c")[half] + str(l)])
                stage(eng, ST[f"peer_d{l}"])
            eng.wait_ge(sem("normed"), 2)
            eng.dma_start(out, nh.rearrange("p a t -> p (a t)")).then_inc(sem("out"), 16)
            eng.wait_ge(sem("out"), 16)

        @block.tensor
        def _(eng):
            mm = nc.tensor.matmul

            def product(u, dst, hi_t, lo_t, i=None, per=0, first=False, last=False, shared=False):
                eng.wait_ge(hi_ready, plus(i, per, nth(u)))
                for t in range(DT):
                    w = w_hi[:, u % 2, t * P:(t + 1) * P]
                    start = first and (t == 0 if shared else t % 2 == 0)
                    mm(dst(t), w, hi_t(t), start=start, stop=False, skip_group_check=True)
                    mm(dst(t), w, lo_t(t), start=False, stop=False, skip_group_check=True)
                eng.wait_ge(taken, plus(i, per, u + 1))
                for t in range(DT):
                    ins = mm(dst(t), w_lo[:, u % 2, t * P:(t + 1) * P], hi_t(t), start=False,
                             stop=last and (t == DT - 1 or not shared), skip_group_check=True)
                ins.then_inc(used, 1)

            def norm(m=None):
                n = norm_count[0]
                norm_count[0] += 1
                eng.wait_ge(sem("sq"), n + 1)
                for t in range(DT):
                    ins = mm(st[:, 3, 0:T], ones, nh[:, t, :], start=t == 0, stop=t == DT - 1)
                ins.then_inc(sem("sumsq"), 1)
                if m is not None:
                    eng.wait_ge(sem("norm_lo"), 2 * m + 2)

            norm_count = [0]

            def ada_total(q, i=None):
                b = q % 2
                eng.wait_ge(taken, plus(i, 16, 8 * q + 8))
                if q >= 2:
                    eng.wait_ge(sem("ada_diag"), plus(i, 2, q - 1))
                for half in range(2):
                    for k in range(2):
                        ins = mm(st[:, 2 * b + half, :], ones, part[:, 2 * b + k, half * 512:half * 512 + 512],
                                 start=k == 0, stop=k == 1)
                ins.then_inc(sem("ada_psum"), 1)

            eng.wait_ge(sem("k1_in"), 16)
            ada_total(0)
            ada_total(1)
            ada_total(2)
            with eng.Fori(0, (N_BLOCKS - 3) // 2) as i:
                for b in range(2):
                    ada_total(3 + b, i)
            eng.wait_ge(sem("zrow"), 1)
            stage(eng, ST["ada"])

            def clear_acc():
                for b in range(4):
                    mm(acc[:, b, :], zrow[0:1, :], zrow[0:1, :].unsqueeze(1).to_broadcast([1, 4, P]), start=True, stop=False,
                       skip_group_check=True)

            def accumulate(u, b, i=None, per=0, last=False):
                product(u, lambda t: acc_t[:, t, :], lambda t: act_hi[:, b, :], lambda t: act_lo[:, b, :],
                        i, per, last=last)

            def tile(dst, u, i=None, per=0):
                product(u, lambda t: dst, lambda t: h_hi[:, t, :], lambda t: h_lo[:, t, :], i, per,
                        first=True, last=True, shared=True)

            def ffn(f):
                norm((0, 2)[f])
                clear_acc()
                base = (U_FFN1, U_FFN2)[f]

                def up(u, j, i=None, per=0):
                    tile(st[:, j, 0:T], u, i, per)
                    tile(st[:, 2 + j, 0:T], u + 1, i, per)

                def body(j, i=None, per=0):
                    up(base + 2 + 3 * j, (j + 1) % 2, i, per)
                    eng.wait_ge(sem("act_lo"), plus(i, 4, FT * f + j + 1))
                    accumulate(base + 4 + 3 * j, j % 2, i, per)

                up(base, 0)
                body(0)
                with eng.Fori(0, (FT - 2) // 4) as i:
                    for j in range(4):
                        body(1 + j, i, 12)
                eng.wait_ge(sem("act_lo"), FT * f + FT)
                accumulate(base + N_FFN - 1, (FT - 1) % 2, last=True)

            ffn(0)
            stage(eng, ST["ffn0"])

            def pairs(base, n, sem_name, before):
                for p in range(n):
                    if p >= 4:
                        eng.wait_ge(sem(sem_name), before + p - 3)
                    for k in range(2):
                        tile(st[:, p % 4, k * T:(k + 1) * T], base + 2 * p + k)

            norm(1)
            pairs(U_MIX, 26, "proj_out", 0)
            eng.wait_ge(sem("sw_in"), 16)
            for t in range(TT):
                for k in range(DT):
                    ins = mm(acc[:, 0, 16 * t:16 * t + 16], nh[:, k, t * P:(t + 1) * P], w_ba[:, k, :],
                             start=k == 0, stop=k == DT - 1)
            ins.then_inc(sem("ba_psum"), 1)
            stage(eng, ST["mix_proj"])

            def kmajor(base, n, at=0, waits=None):
                for k in range(n):
                    if waits is not None:
                        eng.wait_ge(*waits(k))
                    product(base + k, lambda t: acc_t[:, t, :], lambda t: h_hi[:, at + k, :],
                            lambda t: h_lo[:, at + k, :], first=k == 0, last=k == n - 1)

            eng.wait_ge(sem("pooled"), 1)
            for k in range(NPOOL):
                ins = mm(st[:, k // 2, (k % 2) * T:(k % 2) * T + T], w_pool[:, k, :], pooled[:, k, :],
                         start=True, stop=True)
            ins.then_inc(sem("pool_mm"), 1)
            kmajor(U_POOLP, 4, waits=lambda k: (sem("ya0_lo"), k + 1))
            stage(eng, ST["mix_pool"])

            eng.wait_ge(sem("sq_qk"), 1)
            eng.wait_ge(sem("k2_in"), 16)
            onecol = kc("onecol")
            for h in range(16):
                ins = mm(st[0:16, 0, 0:T], onecol[:, 15 - h:31 - h], sq_qk[:, h, :], start=h == 0, stop=h == 15)
            ins.then_inc(sem("sum_qk"), 1)
            for c in range(2):
                mm(st[0:8, 1, c * P:(c + 1) * P], ba_g[:, c, :], upto, start=True, stop=True)
                mm(st[0:8, 1, T + c * P:T + (c + 1) * P], ba_b[:, c, :], ident, start=True, stop=True)
            for c in range(2):
                ins = mm(st[:, 2, 8 * c:8 * c + 8], upto, ba_g[:, c, :], start=True, stop=True)
            ins.then_inc(sem("g_rows"), 1)
            eng.wait_ge(sem("rn"), 1)
            for m in range(8):
                if m >= 4:
                    eng.wait_ge(sem("qk_n"), m - 3)
                for k in range(2):
                    ins = mm(acc[:, m % 4, k * T:(k + 1) * T], select[0:16, 2 * m + k, :], rn[0:16, :],
                             start=True, stop=True)
                ins.then_inc(sem("rn_b"), 1)
            stage(eng, ST["mix_norm"])

            for h in range(HEADS):
                b = h % 2
                if h >= 2:
                    eng.wait_ge(sem("head"), h - 1)
                mm(st[:, b, :], select[0:8, h, :], rows[0:8, :], start=True, stop=True).then_inc(sem("bc"), 1)
                for c in range(2):
                    ck = slice(c * P, (c + 1) * P)
                    mm(st[:, 2 + b, c * P:(c + 1) * P], qkv[:, 8 + h, ck], qkv[:, 8 + h, ck], start=True, stop=True)
                    ins = mm(st[:, 2 + b, T + c * P:T + (c + 1) * P], qkv[:, 8 + h, ck], qkv[:, h, ck],
                             start=True, stop=True)
                ins.then_inc(sem("kkqk"), 1)
            for q in range(6):
                if q >= 4:
                    eng.wait_ge(sem("tok_out"), q - 3)
                for j in range(4):
                    n = 4 * q + j
                    src = qkv[:, 16 + n % 8, (n // 8) * P:(n // 8 + 1) * P] if n < 16 else qkv[:, 8 + n - 16, 0:P]
                    ins = nc.tensor.transpose(acc[:, q % 4, j * P:(j + 1) * P], src, ident)
                ins.then_inc(sem("tok_t"), 1)
            stage(eng, ST["mix_heads"])

            for lv in range(LEVELS):
                eng.wait_ge(sem("lv_off"), lv + 1)
                for g in range(4):
                    if lv >= 1:
                        eng.wait_ge(sem("lv_d"), 4 * (lv - 1) + g + 1)
                    for k in range(4):
                        ins = mm(st[:, g, k * P:(k + 1) * P], off_t[lv % 2][:, 4 * g + k, :], d_m[:, 4 * g + k, :],
                                 start=True, stop=True)
                    ins.then_inc(sem("lv_x"), 1)
                for g in range(4):
                    b = 2 * (g % 2)
                    if 4 * lv + g >= 2:
                        eng.wait_ge(sem("lv_d"), 4 * lv + g - 1)
                    eng.wait_ge(sem("lv_xs"), 4 * lv + g + 1)
                    for k in range(4):
                        n = 4 * g + k
                        mm(acc[:, b, k * P:(k + 1) * P], d_t[:, n, :], x_s[:, n, :], start=True, stop=True)
                        ins = mm(acc[:, b + 1, k * P:(k + 1) * P], x_s[:, n, :], d_t[:, n, :], start=True, stop=True)
                    ins.then_inc(sem("lv_dx"), 1)
            stage(eng, ST["mix_solve"])

            def four(bank, g, name, lhs, rhs):
                for k in range(4):
                    h = 4 * g + k
                    ins = mm(bank[:, k * P:(k + 1) * P], lhs(h), rhs(h), start=True, stop=True)
                ins.then_inc(sem(name), 1)

            for g in range(2):
                four(acc[:, g, :], g, "vn0_psum", lambda h: d_t[:, h, :], lambda h: bv[:, h, :])
            for g in range(2):
                eng.wait_ge(sem("vn0"), g + 1)
                four(acc[:, 2 + g, :], g, "s1_psum", lambda h: k_dec[:, h, :], lambda h: v_new[:, h, :])
            for g in range(2):
                eng.wait_ge(sem("s1"), g + 1)
                four(st[:, g, :], g, "ks1_psum", lambda h: qkv[:, 8 + h, 128:256], lambda h: s1[:, h, :])
            for g in range(2):
                eng.wait_ge(sem("resid"), g + 1)
                four(acc[:, g, :], g, "vn1_psum", lambda h: d_t[:, 8 + h, :], lambda h: resid[:, h, :])
            for m in range(4):
                eng.wait_ge(sem("vn1"), m // 2 + 1)
                if m == 0:
                    eng.wait_ge(sem("resid"), 2)
                for k in range(2):
                    h = 2 * m + k
                    o = st[:, m, k * T:(k + 1) * T]
                    mm(o[:, 0:128], v_new[:, h, :], qk_m[:, h, :], start=True, stop=True)
                    mm(o[:, 128:256], v_new[:, 8 + h, :], qk_m[:, 8 + h, :], start=True, stop=False)
                    ins = mm(o[:, 128:256], s1[:, h, :], q_dec[:, h, :], start=False, stop=True)
                ins.then_inc(sem("o_psum"), 1)
            stage(eng, ST["mix_state"])
            eng.wait_ge(sem("sq_o"), 1)
            for h in range(8):
                ins = mm(st[0:8, 0, 0:T], onecol[:, 15 - h:23 - h], sq_o[:, h, :], start=h == 0, stop=h == 7)
            ins.then_inc(sem("sum_o"), 1)
            eng.wait_ge(sem("rn_o"), 1)
            for m in range(4):
                for k in range(2):
                    ins = mm(acc[:, m, k * T:(k + 1) * T], select[0:8, 2 * m + k, :], rn[0:8, :],
                             start=True, stop=True)
                ins.then_inc(sem("rno_b"), 1)
            stage(eng, ST["mix_o"])
            kmajor(U_DNP, 8, waits=lambda k: (sem("o_lo"), k // 4 + 1))
            kmajor(U_MIXO, 8, waits=lambda k: (sem("merged_lo"), k // 4 + 1))
            stage(eng, ST["mix_out"])

            ffn(1)
            stage(eng, ST["ffn1"])
            norm()
            stage(eng, ST["final1"])

            for l in range(LAYERS):
                U = U_L2 + N_L2 * l
                norm(3 + 2 * l)
                pairs(U + O_QK, 20, "proj2", 20 * l)
                stage(eng, ST[f"proj{l}"])

                def scores_of(h):
                    b, r = h % 2, slice(64 * (h % 2), 64 * (h % 2) + 64)
                    if h >= 2:
                        eng.wait_ge(sem("smax"), AH * l + h - 1)
                    for q in range(2):
                        ins = mm(st[:, b, q * T:(q + 1) * T], qk2[r, h // 2, q * P:(q + 1) * P],
                                 qk2[r, 4 + h // 2, :], start=True, stop=True)
                    ins.then_inc(sem("s_psum"), 1)

                def values_of(h):
                    b = h % 2
                    eng.wait_ge(sem("p"), AH * l + h + 1)
                    if h >= 2:
                        eng.wait_ge(sem("pt"), AH * l + h - 1)
                    nc.tensor.transpose(acc[:, b, 0:128], p_b[b][:, 0, 0:128], ident)
                    nc.tensor.transpose(acc[:, b, 128:256], p_b[b][:, 1, 0:128], ident)
                    nc.tensor.transpose(acc[:, b, 256:384], p_b[b][:, 1, 128:256], ident)\
                        .then_inc(sem("pt_psum"), 1)
                    eng.wait_ge(sem("pt"), AH * l + h + 1)
                    m = h // 2
                    o = acc[64 * b:64 * b + 64, 2 + m // 2, (m % 2) * T:(m % 2) * T + T]
                    mm(o[:, 0:128], v2[:, 0, 64 * h:64 * h + 64], pt_b[b][:, 0:128], start=True, stop=True)
                    mm(o[:, 128:256], v2[:, 0, 64 * h:64 * h + 64], pt_b[b][:, 128:256], start=True, stop=False)
                    mm(o[:, 128:256], v2[:, 1, 64 * h:64 * h + 64], pt_b[b][:, 256:384], start=False, stop=True)\
                        .then_inc(sem("pv"), 1)

                for t in range(TT):
                    for n in range(4):
                        ins = nc.tensor.transpose(acc[:, t, n * P:(n + 1) * P], vt[:, n, t * P:(t + 1) * P], ident)
                ins.then_inc(sem("v_tok"), 1)
                scores_of(0)
                eng.wait_ge(sem("v2"), l + 1)
                for h in range(AH):
                    if h + 1 < AH:
                        scores_of(h + 1)
                    values_of(h)
                stage(eng, ST[f"attn{l}"])
                kmajor(U + O_AP, 4)
                eng.wait_ge(sem("acc_free"), 2 * l + 1)
                kmajor(U + O_CP, 4, at=4)
                kmajor(U + O_OUT, 8, waits=lambda k: (sem("mrg2_lo"), 2 * l + k // 4 + 1))
                stage(eng, ST[f"out{l}"])

                norm(4 + 2 * l)
                pairs(U + O_WQ, 8, "qq", 8 * l)
                eng.wait_ge(sem("qq"), 8 * l + 8)
                for u in range(2):
                    n_u = U + O_SK + u
                    eng.wait_ge(taken, n_u + 1)
                    for t in range(TT):
                        for half in range(2):
                            if u == 1:
                                eng.wait_ge(sem("scores"), 8 * l + 2 * t + half + 1)
                            for k in range(4):
                                n = 4 * half + k
                                for part_ in (w_hi, w_lo):
                                    w = part_[:, n_u % 2, n * P:(n + 1) * P].bitcast(F32)
                                    ins = mm(acc[:, 2 * t + half, k * P:(k + 1) * P],
                                             qq[:, 8 * u + n, t * P:(t + 1) * P], w,
                                             start=part_ is w_hi, stop=part_ is w_lo)
                            ins.then_inc(used if (t, half) == (1, 1) else sem("sk"), 1)
                stage(eng, ST[f"wq{l}"])
                base = U + O_PEER
                n_key = NKEYS * l

                def u_tile(n, i=None):
                    if n_key + n >= 2:
                        eng.wait_ge(sem("gelu"), plus(i, 4, n_key + n - 1))
                    tile(st[:, n % 2, 0:T], base + n, i, 4)

                for n in range(4):
                    u_tile(n)
                with eng.Fori(0, HALF // 4 - 1) as i:
                    for k in range(4):
                        u_tile(4 + k, i)
                eng.wait_ge(sem("sel3"), l + 1)
                for k in range(3):
                    for t in range(TT):
                        at = k * T + t * P
                        ins = nc.tensor.transpose(st[:, 2 + at // 512, at % 512:at % 512 + P],
                                                  sel3[:, k, t * P:(t + 1) * P], ident)
                ins.then_inc(sem("sel_psum"), 1)
                stage(eng, ST[f"peer_a{l}"])

                def token_gates(half, g, i=None):
                    n = 2 * TURNS * l + TURNS * half + g
                    eng.wait_ge(sem("hot_l"), plus(i, 2, n + 1))
                    eng.wait_ge(sem("hot_r"), plus(i, 2, n + 1))
                    if n >= 2:
                        eng.wait_ge(sem("g_mult"), plus(i, 2, n - 1))
                    for k in range(GROUP):
                        ins = mm(st[:, 2 + g % 2, k * HALF:(k + 1) * HALF], hot_l[:, k, :], hot_r[:, k, :],
                                 start=True, stop=True)
                    ins.then_inc(sem("g_psum"), 1)

                def turns(half, unit):
                    unit(0)
                    unit(1)
                    with eng.Fori(0, TURNS // 2 - 1) as i:
                        for g in range(2):
                            unit(2 + 2 * g, i)
                            token_gates(half, g, i)
                            unit(3 + 2 * g, i)
                    unit(HALF - 2)
                    token_gates(half, TURNS - 2)
                    unit(HALF - 1)
                    token_gates(half, TURNS - 1)

                def v_unit(n, i=None):
                    eng.wait_ge(sem("gated_lo"), plus(i, 4, n_key + n + 1))
                    accumulate(base + NKEYS + n, n % 2, i, 4, last=n == NKEYS - 1)

                turns(0, lambda n, i=None: u_tile(HALF + n, i))
                stage(eng, ST[f"peer_b{l}"])
                clear_acc()
                turns(1, v_unit)
                stage(eng, ST[f"peer_c{l}"])
                with eng.Fori(0, HALF // 4 - 1) as i:
                    for k in range(4):
                        v_unit(HALF + k, i)
                for n in range(NKEYS - 4, NKEYS):
                    v_unit(n)
                stage(eng, ST[f"peer_d{l}"])
            norm()


def _columns(a):
    return np.asarray(a).reshape(-1, P).T


def _out_tiles(w):
    return w.reshape(8, P, -1, P).transpose(2, 1, 0, 3).reshape(-1, P, UNIT)


def _row_tiles(w):
    return w.reshape(-1, P, UNIT)


def _constants():
    f = np.arange(P)
    tok = np.arange(T)
    dist = tok[:, None] - tok[None, :]
    dist = np.where(dist >= 0, dist, -NEG).astype(np.float32).reshape(TT, P, T).transpose(1, 0, 2).reshape(P, -1)
    onecol = np.zeros((P, 31), np.float32)
    onecol[:, 15] = 1
    is_q = (f < HEADS)[:, None]
    one = np.ones((P, 1), np.float32)
    parts = dict(ident=np.eye(P), ones=np.ones((P, P)), iota=np.tile(f, (P, 1)), dist=dist, onecol=onecol,
                 iota16=np.tile(np.arange(16), (P, 1)), eps=one * 1e-6, qk_scale=np.where(is_q, 128.0, 1.0),
                 qk_eps=np.where(is_q, 128e-6, 1e-6))
    k1 = np.concatenate([parts[n] for n in _K1], 1).astype(np.float32)
    j, i = f[:, None], f[None, :]
    levels = [((j // (2 * b) == i // (2 * b)) & (j % (2 * b) < b) & (i % (2 * b) >= b)) for b in
              (1 << lv for lv in range(LEVELS))]
    inv = np.concatenate([1.0 / np.minimum(tok + 1, w) for w in POOL_WINDOWS])
    select = np.zeros((P, 16, P))
    for h in range(16):
        select[h, h] = 1
    parts = dict(upto=j <= i, future=np.where(j <= i, 0, NEG), levels=np.concatenate(levels, 1),
                 inv_count=np.tile(inv, (P, 1)), select=select.reshape(P, -1))
    k2 = np.concatenate([parts[n] for n in _K2], 1).astype(np.float32)
    return k1, k2


def _weights(a):
    w = np.empty((N_UNITS, P, UNIT), np.float32)

    def put(at, units):
        w[at:at + len(units)] = units

    put(U_ADA, a["ada_w"][0].reshape(8, P, -1, UNIT).transpose(2, 0, 1, 3).reshape(-1, P, UNIT))
    for l in range(LAYERS):
        put(U_ADA + N_ADA1 + l * N_ADA2,
            a["w_ada_2"][l].reshape(8, P, -1, UNIT).transpose(2, 0, 1, 3).reshape(-1, P, UNIT))
    for base, w_in, w_out in ((U_FFN1, "ffn1_w_in", "ffn1_w_out"), (U_FFN2, "ffn2_w_in", "ffn2_w_out")):
        up = _out_tiles(a[w_in][0])
        down = _row_tiles(a[w_out][0])
        w[base] = up[0]
        w[base + 1] = up[FT]
        w[base + 2:base + N_FFN - 1:3] = up[1:FT]
        w[base + 3:base + N_FFN - 1:3] = up[FT + 1:]
        w[base + 4:base + N_FFN - 1:3] = down[:FT - 1]
        w[base + N_FFN - 1] = down[FT - 1]
    m = a["mix_w_in"][0]
    ba = 512 + 4 * D
    put(U_MIX, _out_tiles(m[:, :ba]))
    put(U_MIX + 36, _out_tiles(m[:, ba + 16:]))
    small_ba = m[:, ba:ba + 16].reshape(8, P, 16).transpose(1, 0, 2).reshape(P, -1)
    pool_w = a["pool_w"][0].transpose(1, 0, 2).reshape(P, -1)
    put(U_POOLP, _row_tiles(a["pool_proj"][0]))
    put(U_DNP, _row_tiles(a["dn_proj"][0]))
    put(U_MIXO, _row_tiles(a["mix_w_out"][0]))
    for l in range(LAYERS):
        U = U_L2 + l * N_L2
        tiles = _out_tiles(a["w_in_2"][l])
        put(U + O_QK, tiles[0:8])
        put(U + O_V, tiles[8:12])
        put(U + O_REST, tiles[12:])
        put(U + O_AP, _row_tiles(a["w_attn_proj_2"][l]))
        put(U + O_CP, _row_tiles(a["w_conv_proj_2"][l]))
        put(U + O_OUT, _row_tiles(a["w_out_2"][l]))
        put(U + O_WQ, _out_tiles(a["w_query_2"][l]))
        keys = a["sub_keys_2"][l].reshape(16, NKEYS, P).transpose(2, 0, 1).reshape(P, 2, UNIT)
        put(U + O_SK, keys.transpose(1, 0, 2))
        u = a["expert_u_2"][l].reshape(NKEYS, NKEYS, 8, P).transpose(1, 3, 2, 0)
        v = a["expert_v_2"][l].reshape(NKEYS, NKEYS, D).transpose(1, 0, 2)
        base = U + O_PEER
        put(base, u.reshape(NKEYS, P, UNIT))
        put(base + NKEYS, v)
    return w, np.concatenate([small_ba, pool_w], 1)


def kernel(**inputs):
    import concourse.bacc as bacc
    from concourse.bass_utils import run_bass_kernel_spmd

    a = {n: np.asarray(x) for n, x in inputs.items()}
    weights, smallw = _weights(a)

    def row(name):
        return np.broadcast_to(a[name].reshape(1, -1), (P, a[name].size))

    cols = dict(c=_columns(a["c"]), c2=_columns(a["c_2"]), ada_b=_columns(a["ada_b"]), b_ada2=_columns(a["b_ada_2"]),
                norm_g=_columns(a["norm_g"]), final_g=_columns(a["final_g"]), conv_w=_columns(a["conv_w"]),
                pool_scale=_columns(a["pool_scale"]), dn_g=_columns(a["dn_norm_g"]), a_log=row("a_log"),
                dt_bias=row("dt_bias"), n1g2=_columns(a["norm1_g_2"]), n2g2=_columns(a["norm2_g_2"]),
                conv_w2=_columns(a["conv_w_2"]), final_g2=_columns(a["final_g_2"]))
    x = a["x"][0].reshape(T, DT, P).transpose(2, 1, 0).reshape(P, -1)
    params = np.concatenate([cols[n] for n in _COLS] + [x], 1)
    k1, k2 = _constants()
    arrays = {"weights": weights, "params": params, "const1": k1, "const2": k2, "smallw": smallw}
    arrays = {n: np.ascontiguousarray(v, dtype=np.float32) for n, v in arrays.items()}

    nc = bacc.Bacc("TRN2", target_bir_lowering=False, num_devices=1)
    args = [nc.dram_tensor(n, v.shape, F32, kind="ExternalInput").ap() for n, v in arrays.items()]
    out = nc.dram_tensor("out", (P, DT * T), F32, kind="ExternalOutput").ap()
    build(nc, *args, out)
    r = run_bass_kernel_spmd(nc, [arrays], core_ids=[0])
    y = np.asarray(r.results[0]["out"])
    return y.reshape(P, DT, T).transpose(2, 1, 0).reshape(1, T, D)
```

```python
from contextlib import ExitStack

import numpy as np

import concourse.bass as bass
from concourse import mybir

ALU = mybir.AluOpType
ACT = mybir.ActivationFunctionType
F32 = mybir.dt.float32
F32R = mybir.dt.float32r
BF16 = mybir.dt.bfloat16
U32 = mybir.dt.uint32
AX = mybir.AxisListType.X

P = 128
T = 256
TT = T // P
D = 1024
DT = D // P
FFN = 2816
FT = FFN // P
POOL_WINDOWS = (2, 4, 8, 16)
NPOOL = len(POOL_WINDOWS)
PADP = 16
HEADS = 8
CONV = 4
CONV2 = 3
LEVELS = 7
AH, AHD = 8, 64
LAYERS = 2
NKEYS = 128
TOPK = 16
PAIRS = HEADS * TOPK
HALF = NKEYS // 2
GROUP = 8
TURNS = T // GROUP
assert 2 * TURNS == HALF and TURNS % 2 == 0
NEG = -1e30

UNIT = 1024
RING = 4
EXP_BEFORE = 4
PACE = 1060
N_ADA1, N_ADA2 = 72, 48
U_FFN1 = 0
N_FFN = 3 * FT
U_MIX = U_FFN1 + N_FFN
N_MIX = 52
U_POOLP = U_MIX + N_MIX
U_DNP = U_POOLP + 4
U_MIXO = U_DNP + 8
U_FFN2 = U_MIXO + 8
U_L2 = U_FFN2 + N_FFN
O_QK, O_V, O_REST, O_AP, O_CP, O_OUT, O_WQ, O_SK, O_PEER = 0, 8, 12, 40, 44, 48, 56, 72, 74
N_L2 = O_PEER + 2 * NKEYS
N_UNITS = U_L2 + LAYERS * N_L2

ADA_RING = 4
N_BLOCKS = (N_ADA1 + LAYERS * N_ADA2) // 8
Q_FFN = (3, 8)
Q_PROJ, Q_OUT = 13, 18
OUT_TAKES = {1: Q_OUT - 1, 12: Q_OUT, 23: Q_OUT + 1}
assert N_UNITS % RING == 0

_COLS = {}


def _layout():
    at = 0
    for name, n in (("c", 8), ("c2", 8), ("ada_b", N_ADA1), ("b_ada2", LAYERS * N_ADA2), ("norm_g", 24),
                    ("final_g", 8), ("conv_w", CONV * 24), ("pool_scale", 4), ("dn_g", 1), ("a_log", 8),
                    ("dt_bias", 8), ("n1g2", 16), ("n2g2", 16), ("conv_w2", LAYERS * CONV2 * 4), ("final_g2", 8)):
        _COLS[name] = (at, n)
        at += n
    return at


N_PAR = _layout()

_K1 = {}


def _layout1():
    at = 0
    for name, n in (("ident", 128), ("ones", 128), ("iota", 128), ("dist", TT * T), ("onecol", 31),
                    ("iota16", 16), ("eps", 1), ("qk_scale", 1), ("qk_eps", 1)):
        _K1[name] = (at, n)
        at += n
    return at


N_K1 = _layout1()
_K2 = {}


def _layout2():
    at = 0
    for name, n in (("upto", 128), ("future", 128), ("levels", LEVELS * 128), ("inv_count", NPOOL * T),
                    ("select", 16 * 128)):
        _K2[name] = (at, n)
        at += n
    return at


N_K2 = _layout2()
N_SMALLW = 8 * 16 + NPOOL * 128
ARENA = T * NKEYS
K2_AT = ARENA - N_K2 - N_SMALLW
EXTRA = 3328


def build(nc, weights, ada_weights, params, const1, const2, smallw, out):
    with ExitStack() as ctx:
        def sb(name, shape, dt=F32):
            return ctx.enter_context(nc.sbuf_tensor(name, shape, dt))

        sems = {}

        def sem(name):
            if name not in sems:
                sems[name] = ctx.enter_context(nc.semaphore(name))
            return sems[name]

        ring = sb("ring", [P, RING, UNIT])
        x_t = sb("x_t", [P, DT, T])
        w_hi = sb("w_hi", [P, 2, UNIT], F32R)
        w_lo = sb("w_lo", [P, 2, UNIT], F32R)
        h_hi = sb("h_hi", [P, DT, T], F32R)
        h_lo = sb("h_lo", [P, DT, T], F32R)
        act_hi = sb("act_hi", [P, 2, T], F32R)
        act_lo = sb("act_lo", [P, 2, T], F32R)
        arena = sb("arena", [P, ARENA])
        extra = sb("extra", [P, EXTRA])
        par = sb("par", [P, N_PAR])
        k1 = sb("k1", [P, N_K1])
        mod = sb("mod", [P, N_ADA1 + LAYERS * N_ADA2])
        nscale = sb("nscale", [P, 7 * 8])
        half_gate = sb("half_gate", [P, 16])
        sc = sb("sc", [P, 8])
        zrow = sb("zrow", [1, P], BF16)
        acc = ctx.enter_context(nc.psum_tensor("acc", [P, 4, 512], F32))
        st = ctx.enter_context(nc.psum_tensor("st", [P, 4, 512], F32))
        acc_t = acc[:, :, :].rearrange("p b (u t) -> p (b u) t", u=2)

        def pc(name, i=0, n=None):
            at, size = _COLS[name]
            return par[:, at + i:at + i + (size - i if n is None else n)]

        def kc(name):
            at, n = _K1[name]
            return k1[:, at:at + n]

        def k2c(name):
            at, n = _K2[name]
            return arena[:, K2_AT + at:K2_AT + at + n]

        def ar(at, *shape, base=None):
            n = int(np.prod(shape))
            v = (arena if base is None else base)[:, at:at + n]
            if len(shape) == 2:
                v = v.rearrange("p (a b) -> p a b", b=shape[1])
            elif len(shape) == 3:
                v = v.rearrange("p (a b c) -> p a b c", b=shape[1], c=shape[2])
            return v

        ident, ones = kc("ident"), kc("ones")
        upto, future = k2c("upto"), k2c("future")
        level_mask = k2c("levels").rearrange("p (l i) -> p l i", l=LEVELS)
        inv_count = k2c("inv_count").rearrange("p (g t) -> p g t", g=NPOOL)
        select = k2c("select").rearrange("p (h i) -> p h i", h=16)
        sw_at = K2_AT + N_K2
        w_ba = arena[:, sw_at:sw_at + 128].rearrange("p (k n) -> p k n", n=16)
        w_pool = arena[:, sw_at + 128:sw_at + N_SMALLW].rearrange("p (g n) -> p g n", g=NPOOL)
        dist = kc("dist")

        gate_s = ar(0, 2, T)
        act = ar(2 * T, 2, T)
        ada_ring = ar(ARENA // 2, ADA_RING, UNIT)
        part = ar(ARENA // 2 + ADA_RING * UNIT, 2, UNIT)
        diag = ar(ARENA // 2 + (ADA_RING + 2) * UNIT, 2, P)
        part_ffn = ar(4 * T, 5, UNIT)
        nh = ar(23816, DT, T)
        std = ar(0, T, base=extra)
        rstd = ar(T, T, base=extra)

        qkv_raw = ar(0, 24, T + 3)
        qkv = ar(6216, 24, T)
        xp = ar(12360, NPOOL, PADP + T)
        pool_a = ar(13448, NPOOL, PADP + T)
        pool_b = ar(14536, NPOOL, PADP + T)
        pooled = ar(15624, NPOOL, T)
        z_s = ar(17672, 8, T)
        g_pool = ar(19720, 8, T)
        g_dn = ar(21768, 8, T)
        merged = ar(23816, 8, T)
        sq_qk = ar(0, 16, T)
        x_s = ar(0, 16, P)
        a_t = ar(2048, 16, P)
        qk_m = ar(4096, 16, P)
        bv = ar(12360, 16, P)
        k_dec = ar(14408, 8, P)
        q_dec = ar(15432, 8, P)
        s1 = ar(16456, 8, P)
        v_new = ar(10312, 16, P)
        resid = ar(2048, 8, P)
        d_m = ar(19720, 16, P)
        d_t = ar(0, 16, P, base=extra)
        off_t = [ar(6216, 16, P), ar(10312, 16, P)]
        o_t = ar(0, 8, T)
        sq_o = ar(0, 8, T, base=extra)
        small = 25864
        rn = ar(small, T)
        rn_s = ar(small + 256, T)
        rows = ar(small + 512, 512)
        ba_b = ar(small + 1024, 2, 8)
        ba_g = ar(small + 1040, 2, 8)
        sp1 = ar(small + 1056, 2, 8)
        sp2 = ar(small + 1072, 2, 8)
        sp3 = ar(small + 1088, 2, 8)
        neg_a = ar(small + 1104, 8)
        g_col = ar(small + 1120, 2, 8)
        g_end = ar(small + 1136, 8)
        k_sc = ar(small + 1144, 8)
        nbe = ar(small + 1152, 8)
        assert small + 1160 <= K2_AT
        dec = [ar(2048 + T * b, T, base=extra) for b in range(2)]
        tmp = [ar(2560 + T * b, T, base=extra) for b in range(2)]
        egb = [ar(3072 + P * b, P, base=extra) for b in range(2)]

        qk2 = ar(0, 8, T)
        v2 = ar(2048, 2, 512)
        bch = ar(3072, 12, T)
        ga2 = ar(6144, 8, T)
        gc2 = ar(8192, 8, T)
        zc = ar(10240, 4, T + 2)
        yc = ar(11272, 4, T)
        s_b = [ar(12296, 2, T), ar(12808, 2, T)]
        p_b = [ar(13320, 2, T), ar(13832, 2, T)]
        pt_b = [ar(14344, 384), ar(14728, 384)]
        vt = ar(15112, 4, T)
        mrg2 = ar(0, 8, T)
        stat = ar(16136, 8, 8)

        experts = arena[:, :].rearrange("p (n t) -> p n t", t=T)
        half1 = ARENA // 2
        qq = ar(0, 16, T)
        scores = ar(half1, 32, NKEYS)
        cand = ar(half1, 16, TOPK * TOPK)
        tv = ar(half1 + 4096, 32, TOPK)
        ti = ar(half1 + 4608, 32 * TOPK).bitcast(U32).rearrange("p (a b) -> p a b", b=TOPK)
        tif = ar(half1 + 5120, 32, TOPK)
        best = ar(half1 + 5632, 16, TOPK)
        bpos = ar(half1 + 5888, 16 * TOPK).bitcast(U32).rearrange("p (a b) -> p a b", b=TOPK)
        pos_u = ar(half1 + 6144, 2 * 256).bitcast(U32).rearrange("p (a b) -> p a b", b=256)
        pos_f = ar(half1 + 6656, 2, 256)
        sel3 = ar(half1 + 7168, 3, 256)
        ge_ = ar(half1 + 7936, 256)
        gsum = ar(half1 + 8192, 16)
        ginv = ar(half1 + 8208, 16)
        hot = ar(half1 + 8224, 2, PAIRS * TOPK)
        selt = ar(512, 3, T, base=extra)
        gate_rest = ar(1280, 2, T, base=extra)
        gate_parts = ar(1792, 384, base=extra).bitcast(BF16).rearrange("p (k t) -> p k t", k=3)
        hot_l = ar(2176, 512, base=extra).bitcast(BF16).rearrange("p (t n) -> p t n", t=GROUP)
        hot_eq = ar(2688, 256, base=extra).bitcast(BF16).rearrange("p (t n) -> p t n", t=GROUP)
        hot_r = [ar(at, 256, base=extra).bitcast(BF16).rearrange("p (t n) -> p t n", t=GROUP)
                 for at in (2944, 1280, 1536)]

        landed = [sem(f"landed{s}") for s in range(RING)]
        hi_ready = sem("w_hi_ready")
        taken = sem("w_taken")
        ada_landed = [sem(f"ada_landed{s}") for s in range(ADA_RING)]
        ada_taken = sem("ada_taken")
        ada_piece = sem("ada_piece")
        ada_diag = sem("ada_diag")
        used = sem("weights_used")

        def nth(u):
            return u - U_FFN1 + 1

        def landed_count(u, i=None, per=0):
            assert per % RING == 0
            n = 16 * (u // RING + 1)
            return n if i is None else i * (16 * (per // RING)) + n

        def plus(i, per, n):
            return n if i is None else i * per + n
        stage_done = sem("stage_done")

        def stage(eng, n):
            eng.drain().then_inc(stage_done, 1)
            eng.wait_ge(stage_done, 4 * n)

        def linker(eng, name):
            chain = sem(name)
            count = [0]

            def link(ins):
                ins.then_inc(chain, 1)
                count[0] += 1
                eng.wait_ge(chain, count[0])
            return link

        ST = {}
        for name in ("ada", "ffn0", "mix_proj", "mix_pool", "mix_norm", "mix_heads", "mix_solve", "mix_state", "mix_o",
                     "mix_out", "ffn1", "final1"):
            ST[name] = len(ST) + 1
        for l in range(LAYERS):
            for name in ("proj", "attn", "out", "wq", "peer_a", "peer_b", "peer_c", "peer_d"):
                ST[f"{name}{l}"] = len(ST) + 1

        def quarter(banks, r):
            return banks[:, r // 2, (r % 2) * T:(r % 2) * T + T]

        def shift1(s):
            return mod[:, 24 * s:24 * s + 8]

        def scale1(s):
            return mod[:, 24 * s + 8:24 * s + 16]

        def gate1(s):
            return mod[:, 24 * s + 16:24 * s + 24]

        def mod2(l, k):
            at = N_ADA1 + N_ADA2 * l + 8 * k
            return mod[:, at:at + 8]

        block = ctx.enter_context(nc.Block())

        @block.sync
        def _(sp):
            sp.dma_start(par[:, :], params[:, 0:N_PAR]).then_inc(sem("par_in"), 16)
            sp.wait_ge(ada_landed[1], 16)
            sp.dma_start(x_t[:, :, :].rearrange("p a t -> p (a t)"), params[:, N_PAR:N_PAR + DT * T])\
              .then_inc(sem("x_in"), 16)
            for s in range(RING):
                sp.dma_start(ring[:, s, :], weights[s]).then_inc(landed[s], 16)
            with sp.Fori(1, N_UNITS // RING) as i:
                for s in range(RING):
                    sp.wait_ge(taken, i * RING + (s + 1 - RING))
                    sp.dma_start(ring[:, s, :],
                                 weights[bass.ds(i * RING + s, 1), :, :].rearrange("a p n -> p (a n)"))\
                      .then_inc(landed[s], 16)

        @block.scalar
        def _(eng):
            link = linker(eng, "act_chain")
            nc_a = nc.scalar
            eng.dma_start(k1[:, :], const1).then_inc(sem("k1_in"), 16)
            def hi(u, i=None, per=0):
                eng.wait_ge(landed[u % RING], landed_count(u, i, per))
                if u >= U_FFN1 + 2:
                    eng.wait_ge(used, plus(i, per, nth(u - 2)))
                nc_a.activation(w_hi[:, u % 2, :], ring[:, u % RING, :], ACT.Copy).then_inc(hi_ready, 1)

            def step(u, i=None, per=0):
                if u + 2 < N_UNITS:
                    hi(u + 2, i, per)
                else:
                    eng.wait_ge(used, nth(u))

            def steps(u, n):
                for k in range(n):
                    step(u + k)

            def split(name, before, src, n):
                for half in range(2):
                    t = slice(half * n // 2, (half + 1) * n // 2)
                    eng.wait_ge(sem(name + "_full"), before + half + 1)
                    nc_a.activation(h_hi[:, t, :], src[:, t, :], ACT.Copy).then_inc(sem(name + "_hi"), 1)

            def squares(n):
                for t in range(DT):
                    if n > 0:
                        eng.wait_ge(sem("x_tile"), DT * (n - 1) + t + 1)
                    nc_a.activation(nh[:, t, :], x_t[:, t, :], ACT.Square).then_inc(sem("sq"), 1)
                eng.wait_ge(sem("sumsq"), n + 1)
                nc_a.activation(std, st[:, 3, 0:T], ACT.Sqrt, scale=1.0 / D, bias=kc("eps")).then_inc(sem("std"), 1)

            def norm(m, shift):
                for t in range(DT):
                    eng.wait_ge(sem("nh"), DT * m + t + 1)
                    nc_a.activation(h_hi[:, t, :], nh[:, t, :], ACT.Identity, bias=shift[:, t:t + 1])\
                        .then_inc(sem("norm_hi"), 1)

            eng.wait_ge(sem("par_in"), 16)
            eng.wait_ge(sem("k1_in"), 16)
            nc_a.activation(sc[:, :], pc("c"), ACT.Silu).then_inc(sem("silu_c"), 1)
            hi(U_FFN1)
            hi(U_FFN1 + 1)
            eng.wait_ge(sem("x_in"), 16)
            squares(0)
            stage(eng, ST["ada"])

            def ffn(f):
                if f == 0:
                    eng.dma_start(arena[:, K2_AT:K2_AT + N_K2], const2).then_inc(sem("k2_in"), 16)
                    eng.dma_start(arena[:, sw_at:sw_at + N_SMALLW], smallw).then_inc(sem("sw_in"), 16)
                norm((0, 2)[f], shift1(2 * f))
                base = (U_FFN1, U_FFN2)[f]

                def silu(b):
                    nc_a.activation(gate_s[:, b, :], st[:, b, 0:T], ACT.Silu).then_inc(sem("silu_gate"), 1)

                def upper(j, i=None):
                    eng.wait_ge(sem("act"), plus(i, 4, FT * f + j + 1))
                    nc_a.activation(act_hi[:, j % 2, :], act[:, j % 2, :], ACT.Copy).then_inc(sem("act_hi"), 1)

                def body(j, i=None, per=0):
                    silu((j + 1) % 2)
                    step(base + 3 + 3 * j, i, per)
                    upper(j + 1, i)
                    step(base + 4 + 3 * j, i, per)
                    step(base + 5 + 3 * j, i, per)

                step(base)
                silu(0)
                step(base + 1)
                upper(0)
                step(base + 2)
                body(0)
                with eng.Fori(0, (FT - 2) // 4) as i:
                    for j in range(4):
                        body(1 + j, i, 12)

            ffn(0)
            squares(1)
            stage(eng, ST["ffn0"])

            norm(1, shift1(1))
            for p in range(14):
                steps(U_MIX + 2 * p, 2)
                src = st[:, p % 4, :].rearrange("p (u t) -> p u t", u=2)
                if p < 2:
                    dst = xp[:, 2 * p:2 * p + 2, PADP:PADP + T]
                else:
                    dst = qkv_raw[:, 2 * (p - 2):2 * (p - 1), 3:3 + T]
                nc_a.activation(dst, src, ACT.Copy).then_inc(sem("proj_out"), 1)
                if p >= 4:
                    m = p - 4
                    eng.wait_ge(sem("conv"), m + 1)
                    nc_a.activation(qkv[:, 2 * m:2 * m + 2, :], qkv[:, 2 * m:2 * m + 2, :], ACT.Silu)\
                        .then_inc(sem("qkv_silu"), 1)
            for p in range(14, 26):
                steps(U_MIX + 2 * p, 2)
                if p < 16:
                    m = p - 4
                    eng.wait_ge(sem("conv"), m + 1)
                    nc_a.activation(qkv[:, 2 * m:2 * m + 2, :], qkv[:, 2 * m:2 * m + 2, :], ACT.Silu)\
                        .then_inc(sem("qkv_silu"), 1)
                m = p - 14
                dst = (z_s, g_pool, g_dn)[m // 4][:, 2 * (m % 4):2 * (m % 4) + 2, :]
                src = st[:, p % 4, :].rearrange("p (u t) -> p u t", u=2)
                nc_a.activation(dst, src, ACT.Silu if m < 4 else ACT.Sigmoid).then_inc(sem("proj_out"), 1)
            eng.wait_ge(sem("ba_psum"), 1)
            ba_ps = acc[:, 0, 0:32].rearrange("p (c n) -> p c n", n=16)
            nc_a.activation(ba_b, ba_ps[:, :, 0:8], ACT.Sigmoid).then_inc(sem("beta"), 1)
            link(nc_a.activation(neg_a, pc("a_log"), ACT.Exp))
            eng.wait_ge(sem("a_in"), 1)
            link(nc_a.activation(sp2, sp1, ACT.Abs))
            link(nc_a.activation(sp2, sp2, ACT.Exp, scale=-1.0))
            nc_a.activation(sp3, sp2, ACT.Ln, bias=1.0).then_inc(sem("ln1p"), 1)
            stage(eng, ST["mix_proj"])
            eng.wait_ge(sem("pool_mm"), 1)
            for g in range(NPOOL):
                nc_a.activation(h_hi[:, g, :], st[:, g // 2, (g % 2) * T:(g % 2) * T + T], ACT.Copy,
                                scale=pc("pool_scale", g, 1)).then_inc(sem("ya0_hi"), 1)
            steps(U_POOLP, 4)
            stage(eng, ST["mix_pool"])

            eng.wait_ge(sem("sum_qk"), 1)
            nc_a.activation(rn_s[0:16, :], st[0:16, 0, 0:T], ACT.Sqrt, scale=kc("qk_scale")[0:16, :],
                            bias=kc("qk_eps")[0:16, :]).then_inc(sem("std_qk"), 1)
            stage(eng, ST["mix_norm"])

            for h in range(HEADS):
                b = h % 2
                eng.wait_ge(sem("dec_arg"), h + 1)
                nc_a.activation(dec[b], dec[b], ACT.Exp).then_inc(sem("dec"), 1)
                nc_a.activation(egb[b], st[:, b, 128:256], ACT.Exp).then_inc(sem("dec"), 1)
            eng.wait_ge(sem("k_arg"), 1)
            link(nc_a.activation(k_sc, k_sc, ACT.Exp))
            link(nc_a.activation(nbe, g_col[:, 1, :], ACT.Exp))
            for q in range(6):
                eng.wait_ge(sem("tok_t"), q + 1)
                for j in range(4):
                    n = 4 * q + j
                    src = acc[:, q % 4, j * 128:(j + 1) * 128]
                    if n < 16:
                        ins = nc_a.activation(bv[:, n, :], src, ACT.Copy, scale=ba_b[:, n // 8, n % 8:n % 8 + 1])
                    else:
                        ins = nc_a.activation(k_dec[:, n - 16, :], src, ACT.Copy, scale=k_sc[:, n - 16:n - 15])
                ins.then_inc(sem("tok_out"), 1)
            stage(eng, ST["mix_heads"])

            for lv in range(1, LEVELS):
                for g in range(4):
                    eng.wait_ge(sem("lv_x"), 4 * lv + g + 1)
                    nc_a.activation(x_s[:, 4 * g:4 * g + 4, :], st[:, g, :].rearrange("p (a b) -> p a b", b=128),
                                    ACT.Copy).then_inc(sem("lv_xs"), 1)
            stage(eng, ST["mix_solve"])

            def out_of(dst, src, name):
                nc_a.activation(dst, src.rearrange("p (a b) -> p a b", b=128), ACT.Copy).then_inc(sem(name), 1)

            for g in range(2):
                eng.wait_ge(sem("vn0_psum"), g + 1)
                out_of(v_new[:, 4 * g:4 * g + 4, :], acc[:, g, :], "vn0")
            for g in range(2):
                eng.wait_ge(sem("s1_psum"), g + 1)
                out_of(s1[:, 4 * g:4 * g + 4, :], acc[:, 2 + g, :], "s1")
            for g in range(2):
                eng.wait_ge(sem("vn1_psum"), g + 1)
                out_of(v_new[:, 8 + 4 * g:12 + 4 * g, :], acc[:, g, :], "vn1")
            for m in range(4):
                eng.wait_ge(sem("o_psum"), m + 1)
                nc_a.activation(o_t[:, 2 * m:2 * m + 2, :], st[:, m, :].rearrange("p (u t) -> p u t", u=2),
                                ACT.Copy).then_inc(sem("o_t"), 1)
            stage(eng, ST["mix_state"])
            eng.wait_ge(sem("sum_o"), 1)
            nc_a.activation(rn_s[0:8, :], st[0:8, 0, 0:T], ACT.Sqrt, scale=1.0 / P, bias=kc("eps")[0:8, :])\
                .then_inc(sem("std_o"), 1)
            split("o", 0, o_t, 8)
            stage(eng, ST["mix_o"])
            steps(U_DNP, 8)
            split("merged", 0, merged, 8)
            steps(U_MIXO, 8)
            squares(2)
            stage(eng, ST["mix_out"])

            ffn(1)
            squares(3)
            stage(eng, ST["ffn1"])
            squares(4)
            stage(eng, ST["final1"])

            for l in range(LAYERS):
                U = U_L2 + N_L2 * l
                norm(3 + 2 * l, mod2(l, 0))
                for p in range(20):
                    steps(U + O_QK + 2 * p, 2)
                    src = st[:, p % 4, :].rearrange("p (u t) -> p u t", u=2)
                    if p < 4:
                        dst = qk2[:, 2 * p:2 * p + 2, :]
                    elif p < 6:
                        dst = vt[:, 2 * p - 8:2 * p - 6, :]
                    elif p < 12:
                        dst = bch[:, 2 * p - 12:2 * p - 10, :]
                    else:
                        dst = (ga2, gc2)[(p - 12) // 4][:, 2 * ((p - 12) % 4):2 * ((p - 12) % 4) + 2, :]
                    nc_a.activation(dst, src, ACT.Copy if p < 12 else ACT.Sigmoid).then_inc(sem("proj2"), 1)
                stage(eng, ST[f"proj{l}"])

                eng.wait_ge(sem("v_tok"), l + 1)
                nc_a.activation(v2, acc[:, 0:2, :], ACT.Copy).then_inc(sem("v2"), 1)
                for h in range(AH):
                    b = h % 2
                    n = AH * l + h
                    eng.wait_ge(sem("smax"), n + 1)
                    for q in range(2):
                        nc_a.activation(p_b[b][:, q, :], s_b[b][:, q, :], ACT.Exp, scale=AHD ** -0.5,
                                        bias=stat[:, b, 2 + q:3 + q], accum_out=stat[:, b, 4 + q:5 + q])\
                            .then_inc(sem("pexp"), 1)
                    eng.wait_ge(sem("pt_psum"), n + 1)
                    nc_a.activation(pt_b[b], acc[:, b, 0:384], ACT.Copy).then_inc(sem("pt"), 1)
                for m in range(2):
                    eng.wait_ge(sem("pv"), 8 * l + 4 * m + 4)
                    nc_a.activation(h_hi[:, 2 * m:2 * m + 2, :], acc[:, 2 + m, :].rearrange("p (u t) -> p u t", u=2),
                                    ACT.Copy).then_inc(sem("y_hi"), 1)
                eng.wait_ge(sem("yc_full"), l + 1)
                nc_a.activation(h_hi[:, 4:8, :], yc, ACT.Copy).then_inc(sem("yc_hi"), 1)
                stage(eng, ST[f"attn{l}"])
                steps(U + O_AP, 8)
                split("mrg2", 2 * l, mrg2, 8)
                steps(U + O_OUT, 8)
                squares(5 + 2 * l)
                stage(eng, ST[f"out{l}"])

                norm(4 + 2 * l, mod2(l, 3))
                for p in range(8):
                    steps(U + O_WQ + 2 * p, 2)
                    nc_a.activation(qq[:, 2 * p:2 * p + 2, :], st[:, p % 4, :].rearrange("p (u t) -> p u t", u=2),
                                    ACT.Copy).then_inc(sem("qq"), 1)
                if l == 0:
                    eng.wait_ge(ada_taken, 8 * N_BLOCKS)
                for u in range(2):
                    for t in range(TT):
                        for half in range(2):
                            if (t, half) == (1, 1):
                                step(U + O_SK + u)
                            else:
                                eng.wait_ge(sem("sk"), 6 * l + 3 * u + 2 * t + half + 1)
                            nc_a.activation(scores[:, 16 * t + 8 * u + 4 * half:16 * t + 8 * u + 4 * half + 4, :],
                                            acc[:, 2 * t + half, :].rearrange("p (a b) -> p a b", b=128), ACT.Copy)\
                                .then_inc(sem("scores"), 1)
                stage(eng, ST[f"wq{l}"])
                base = U + O_PEER
                n_key = NKEYS * l

                def gelu_of(n, i=None):
                    dst = experts[:, n, :] if i is None else \
                        experts[:, bass.ds(i * 4 + n, 1), :].rearrange("p a t -> p (a t)")
                    nc_a.activation(dst, st[:, n % 2, 0:T], ACT.Gelu_apprx_tanh).then_inc(sem("gelu"), 1)

                def u_half(first, between=None):
                    step(base + first)
                    with eng.Fori(0, HALF // 4 - 1) as i:
                        for k in range(4):
                            gelu_of(first + k, i)
                            step(base + first + k + 1, i, 4)
                    if between is not None:
                        between()
                    for n in range(first + HALF - EXP_BEFORE, first + HALF):
                        gelu_of(n)
                        if n + 1 < first + HALF:
                            step(base + n + 1)

                def gates_exp():
                    eng.wait_ge(sem("best_c"), l + 1)
                    nc_a.activation(ge_, ge_, ACT.Exp).then_inc(sem("gexp"), 1)

                u_half(0, gates_exp)
                eng.wait_ge(sem("sel_psum"), l + 1)
                nc_a.activation(selt, st[:, 2:4, :].rearrange("p a b -> p (a b)")[:, 0:3 * T]
                                .rearrange("p (k t) -> p k t", k=3), ACT.Copy).then_inc(sem("selt"), 1)
                stage(eng, ST[f"peer_a{l}"])
                u_half(HALF)
                stage(eng, ST[f"peer_b{l}"])

                def upper(n, i=None):
                    src = experts[:, n, :] if i is None else \
                        experts[:, bass.ds(i * 4 + n, 1), :].rearrange("p a t -> p (a t)")
                    nc_a.activation(act_hi[:, n % 2, :], src, ACT.Copy).then_inc(sem("gated_hi"), 1)

                def v_half(first):
                    v_base = base + NKEYS
                    upper(first)
                    upper(first + 1)
                    with eng.Fori(0, HALF // 4 - 1) as i:
                        for k in range(4):
                            eng.wait_ge(used, plus(i, 4, nth(v_base + first + k)))
                            upper(first + k + 2, i)
                            step(v_base + first + k, i, 4)
                    for n in range(first + HALF - 4, first + HALF):
                        if n + 2 < first + HALF:
                            eng.wait_ge(used, nth(v_base + n))
                            upper(n + 2)
                        step(v_base + n)

                v_half(0)
                stage(eng, ST[f"peer_c{l}"])
                v_half(HALF)
                squares(6 + 2 * l)
                stage(eng, ST[f"peer_d{l}"])

        @block.vector
        def _(eng):
            link = linker(eng, "dve_chain")
            v = nc.vector
            v.memset(zrow[:, :], 0.0).then_inc(sem("zrow"), 1)

            def lo(u, i=None, per=0):
                eng.wait_ge(hi_ready, plus(i, per, nth(u)))
                v.tensor_tensor(w_lo[:, u % 2, :], ring[:, u % RING, :], w_hi[:, u % 2, :], ALU.subtract)\
                    .then_inc(taken, 1)

            def step(u, i=None, per=0):
                if u + 2 < N_UNITS:
                    lo(u + 2, i, per)
                else:
                    eng.wait_ge(used, nth(u))

            def steps(u, n):
                for k in range(n):
                    step(u + k)

            def split(name, before, src, n, at=0):
                for half in range(2):
                    t = slice(half * n // 2, (half + 1) * n // 2)
                    eng.wait_ge(sem(name + "_hi"), before + half + 1)
                    v.tensor_tensor(h_lo[:, t, :], src[:, t, :], h_hi[:, t, :], ALU.subtract)\
                        .then_inc(sem(name + "_lo"), 1)

            def norm(n, a, b, dst, m=None):
                eng.wait_ge(sem("std"), n + 1)
                link(v.reciprocal(rstd, std))

                def lower(t):
                    eng.wait_ge(sem("norm_hi"), DT * m + t + 1)
                    v.scalar_tensor_tensor(out=h_lo[:, t, :], in0=nh[:, t, :], scalar=b[:, t:t + 1],
                                           in1=h_hi[:, t, :], op0=ALU.add, op1=ALU.subtract)\
                        .then_inc(sem("norm_lo"), 1)

                for t in range(DT):
                    ins = v.scalar_tensor_tensor(out=dst[:, t, :], in0=x_t[:, t, :], scalar=a[:, t:t + 1], in1=rstd,
                                                 op0=ALU.mult, op1=ALU.mult)
                    ins.then_inc(sem("nh" if b is not None else "normed" if n == 8 else "x_tile"), 1)
                    if b is not None and t >= 2:
                        lower(t - 2)
                if b is not None:
                    lower(DT - 2)
                    lower(DT - 1)

            def mac(q, k, sums, i=None):
                n = 8 * q + k
                vec = sc if q < N_ADA1 // 8 else pc("c2")
                w = ada_ring[:, n % ADA_RING, :]
                eng.wait_ge(ada_landed[n % ADA_RING], plus(i, 16 * (8 // ADA_RING), 16 * (n // ADA_RING + 1)))
                if k == 0:
                    ins = v.tensor_scalar(sums, w, vec[:, k:k + 1], None, ALU.mult)
                else:
                    eng.wait_ge(ada_taken, plus(i, 8, n))
                    ins = v.scalar_tensor_tensor(out=sums, in0=w, scalar=vec[:, k:k + 1], in1=sums,
                                                 op0=ALU.mult, op1=ALU.add)
                ins.then_inc(ada_taken, 1)

            def take(q, r, src, i=None, upto=None, between=None):
                n = 4 * q + r
                eng.wait_ge(ada_piece, plus(i, 4, 4 * q + (r if upto is None else upto) + 1))
                if n > 0:
                    eng.wait_ge(sem("ada_mod"), plus(i, 4, n))
                v.tensor_tensor(diag, src.rearrange("p (u n) -> p u n", n=P),
                                ident.unsqueeze(1).to_broadcast([P, 2, P]), ALU.mult).then_inc(ada_diag, 1)
                if between is not None:
                    between()
                eng.wait_ge(ada_diag, plus(i, 4, n + 1))
                dst = mod[:, 2 * n:2 * n + 2] if i is None else mod[:, bass.ds(i * 8 + 2 * n, 2)]
                v.tensor_reduce(dst, diag, AX, ALU.add).then_inc(sem("ada_mod"), 1)

            def take_block(q, banks):
                for r in range(4):
                    take(q, r, quarter(banks, r), upto=r | 1)

            def add_bias(first, last):
                cols = slice(8 * first, 8 * last)
                eng.wait_ge(sem("ada_mod"), 4 * last)
                link(v.tensor_tensor(mod[:, cols], mod[:, cols], pc("ada_b", 8 * first, 8 * (last - first)), ALU.add))

            def scale1_of(s):
                link(v.scalar_tensor_tensor(out=nscale[:, 8 * s:8 * s + 8], in0=scale1(s), scalar=1.0,
                                            in1=pc("norm_g", 8 * s, 8), op0=ALU.add, op1=ALU.mult))

            def scale2_of(l, k):
                at = 24 + 16 * l + 8 * k
                link(v.scalar_tensor_tensor(out=nscale[:, at:at + 8], in0=mod2(l, 3 * k + 1), scalar=1.0,
                                            in1=pc(("n1g2", "n2g2")[k], 8 * l, 8), op0=ALU.add, op1=ALU.mult))

            eng.wait_ge(sem("par_in"), 16)
            eng.wait_ge(sem("silu_c"), 1)
            eng.wait_ge(sem("k1_in"), 16)
            for q in range(Q_FFN[0]):
                for k in range(8):
                    mac(q, k, part[:, q % 2, :])
                    if k == 3 and q > 0:
                        take_block(q - 1, st[:, 2 * ((q - 1) % 2):, :])
            lo(U_FFN1)
            lo(U_FFN1 + 1)
            take_block(Q_FFN[0] - 1, st[:, 2 * ((Q_FFN[0] - 1) % 2):, :])
            add_bias(0, Q_FFN[0])
            scale1_of(0)
            eng.wait_ge(sem("x_in"), 16)
            stage(eng, ST["ada"])

            def add_to_x(gate):
                for t in range(DT):
                    ins = v.scalar_tensor_tensor(out=x_t[:, t, :], in0=acc_t[:, t, :], scalar=gate[:, t:t + 1],
                                                 in1=x_t[:, t, :], op0=ALU.mult, op1=ALU.add)
                    ins.then_inc(sem("x_tile"), 1)

            def ffn(f):
                norm((0, 2)[f], nscale[:, 16 * f:16 * f + 8], shift1(2 * f), nh, (0, 2)[f])
                base = (U_FFN1, U_FFN2)[f]

                def mult(j, i=None):
                    eng.wait_ge(sem("silu_gate"), plus(i, 4, FT * f + j + 1))
                    b = j % 2
                    v.tensor_tensor(act[:, b, :], gate_s[:, b, :], st[:, 2 + b, 0:T], ALU.mult).then_inc(sem("act"), 1)

                def lower(j, i=None):
                    eng.wait_ge(sem("act_hi"), plus(i, 4, FT * f + j + 1))
                    b = j % 2
                    v.tensor_tensor(act_lo[:, b, :], act[:, b, :], act_hi[:, b, :], ALU.subtract)\
                        .then_inc(sem("act_lo"), 1)

                q0 = Q_FFN[f]

                def body(j, i=None, per=0):
                    t, k = max(j - 1, 0) // 4, (j - 1) % 4
                    sums = part_ffn[:, t, :] if i is None else \
                        part_ffn[:, bass.ds(i * 1 + t, 1), :].rearrange("p a n -> p (a n)")
                    step(base + 2 + 3 * j, i, per)
                    if j > 0:
                        mac(q0 + t, 2 * k, sums, i)
                    step(base + 3 + 3 * j, i, per)
                    mult(j + 1, i)

                    def rest():
                        if j > 0:
                            mac(q0 + t, 2 * k + 1, sums, i)
                        lower(j + 1, i)
                        step(base + 4 + 3 * j, i, per)

                    if j > 4:
                        take(q0 + t - 1, k, st[:, 2 + (j + 1) % 2, T:2 * T], i, between=rest)
                    else:
                        rest()

                step(base)
                step(base + 1)
                mult(0)
                lower(0)
                for j in range(5):
                    body(j)
                with eng.Fori(0, (FT - 6) // 4) as i:
                    for j in range(4):
                        body(5 + j, i, 12)
                take_block(q0 + 4, st[:, 2:4, :])
                add_bias(q0, q0 + 5)
                link(v.tensor_scalar(half_gate[:, 8 * f:8 * f + 8], gate1(2 * f), 0.5, None, ALU.mult))
                step(base + N_FFN - 1)
                add_to_x(half_gate[:, 8 * f:8 * f + 8])

            ffn(0)
            scale1_of(1)
            scale1_of(2)
            stage(eng, ST["ffn0"])

            norm(1, nscale[:, 8:16], shift1(1), nh, 1)
            v.memset(qkv_raw[:, :, 0:3], 0.0).then_inc(sem("pad"), 1)
            eng.wait_ge(sem("pad"), 1)

            def conv(m):
                eng.wait_ge(sem("proj_out"), m + 3)
                for j in range(CONV):
                    for t in (2 * m, 2 * m + 1):
                        w = pc("conv_w", 24 * j + t, 1)
                        if j == 0:
                            ins = v.tensor_scalar(qkv[:, t, :], qkv_raw[:, t, 0:T], w, None, ALU.mult)
                        else:
                            ins = v.scalar_tensor_tensor(out=qkv[:, t, :], in0=qkv_raw[:, t, j:j + T], scalar=w,
                                                         in1=qkv[:, t, :], op0=ALU.mult, op1=ALU.add)
                    if j < CONV - 1:
                        link(ins)
                ins.then_inc(sem("conv"), 1)

            for p in range(26):
                steps(U_MIX + 2 * p, 2)
                if 3 <= p < 15:
                    conv(p - 3)
            eng.wait_ge(sem("ba_psum"), 1)
            ba_ps = acc[:, 0, 0:32].rearrange("p (c n) -> p c n", n=16)
            eng.wait_ge(sem("beta"), 1)
            v.tensor_tensor(sp1, ba_ps[:, :, 8:16], pc("dt_bias").unsqueeze(1).to_broadcast([P, 2, 8]), ALU.add)\
                .then_inc(sem("a_in"), 1)
            eng.wait_ge(sem("ln1p"), 1)
            link(v.scalar_tensor_tensor(out=sp1, in0=sp1, scalar=0.0, in1=sp3, op0=ALU.max, op1=ALU.add))
            link(v.scalar_tensor_tensor(out=ba_g, in0=sp1, scalar=-1.0,
                                        in1=neg_a.unsqueeze(1).to_broadcast([P, 2, 8]), op0=ALU.mult, op1=ALU.mult))
            stage(eng, ST["mix_proj"])

            eng.wait_ge(sem("pool_mm"), 1)
            for g in range(NPOOL):
                eng.wait_ge(sem("ya0_hi"), 2 * (g // 2) + 2)
                v.scalar_tensor_tensor(out=h_lo[:, g, :], in0=st[:, g // 2, (g % 2) * T:(g % 2) * T + T],
                                       scalar=pc("pool_scale", g, 1), in1=h_hi[:, g, :], op0=ALU.mult,
                                       op1=ALU.subtract).then_inc(sem("ya0_lo"), 1)
            v.tensor_tensor(sq_qk, qkv[:, 0:16, :], qkv[:, 0:16, :], ALU.mult).then_inc(sem("sq_qk"), 1)
            steps(U_POOLP, 4)
            link(v.tensor_tensor(merged, acc_t, g_pool, ALU.mult))
            stage(eng, ST["mix_pool"])

            eng.wait_ge(sem("std_qk"), 1)
            v.reciprocal(rn[0:16, :], rn_s[0:16, :]).then_inc(sem("rn"), 1)
            eng.wait_ge(sem("g_rows"), 1)
            v.tensor_copy(rows[0:8, :], st[0:8, 1, :]).then_inc(sem("rows"), 1)
            v.tensor_copy(g_col, st[:, 2, 0:16].rearrange("p (c n) -> p c n", n=8)).then_inc(sem("rows"), 1)
            for m in range(8):
                eng.wait_ge(sem("rn_b"), m + 1)
                v.tensor_tensor(qkv[:, 2 * m:2 * m + 2, :], qkv[:, 2 * m:2 * m + 2, :],
                                acc[:, m % 4, :].rearrange("p (u t) -> p u t", u=2), ALU.mult)\
                    .then_inc(sem("qk_n"), 1)
            stage(eng, ST["mix_norm"])

            for h in range(HEADS):
                b = h % 2
                eng.wait_ge(sem("bc"), h + 1)
                dec3 = dec[b].rearrange("p (c i) -> p c i", c=2)
                tmp3 = tmp[b].rearrange("p (c i) -> p c i", c=2)
                v.tensor_copy(g_end[:, h:h + 1], st[:, b, 127:128])
                for c in range(2):
                    ins = v.scalar_tensor_tensor(out=dec3[:, c, :], in0=st[:, b, c * 128:(c + 1) * 128],
                                                 scalar=g_col[:, c, h:h + 1], in1=future,
                                                 op0=ALU.subtract, op1=ALU.add)
                ins.then_inc(sem("dec_arg"), 1)
                eng.wait_ge(sem("dec"), 2 * h + 2)
                eng.wait_ge(sem("kkqk"), h + 1)
                kk = st[:, 2 + b, 0:256].rearrange("p (c i) -> p c i", c=2)
                qk = st[:, 2 + b, 256:512].rearrange("p (c i) -> p c i", c=2)
                link(v.tensor_tensor(tmp3, kk, dec3, ALU.mult))
                both = a_t.rearrange("p (c h) i -> p c h i", c=2)[:, :, h, :]
                v.tensor_tensor(both, tmp3, st[:, b, 256:512].rearrange("p (c i) -> p c i", c=2), ALU.mult)
                v.tensor_tensor(qk_m.rearrange("p (c h) i -> p c h i", c=2)[:, :, h, :], qk, dec3, ALU.mult)
                v.tensor_tensor(q_dec[:, h, :], qkv[:, h, 128:256], egb[b], ALU.mult).then_inc(sem("head"), 1)
            eng.wait_ge(sem("head"), HEADS)
            v.tensor_tensor(k_sc, g_end, g_col[:, 0, :], ALU.subtract).then_inc(sem("k_arg"), 1)
            v.tensor_copy(d_m, ident.unsqueeze(1).to_broadcast([P, 16, P]))
            v.tensor_copy(d_t, ident.unsqueeze(1).to_broadcast([P, 16, P]))
            stage(eng, ST["mix_heads"])

            for g in range(4):
                eng.wait_ge(sem("lv_x"), g + 1)
                sl = slice(4 * g, 4 * g + 4)
                v.tensor_tensor(d_m[:, sl, :], d_m[:, sl, :], st[:, g, :].rearrange("p (a b) -> p a b", b=128),
                                ALU.subtract)
                v.tensor_tensor(d_t[:, sl, :], d_t[:, sl, :], off_t[0][:, sl, :], ALU.subtract)\
                    .then_inc(sem("lv_d"), 1)
            for lv in range(1, LEVELS):
                for g in range(4):
                    eng.wait_ge(sem("lv_dx"), 4 * (lv - 1) + g + 1)
                    b = 2 * (g % 2)
                    sl = slice(4 * g, 4 * g + 4)
                    if lv < LEVELS - 1:
                        v.tensor_tensor(d_m[:, sl, :], d_m[:, sl, :],
                                        acc[:, b, :].rearrange("p (a b) -> p a b", b=128), ALU.subtract)
                    v.tensor_tensor(d_t[:, sl, :], d_t[:, sl, :],
                                    acc[:, b + 1, :].rearrange("p (a b) -> p a b", b=128),
                                    ALU.subtract).then_inc(sem("lv_d"), 1)
            link(v.scalar_tensor_tensor(out=nbe, in0=nbe, scalar=-1.0, in1=ba_b[:, 1, :], op0=ALU.mult, op1=ALU.mult))
            stage(eng, ST["mix_solve"])

            for h in range(HEADS):
                if h % 4 == 0:
                    eng.wait_ge(sem("ks1_psum"), h // 4 + 1)
                ins = v.scalar_tensor_tensor(out=resid[:, h, :], in0=st[:, h // 4, (h % 4) * 128:(h % 4) * 128 + 128],
                                             scalar=nbe[:, h:h + 1], in1=bv[:, 8 + h, :], op0=ALU.mult, op1=ALU.add)
                if h % 4 == 3:
                    ins.then_inc(sem("resid"), 1)
            eng.wait_ge(sem("o_t"), 4)
            v.tensor_tensor(sq_o, o_t, o_t, ALU.mult).then_inc(sem("sq_o"), 1)
            stage(eng, ST["mix_state"])
            eng.wait_ge(sem("std_o"), 1)
            v.reciprocal(rn[0:8, :], rn_s[0:8, :]).then_inc(sem("rn_o"), 1)
            for m in range(4):
                eng.wait_ge(sem("rno_b"), m + 1)
                o2 = o_t[:, 2 * m:2 * m + 2, :]
                link(v.scalar_tensor_tensor(out=o2, in0=o2, scalar=pc("dn_g"),
                                            in1=acc[:, m, :].rearrange("p (u t) -> p u t", u=2),
                                            op0=ALU.mult, op1=ALU.mult))
                ins = v.tensor_tensor(o2, o2, z_s[:, 2 * m:2 * m + 2, :], ALU.mult)
                if m % 2 == 1:
                    ins.then_inc(sem("o_full"), 1)
            split("o", 0, o_t, 8)
            stage(eng, ST["mix_o"])
            steps(U_DNP, 8)
            for half in range(2):
                t = slice(4 * half, 4 * half + 4)
                link(v.tensor_tensor(g_dn[:, t, :], acc_t[:, t, :], g_dn[:, t, :], ALU.mult))
                v.tensor_tensor(merged[:, t, :], merged[:, t, :], g_dn[:, t, :], ALU.add)\
                    .then_inc(sem("merged_full"), 1)
            split("merged", 0, merged, 8)
            steps(U_MIXO, 8)
            add_to_x(gate1(1))
            stage(eng, ST["mix_out"])

            ffn(1)
            stage(eng, ST["ffn1"])
            norm(3, pc("final_g"), None, x_t)
            scale2_of(0, 0)
            stage(eng, ST["final1"])

            for l in range(LAYERS):
                U = U_L2 + N_L2 * l
                norm(4 + 2 * l, nscale[:, 24 + 16 * l:32 + 16 * l], mod2(l, 0), nh, 3 + 2 * l)
                for k in range(40):
                    step(U + O_QK + k)
                    if l == 0:
                        mac(Q_PROJ + k // 8, k % 8, part[:, (Q_PROJ + k // 8) % 2, :])
                        if k % 8 == 2 and k > 8:
                            q = Q_PROJ + k // 8 - 1
                            take_block(q, acc[:, 2 * (q % 2):, :])
                stage(eng, ST[f"proj{l}"])
                for h in range(AH):
                    b = h % 2
                    n = AH * l + h
                    eng.wait_ge(sem("s_psum"), n + 1)
                    link(v.scalar_tensor_tensor(out=s_b[b], in0=dist.rearrange("p (q s) -> p q s", q=2),
                                                scalar=-(2.0 ** (-8.0 * (h + 1) / AH)) * AHD ** 0.5,
                                                in1=st[:, b, :].rearrange("p (q s) -> p q s", q=2),
                                                op0=ALU.mult, op1=ALU.add))
                    link(v.tensor_reduce(stat[:, b, 0:2], s_b[b], AX, ALU.max))
                    v.tensor_scalar(stat[:, b, 2:4], stat[:, b, 0:2], -(AHD ** -0.5), None, ALU.mult)\
                        .then_inc(sem("smax"), 1)
                    eng.wait_ge(sem("pexp"), 2 * n + 2)
                    link(v.reciprocal(stat[:, b, 6:8], stat[:, b, 4:6]))
                    for q in range(2):
                        ins = v.tensor_scalar(p_b[b][:, q, :], p_b[b][:, q, :], stat[:, b, 6 + q:7 + q], None, ALU.mult)
                    ins.then_inc(sem("p"), 1)
                eng.wait_ge(sem("zc"), l + 1)
                for j in range(CONV2):
                    for t in range(4):
                        w = pc("conv_w2", (l * CONV2 + j) * 4 + t, 1)
                        if j == 0:
                            ins = v.tensor_scalar(yc[:, t, :], zc[:, t, 0:T], w, None, ALU.mult)
                        else:
                            ins = v.scalar_tensor_tensor(out=yc[:, t, :], in0=zc[:, t, j:j + T], scalar=w,
                                                         in1=yc[:, t, :], op0=ALU.mult, op1=ALU.add)
                    link(ins)
                v.tensor_tensor(yc, yc, bch[:, 0:4, :], ALU.mult).then_inc(sem("yc_full"), 1)
                for m in range(2):
                    eng.wait_ge(sem("y_hi"), 2 * l + m + 1)
                    v.tensor_tensor(h_lo[:, 2 * m:2 * m + 2, :], acc[:, 2 + m, :].rearrange("p (u t) -> p u t", u=2),
                                    h_hi[:, 2 * m:2 * m + 2, :], ALU.subtract)
                eng.wait_ge(sem("yc_hi"), l + 1)
                v.tensor_tensor(h_lo[:, 4:8, :], yc, h_hi[:, 4:8, :], ALU.subtract)
                stage(eng, ST[f"attn{l}"])

                def out_steps(first, n, banks=st):
                    for k in range(first, first + n):
                        step(U + O_AP + k)
                        if l == 0:
                            for m in range(3 * k // 4, 3 * (k + 1) // 4):
                                mac(Q_OUT + m // 8, m % 8, part[:, (Q_OUT + m // 8) % 2, :])
                            if k in OUT_TAKES:
                                q = OUT_TAKES[k]
                                take_block(q, banks[:, 2 * (q % 2):, :])

                out_steps(0, 4)
                v.tensor_tensor(mrg2, acc_t, ga2, ALU.mult).then_inc(sem("acc_free"), 1)
                out_steps(4, 4)
                v.tensor_tensor(gc2, acc_t, gc2, ALU.mult).then_inc(sem("acc_free"), 1)
                eng.wait_ge(sem("acc_free"), 2 * l + 2)
                for half in range(2):
                    t = slice(4 * half, 4 * half + 4)
                    v.tensor_tensor(mrg2[:, t, :], mrg2[:, t, :], gc2[:, t, :], ALU.add).then_inc(sem("mrg2_full"), 1)
                split("mrg2", 2 * l, mrg2, 8)
                out_steps(8, 8)
                add_to_x(mod2(l, 2))
                if l == 0:
                    add_bias(Q_PROJ, Q_OUT)
                    scale2_of(0, 1)
                stage(eng, ST[f"out{l}"])

                norm(5 + 2 * l, nscale[:, 32 + 16 * l:40 + 16 * l], mod2(l, 3), nh, 4 + 2 * l)
                out_steps(16, 16, acc)
                steps(U + O_SK, 2)
                if l == 0:
                    q = N_BLOCKS - 1
                    take_block(q, st[:, 2 * (q % 2):, :])
                    add_bias(Q_OUT, N_BLOCKS)
                    scale2_of(1, 0)
                    scale2_of(1, 1)
                stage(eng, ST[f"wq{l}"])
                base = U + O_PEER

                paced = {"work": 0, "units": 0}

                def pace(n):
                    paced["work"] += n
                    while paced["units"] < HALF and paced["work"] >= PACE * (paced["units"] + 1):
                        step(base + paced["units"])
                        paced["units"] += 1

                def top16(src, vals, places, n, width):
                    for half in range(2):
                        at = slice(8 * half, 8 * half + 8)
                        for k in range(n):
                            ins = v.max(vals[:, k, at], src[:, k, :])
                            pace(width)
                        link(ins)
                        for k in range(n):
                            ins = v.max_index(places[:, k, at], vals[:, k, at], src[:, k, :])
                            pace(width)
                        link(ins)
                        if half == 0:
                            for k in range(n):
                                ins = v.match_replace(src[:, k, :], vals[:, k, at], src[:, k, :], -3.4028234e38)
                                pace(width)
                            link(ins)

                top16(scores, tv, ti, 32, NKEYS)
                link(v.tensor_copy(tif, ti))
                tv5 = tv.rearrange("p (g s) k -> p g s k", s=2)
                for t in range(TT):
                    g = slice(8 * t, 8 * t + 8)
                    ins = v.tensor_tensor(cand[:, g, :].rearrange("p g (a b) -> p g a b", b=TOPK),
                                          tv5[:, g, 0, :].unsqueeze(3).to_broadcast([P, 8, TOPK, TOPK]),
                                          tv5[:, g, 1, :].unsqueeze(2).to_broadcast([P, 8, TOPK, TOPK]), ALU.add)
                    pace(8 * TOPK * TOPK)
                link(ins)
                top16(cand, best, bpos, 16, TOPK * TOPK)
                v.tensor_tensor(ge_.rearrange("p (g k) -> p g k", k=TOPK), best,
                                best[:, :, 0:1].to_broadcast([P, 16, TOPK]), ALU.subtract).then_inc(sem("best_c"), 1)
                bp = bpos.rearrange("p a b -> p (a b)")
                v.tensor_single_scalar(pos_u[:, 0, :], bp, 4, ALU.logical_shift_right)
                link(v.tensor_single_scalar(pos_u[:, 1, :], bp, 15, ALU.bitwise_and))
                link(v.tensor_copy(pos_f, pos_u))
                tif5 = tif.rearrange("p (g s) k -> p g s k", s=2)
                iota16 = kc("iota16")

                def one_hot(r):
                    t, s = r // 2, r % 2
                    v.tensor_tensor(hot[:, s, :].rearrange("p (n a) -> p n a", a=TOPK),
                                    pos_f[:, s, 128 * t:128 * t + 128].unsqueeze(2).to_broadcast([P, PAIRS, TOPK]),
                                    iota16.unsqueeze(1).to_broadcast([P, PAIRS, TOPK]), ALU.is_equal)                        .then_inc(sem("place"), 1)
                    pace(PAIRS * TOPK)

                def key_number(r):
                    t, s = r // 2, r % 2
                    eng.wait_ge(sem("place_key"), 4 * l + r + 1)
                    link(v.tensor_reduce(sel3[:, s, 128 * t:128 * t + 128],
                                         hot[:, s, :].rearrange("p (n a) -> p n a", a=TOPK), AX, ALU.add))
                    pace(PAIRS * TOPK)

                one_hot(0)
                one_hot(1)
                for r in range(4):
                    key_number(r)
                    if r + 2 < 4:
                        one_hot(r + 2)
                while paced["units"] < HALF - EXP_BEFORE + 1:
                    pace(PACE)
                eng.wait_ge(sem("gexp"), l + 1)
                ge3 = ge_.rearrange("p (g k) -> p g k", k=TOPK)
                link(v.tensor_reduce(gsum, ge3, AX, ALU.add))
                link(v.reciprocal(ginv, gsum))
                v.tensor_tensor(sel3[:, 2, :].rearrange("p (g k) -> p g k", k=TOPK), ge3,
                                ginv.unsqueeze(2).to_broadcast([P, 16, TOPK]), ALU.mult).then_inc(sem("sel3"), 1)
                while paced["units"] < HALF:
                    pace(PACE)
                stage(eng, ST[f"peer_a{l}"])

                def build(k, half, g, i=None):
                    n = 2 * TURNS * l + TURNS * half + g
                    if g > 0:
                        eng.wait_ge(sem("g_psum"), plus(i, 2, n))
                    at = slice(GROUP * g, GROUP * g + GROUP) if i is None else                         bass.ds(i * (2 * GROUP) + GROUP * g, GROUP)
                    dst = (hot_l, hot_eq)[k]
                    width = (NKEYS, HALF)[k]
                    numbers = (kc("iota"), kc("iota")[:, HALF * half:HALF * half + HALF])[k]
                    v.tensor_tensor(dst, selt[:, k, at].unsqueeze(2).to_broadcast([P, GROUP, width]),
                                    numbers.unsqueeze(1).to_broadcast([P, GROUP, width]), ALU.is_equal)\
                        .then_inc(sem(("hot_l", "hot_eq")[k]), 1)

                def multiply(half, g, i=None):
                    n = 2 * TURNS * l + TURNS * half + g
                    eng.wait_ge(sem("g_psum"), plus(i, 2, n + 1))
                    at = slice(GROUP * g, GROUP * g + GROUP) if i is None else                         bass.ds(i * (2 * GROUP) + GROUP * g, GROUP)
                    here = experts[:, HALF * half:HALF * half + HALF, at].rearrange("p n t -> p t n")
                    v.tensor_tensor(here, here, st[:, 2 + g % 2, :].rearrange("p (t n) -> p t n", t=GROUP),
                                    ALU.mult).then_inc(sem("g_mult"), 1)

                def lower(n, i=None):
                    eng.wait_ge(sem("gated_hi"), plus(i, 4, NKEYS * l + n + 1))
                    src = experts[:, n, :] if i is None else                         experts[:, bass.ds(i * 4 + n, 1), :].rearrange("p a t -> p (a t)")
                    v.tensor_tensor(act_lo[:, n % 2, :], src, act_hi[:, n % 2, :], ALU.subtract)                        .then_inc(sem("gated_lo"), 1)

                def turns(half, turn):
                    turn(half, 0)
                    with eng.Fori(0, TURNS // 2 - 1) as i:
                        for g in range(2):
                            turn(half, 1 + g, i)
                    turn(half, TURNS - 1)
                    multiply(half, TURNS - 1)

                def u_turn(half, g, i=None):
                    u = base + HALF + 2 * g
                    build(1, half, g, i)
                    step(u, i, 4)
                    if g > 0:
                        multiply(half, g - 1, i)
                    build(0, half, g, i)
                    step(u + 1, i, 4)

                def v_turn(half, g, i=None):
                    u = base + NKEYS + 2 * g
                    if g < TURNS - 1:
                        lower(2 * g + 2, i)
                    build(1, half, g, i)
                    step(u, i, 4)
                    if g > 0:
                        multiply(half, g - 1, i)
                    if g < TURNS - 1:
                        lower(2 * g + 3, i)
                    build(0, half, g, i)
                    step(u + 1, i, 4)

                eng.wait_ge(sem("selt"), l + 1)
                link(v.tensor_copy(gate_parts[:, 0, :], selt[:, 2, :]))
                link(v.tensor_tensor(gate_rest[:, 0, :], selt[:, 2, :], gate_parts[:, 0, :], ALU.subtract))
                link(v.tensor_copy(gate_parts[:, 1, :], gate_rest[:, 0, :]))
                link(v.tensor_tensor(gate_rest[:, 1, :], gate_rest[:, 0, :], gate_parts[:, 1, :], ALU.subtract))
                link(v.tensor_copy(gate_parts[:, 2, :], gate_rest[:, 1, :]))
                turns(0, u_turn)
                stage(eng, ST[f"peer_b{l}"])
                lower(0)
                lower(1)
                turns(1, v_turn)
                stage(eng, ST[f"peer_c{l}"])
                v_base = base + NKEYS
                lower(HALF)
                lower(HALF + 1)
                with eng.Fori(0, HALF // 4 - 1) as i:
                    for k in range(4):
                        lower(HALF + k + 2, i)
                        step(v_base + HALF + k, i, 4)
                for n in range(NKEYS - 4, NKEYS):
                    if n + 2 < NKEYS:
                        lower(n + 2)
                    step(v_base + n)
                add_to_x(mod2(l, 5))
                stage(eng, ST[f"peer_d{l}"])
            norm(8, pc("final_g2"), None, nh)

        @block.gpsimd
        def _(eng):
            link = linker(eng, "pool_chain")
            g = nc.gpsimd
            def ada_loads(first, last):
                def load(n, i):
                    eng.wait_ge(ada_taken, i * ADA_RING + (n - ADA_RING + 1))
                    src = ada_weights[bass.ds(i * ADA_RING + n, 1), :, :].rearrange("a p n -> p (a n)")
                    eng.dma_start(ada_ring[:, n % ADA_RING, :], src).then_inc(ada_landed[n % ADA_RING], 16)

                with eng.Fori(0, (last - first) // ADA_RING) as i:
                    for k in range(ADA_RING):
                        load(first + k, i)

            def first_loads(first):
                for n in range(first, first + ADA_RING):
                    eng.dma_start(ada_ring[:, n % ADA_RING, :], ada_weights[n])\
                       .then_inc(ada_landed[n % ADA_RING], 16)

            first_loads(0)
            ada_loads(ADA_RING, 8 * Q_FFN[0])
            stage(eng, ST["ada"])
            ada_loads(8 * Q_FFN[0], 8 * Q_FFN[1])
            stage(eng, ST["ffn0"])
            for buf in (xp, pool_a, pool_b):
                ins = g.memset(buf[:, :, 0:PADP], 0.0)
            link(ins)
            eng.wait_ge(sem("proj_out"), 2)
            src = xp
            for k in range(NPOOL):
                dst = (pool_a, pool_b)[k % 2]
                w = 1 << k
                link(g.tensor_tensor(dst[:, k:NPOOL, PADP:PADP + T], src[:, k:NPOOL, PADP:PADP + T],
                                     src[:, k:NPOOL, PADP - w:PADP + T - w], ALU.add))
                src = dst
            eng.wait_ge(sem("k2_in"), 16)
            for k in range(NPOOL):
                ins = g.tensor_tensor(pooled[:, k, :], (pool_a, pool_b)[k % 2][:, k, PADP:PADP + T],
                                      inv_count[:, k, :], ALU.mult)
            link(ins)
            g.tensor_tensor(pooled, pooled, xp[:, :, PADP:PADP + T], ALU.subtract).then_inc(sem("pooled"), 1)
            stage(eng, ST["mix_proj"])
            stage(eng, ST["mix_pool"])
            stage(eng, ST["mix_norm"])
            stage(eng, ST["mix_heads"])
            for lv in range(LEVELS):
                if lv >= 2:
                    eng.wait_ge(sem("lv_x"), 4 * (lv - 1))
                if lv == 2:
                    eng.wait_ge(sem("lv_d"), 4)
                g.tensor_tensor(off_t[lv % 2], a_t, level_mask[:, lv, :].unsqueeze(1).to_broadcast([P, 16, P]),
                                ALU.mult).then_inc(sem("lv_off"), 1)
            for name in ("mix_solve", "mix_state", "mix_o", "mix_out"):
                stage(eng, ST[name])
            ada_loads(8 * Q_FFN[1], 8 * Q_PROJ)
            stage(eng, ST["ffn1"])
            first_loads(8 * Q_PROJ)
            stage(eng, ST["final1"])
            for l in range(LAYERS):
                if l == 0:
                    ada_loads(8 * Q_PROJ + ADA_RING, 8 * Q_OUT)
                stage(eng, ST[f"proj{l}"])
                link(g.memset(zc[:, :, 0:2], 0.0))
                g.tensor_tensor(zc[:, :, 2:2 + T], bch[:, 4:8, :], bch[:, 8:12, :], ALU.mult).then_inc(sem("zc"), 1)
                if l == 0:
                    first_loads(8 * Q_OUT)
                stage(eng, ST[f"attn{l}"])
                if l == 0:
                    ada_loads(8 * Q_OUT + ADA_RING, 8 * Q_OUT + 3 * 16 // 4)
                stage(eng, ST[f"out{l}"])
                if l == 0:
                    ada_loads(8 * Q_OUT + 3 * 16 // 4, 8 * N_BLOCKS)
                stage(eng, ST[f"wq{l}"])
                tif5 = tif.rearrange("p (g s) k -> p g s k", s=2)
                for r in range(4):
                    t, s = r // 2, r % 2
                    eng.wait_ge(sem("place"), 4 * l + r + 1)
                    hv = hot[:, s, :].rearrange("p (g k a) -> p g k a", k=TOPK, a=TOPK)
                    g.tensor_tensor(hv, hv, tif5[:, 8 * t:8 * t + 8, s, :].unsqueeze(2)
                                    .to_broadcast([P, 8, TOPK, TOPK]), ALU.mult).then_inc(sem("place_key"), 1)
                stage(eng, ST[f"peer_a{l}"])

                def weigh(half, n, i=None):
                    eng.wait_ge(sem("hot_eq"), plus(i, 1, 2 * TURNS * l + TURNS * half + n + 1))
                    at = slice(GROUP * n, GROUP * n + GROUP) if i is None else bass.ds(i * GROUP + GROUP * n, GROUP)
                    for k in range(3):
                        g.tensor_tensor(hot_r[k], hot_eq, gate_parts[:, k, at].unsqueeze(2)
                                        .to_broadcast([P, GROUP, HALF]), ALU.mult).then_inc(sem("hot_r"), 1)

                for half in range(2):
                    with eng.Fori(0, TURNS) as i:
                        weigh(half, 0, i)
                    stage(eng, ST[("peer_b", "peer_c")[half] + str(l)])
                stage(eng, ST[f"peer_d{l}"])
            eng.wait_ge(sem("normed"), DT)
            eng.dma_start(out, nh.rearrange("p a t -> p (a t)")).then_inc(sem("out"), 16)
            eng.wait_ge(sem("out"), 16)

        @block.tensor
        def _(eng):
            mm = nc.tensor.matmul

            def product(u, dst, hi_t, lo_t, i=None, per=0, first=False, last=False, shared=False, fresh=None):
                eng.wait_ge(hi_ready, plus(i, per, nth(u)))
                for t in range(DT):
                    w = w_hi[:, u % 2, t * P:(t + 1) * P]
                    start = first and (t == 0 if shared else t % 2 == 0)
                    if fresh is not None:
                        eng.wait_ge(sem("norm_lo"), DT * fresh + t + 1)
                    mm(dst(t), w, hi_t(t), start=start, stop=False, skip_group_check=True)
                    mm(dst(t), w, lo_t(t), start=False, stop=False, skip_group_check=True)
                eng.wait_ge(taken, plus(i, per, u + 1))
                for t in range(DT):
                    ins = mm(dst(t), w_lo[:, u % 2, t * P:(t + 1) * P], hi_t(t), start=False,
                             stop=last and (t == DT - 1 or not shared), skip_group_check=True)
                ins.then_inc(used, 1)

            def squares(n):
                for t in range(DT):
                    eng.wait_ge(sem("sq"), DT * n + t + 1)
                    ins = mm(st[:, 3, 0:T], ones, nh[:, t, :], start=t == 0, stop=t == DT - 1)
                ins.then_inc(sem("sumsq"), 1)

            def piece(q, r, dst, sums, i=None):
                eng.wait_ge(ada_taken, plus(i, 8, 8 * q + 8))
                mm(dst, ones, sums, start=True, stop=True, skip_group_check=True).then_inc(ada_piece, 1)

            def total(q, banks, reused=True):
                if reused:
                    eng.wait_ge(ada_diag, 4 * (q - 1))
                for r in range(4):
                    piece(q, r, quarter(banks, r), part[:, q % 2, r * T:(r + 1) * T])

            eng.wait_ge(sem("k1_in"), 16)
            for q in range(Q_FFN[0]):
                total(q, st[:, 2 * (q % 2):, :], reused=q >= 2)
            eng.wait_ge(sem("zrow"), 1)
            squares(0)
            stage(eng, ST["ada"])

            def clear_acc():
                for b in range(4):
                    mm(acc[:, b, :], zrow[0:1, :], zrow[0:1, :].unsqueeze(1).to_broadcast([1, 4, P]), start=True, stop=False,
                       skip_group_check=True)

            def accumulate(u, b, i=None, per=0, last=False):
                product(u, lambda t: acc_t[:, t, :], lambda t: act_hi[:, b, :], lambda t: act_lo[:, b, :],
                        i, per, last=last)

            def tile(dst, u, i=None, per=0, fresh=None):
                product(u, lambda t: dst, lambda t: h_hi[:, t, :], lambda t: h_lo[:, t, :], i, per,
                        first=True, last=True, shared=True, fresh=fresh)

            def ffn(f):
                clear_acc()
                base = (U_FFN1, U_FFN2)[f]

                def up(u, j, i=None, per=0, fresh=None):
                    tile(st[:, j, 0:T], u, i, per, fresh)
                    tile(st[:, 2 + j, 0:T], u + 1, i, per)

                q0 = Q_FFN[f]

                def body(j, i=None, per=0):
                    if j > 4:
                        t, r = (j - 1) // 4 - 1, (j - 1) % 4
                        sums = part_ffn[:, t, r * T:(r + 1) * T] if i is None else \
                            part_ffn[:, bass.ds(i * 1 + t, 1), r * T:(r + 1) * T].rearrange("p a n -> p (a n)")
                        piece(q0 + t, r, st[:, 2 + (j + 1) % 2, T:2 * T], sums, i)
                    up(base + 2 + 3 * j, (j + 1) % 2, i, per)
                    eng.wait_ge(sem("act_lo"), plus(i, 4, FT * f + j + 1))
                    accumulate(base + 4 + 3 * j, j % 2, i, per)

                up(base, 0, fresh=(0, 2)[f])
                for j in range(5):
                    body(j)
                with eng.Fori(0, (FT - 6) // 4) as i:
                    for j in range(4):
                        body(5 + j, i, 12)
                eng.wait_ge(sem("act_lo"), FT * f + FT)
                for r in range(4):
                    piece(q0 + 4, r, quarter(st[:, 2:4, :], r), part_ffn[:, 4, r * T:(r + 1) * T])
                accumulate(base + N_FFN - 1, (FT - 1) % 2, last=True)

            ffn(0)
            squares(1)
            stage(eng, ST["ffn0"])

            def pairs(base, n, sem_name, before, fresh, behind=None):
                for p in range(n):
                    if p >= 4:
                        eng.wait_ge(sem(sem_name), before + p - 3)
                    for k in range(2):
                        tile(st[:, p % 4, k * T:(k + 1) * T], base + 2 * p + k,
                             fresh=fresh if (p, k) == (0, 0) else None)
                        if behind is not None:
                            behind(2 * p + k)

            pairs(U_MIX, 26, "proj_out", 0, 1)
            eng.wait_ge(sem("sw_in"), 16)
            for t in range(TT):
                for k in range(DT):
                    for half in (h_hi, h_lo):
                        ins = mm(acc[:, 0, 16 * t:16 * t + 16], half[:, k, t * P:(t + 1) * P].bitcast(F32),
                                 w_ba[:, k, :], start=k == 0 and half is h_hi, stop=k == DT - 1 and half is h_lo)
            ins.then_inc(sem("ba_psum"), 1)
            stage(eng, ST["mix_proj"])

            def kmajor(base, n, at=0, waits=None, behind=None):
                for k in range(n):
                    if waits is not None:
                        eng.wait_ge(*waits(k))
                    product(base + k, lambda t: acc_t[:, t, :], lambda t: h_hi[:, at + k, :],
                            lambda t: h_lo[:, at + k, :], first=k == 0, last=k == n - 1)
                    if behind is not None:
                        behind(k)

            eng.wait_ge(sem("pooled"), 1)
            for k in range(NPOOL):
                ins = mm(st[:, k // 2, (k % 2) * T:(k % 2) * T + T], w_pool[:, k, :], pooled[:, k, :],
                         start=True, stop=True)
            ins.then_inc(sem("pool_mm"), 1)
            kmajor(U_POOLP, 4, waits=lambda k: (sem("ya0_lo"), k + 1))
            stage(eng, ST["mix_pool"])

            eng.wait_ge(sem("sq_qk"), 1)
            eng.wait_ge(sem("k2_in"), 16)
            onecol = kc("onecol")
            for h in range(16):
                ins = mm(st[0:16, 0, 0:T], onecol[:, 15 - h:31 - h], sq_qk[:, h, :], start=h == 0, stop=h == 15)
            ins.then_inc(sem("sum_qk"), 1)
            for c in range(2):
                mm(st[0:8, 1, c * P:(c + 1) * P], ba_g[:, c, :], upto, start=True, stop=True)
                mm(st[0:8, 1, T + c * P:T + (c + 1) * P], ba_b[:, c, :], ident, start=True, stop=True)
            for c in range(2):
                ins = mm(st[:, 2, 8 * c:8 * c + 8], upto, ba_g[:, c, :], start=True, stop=True)
            ins.then_inc(sem("g_rows"), 1)
            eng.wait_ge(sem("rn"), 1)
            for m in range(8):
                if m >= 4:
                    eng.wait_ge(sem("qk_n"), m - 3)
                for k in range(2):
                    ins = mm(acc[:, m % 4, k * T:(k + 1) * T], select[0:16, 2 * m + k, :], rn[0:16, :],
                             start=True, stop=True)
                ins.then_inc(sem("rn_b"), 1)
            stage(eng, ST["mix_norm"])

            for h in range(HEADS):
                b = h % 2
                if h >= 2:
                    eng.wait_ge(sem("head"), h - 1)
                mm(st[:, b, :], select[0:8, h, :], rows[0:8, :], start=True, stop=True).then_inc(sem("bc"), 1)
                for c in range(2):
                    ck = slice(c * P, (c + 1) * P)
                    mm(st[:, 2 + b, c * P:(c + 1) * P], qkv[:, 8 + h, ck], qkv[:, 8 + h, ck], start=True, stop=True)
                    ins = mm(st[:, 2 + b, T + c * P:T + (c + 1) * P], qkv[:, 8 + h, ck], qkv[:, h, ck],
                             start=True, stop=True)
                ins.then_inc(sem("kkqk"), 1)
            for q in range(6):
                if q >= 4:
                    eng.wait_ge(sem("tok_out"), q - 3)
                for j in range(4):
                    n = 4 * q + j
                    src = qkv[:, 16 + n % 8, (n // 8) * P:(n // 8 + 1) * P] if n < 16 else qkv[:, 8 + n - 16, 0:P]
                    ins = nc.tensor.transpose(acc[:, q % 4, j * P:(j + 1) * P], src, ident)
                ins.then_inc(sem("tok_t"), 1)
            stage(eng, ST["mix_heads"])

            for lv in range(LEVELS):
                eng.wait_ge(sem("lv_off"), lv + 1)
                for g in range(4):
                    if lv >= 1:
                        eng.wait_ge(sem("lv_d"), 4 * (lv - 1) + g + 1)
                    for k in range(4):
                        ins = mm(st[:, g, k * P:(k + 1) * P], off_t[lv % 2][:, 4 * g + k, :], d_m[:, 4 * g + k, :],
                                 start=True, stop=True)
                    ins.then_inc(sem("lv_x"), 1)
                if lv == 0:
                    continue
                for g in range(4):
                    b = 2 * (g % 2)
                    eng.wait_ge(sem("lv_d"), 4 * lv + g - 1)
                    eng.wait_ge(sem("lv_xs"), 4 * (lv - 1) + g + 1)
                    for k in range(4):
                        n = 4 * g + k
                        if lv < LEVELS - 1:
                            mm(acc[:, b, k * P:(k + 1) * P], d_t[:, n, :], x_s[:, n, :], start=True, stop=True)
                        ins = mm(acc[:, b + 1, k * P:(k + 1) * P], x_s[:, n, :], d_t[:, n, :], start=True, stop=True)
                    ins.then_inc(sem("lv_dx"), 1)
            stage(eng, ST["mix_solve"])

            def four(bank, g, name, lhs, rhs):
                for k in range(4):
                    h = 4 * g + k
                    ins = mm(bank[:, k * P:(k + 1) * P], lhs(h), rhs(h), start=True, stop=True)
                ins.then_inc(sem(name), 1)

            for g in range(2):
                four(acc[:, g, :], g, "vn0_psum", lambda h: d_t[:, h, :], lambda h: bv[:, h, :])
            for g in range(2):
                eng.wait_ge(sem("vn0"), g + 1)
                four(acc[:, 2 + g, :], g, "s1_psum", lambda h: k_dec[:, h, :], lambda h: v_new[:, h, :])
            for g in range(2):
                eng.wait_ge(sem("s1"), g + 1)
                four(st[:, g, :], g, "ks1_psum", lambda h: qkv[:, 8 + h, 128:256], lambda h: s1[:, h, :])
            for g in range(2):
                eng.wait_ge(sem("resid"), g + 1)
                four(acc[:, g, :], g, "vn1_psum", lambda h: d_t[:, 8 + h, :], lambda h: resid[:, h, :])
            for m in range(4):
                eng.wait_ge(sem("vn1"), m // 2 + 1)
                if m == 0:
                    eng.wait_ge(sem("resid"), 2)
                for k in range(2):
                    h = 2 * m + k
                    o = st[:, m, k * T:(k + 1) * T]
                    mm(o[:, 0:128], v_new[:, h, :], qk_m[:, h, :], start=True, stop=True)
                    mm(o[:, 128:256], v_new[:, 8 + h, :], qk_m[:, 8 + h, :], start=True, stop=False)
                    ins = mm(o[:, 128:256], s1[:, h, :], q_dec[:, h, :], start=False, stop=True)
                ins.then_inc(sem("o_psum"), 1)
            stage(eng, ST["mix_state"])
            eng.wait_ge(sem("sq_o"), 1)
            for h in range(8):
                ins = mm(st[0:8, 0, 0:T], onecol[:, 15 - h:23 - h], sq_o[:, h, :], start=h == 0, stop=h == 7)
            ins.then_inc(sem("sum_o"), 1)
            eng.wait_ge(sem("rn_o"), 1)
            for m in range(4):
                for k in range(2):
                    ins = mm(acc[:, m, k * T:(k + 1) * T], select[0:8, 2 * m + k, :], rn[0:8, :],
                             start=True, stop=True)
                ins.then_inc(sem("rno_b"), 1)
            stage(eng, ST["mix_o"])
            kmajor(U_DNP, 8, waits=lambda k: (sem("o_lo"), k // 4 + 1))
            kmajor(U_MIXO, 8, waits=lambda k: (sem("merged_lo"), k // 4 + 1))
            squares(2)
            stage(eng, ST["mix_out"])

            ffn(1)
            squares(3)
            stage(eng, ST["ffn1"])
            squares(4)
            stage(eng, ST["final1"])

            for l in range(LAYERS):
                U = U_L2 + N_L2 * l

                def behind_proj(k):
                    if l == 0 and k % 8 == 1 and k > 8:
                        q = Q_PROJ + k // 8 - 1
                        total(q, acc[:, 2 * (q % 2):, :])

                pairs(U + O_QK, 20, "proj2", 20 * l, 3 + 2 * l, behind_proj)
                stage(eng, ST[f"proj{l}"])

                def scores_of(h):
                    b, r = h % 2, slice(64 * (h % 2), 64 * (h % 2) + 64)
                    if h >= 2:
                        eng.wait_ge(sem("smax"), AH * l + h - 1)
                    for q in range(2):
                        ins = mm(st[:, b, q * T:(q + 1) * T], qk2[r, h // 2, q * P:(q + 1) * P],
                                 qk2[r, 4 + h // 2, :], start=True, stop=True)
                    ins.then_inc(sem("s_psum"), 1)

                def values_of(h):
                    b = h % 2
                    eng.wait_ge(sem("p"), AH * l + h + 1)
                    if h >= 2:
                        eng.wait_ge(sem("pt"), AH * l + h - 1)
                    nc.tensor.transpose(acc[:, b, 0:128], p_b[b][:, 0, 0:128], ident)
                    nc.tensor.transpose(acc[:, b, 128:256], p_b[b][:, 1, 0:128], ident)
                    nc.tensor.transpose(acc[:, b, 256:384], p_b[b][:, 1, 128:256], ident)\
                        .then_inc(sem("pt_psum"), 1)
                    eng.wait_ge(sem("pt"), AH * l + h + 1)
                    m = h // 2
                    o = acc[64 * b:64 * b + 64, 2 + m // 2, (m % 2) * T:(m % 2) * T + T]
                    mm(o[:, 0:128], v2[:, 0, 64 * h:64 * h + 64], pt_b[b][:, 0:128], start=True, stop=True)
                    mm(o[:, 128:256], v2[:, 0, 64 * h:64 * h + 64], pt_b[b][:, 128:256], start=True, stop=False)
                    mm(o[:, 128:256], v2[:, 1, 64 * h:64 * h + 64], pt_b[b][:, 256:384], start=False, stop=True)\
                        .then_inc(sem("pv"), 1)

                for t in range(TT):
                    for n in range(4):
                        ins = nc.tensor.transpose(acc[:, t, n * P:(n + 1) * P], vt[:, n, t * P:(t + 1) * P], ident)
                ins.then_inc(sem("v_tok"), 1)
                scores_of(0)
                eng.wait_ge(sem("v2"), l + 1)
                for h in range(AH):
                    if h + 1 < AH:
                        scores_of(h + 1)
                    values_of(h)
                stage(eng, ST[f"attn{l}"])

                def behind_out(k, banks=st):
                    if l == 0 and k + 1 in OUT_TAKES:
                        q = OUT_TAKES[k + 1]
                        total(q, banks[:, 2 * (q % 2):, :])

                kmajor(U + O_AP, 4, behind=behind_out)
                eng.wait_ge(sem("acc_free"), 2 * l + 1)
                kmajor(U + O_CP, 4, at=4, behind=lambda k: behind_out(4 + k))
                kmajor(U + O_OUT, 8, waits=lambda k: (sem("mrg2_lo"), 2 * l + k // 4 + 1),
                       behind=lambda k: behind_out(8 + k))
                squares(5 + 2 * l)
                stage(eng, ST[f"out{l}"])

                pairs(U + O_WQ, 8, "qq", 8 * l, 4 + 2 * l, lambda k: behind_out(16 + k, acc))
                eng.wait_ge(sem("qq"), 8 * l + 8)
                for u in range(2):
                    n_u = U + O_SK + u
                    eng.wait_ge(taken, n_u + 1)
                    for t in range(TT):
                        for half in range(2):
                            if u == 1:
                                eng.wait_ge(sem("scores"), 8 * l + 2 * t + half + 1)
                            for k in range(4):
                                n = 4 * half + k
                                for part_ in (w_hi, w_lo):
                                    w = part_[:, n_u % 2, n * P:(n + 1) * P].bitcast(F32)
                                    ins = mm(acc[:, 2 * t + half, k * P:(k + 1) * P],
                                             qq[:, 8 * u + n, t * P:(t + 1) * P], w,
                                             start=part_ is w_hi, stop=part_ is w_lo)
                            ins.then_inc(used if (t, half) == (1, 1) else sem("sk"), 1)
                if l == 0:
                    q = N_BLOCKS - 1
                    total(q, st[:, 2 * (q % 2):, :])
                stage(eng, ST[f"wq{l}"])
                base = U + O_PEER
                n_key = NKEYS * l

                def u_tile(n, i=None):
                    if n_key + n >= 2:
                        eng.wait_ge(sem("gelu"), plus(i, 4, n_key + n - 1))
                    tile(st[:, n % 2, 0:T], base + n, i, 4)

                for n in range(4):
                    u_tile(n)
                with eng.Fori(0, HALF // 4 - 1) as i:
                    for k in range(4):
                        u_tile(4 + k, i)
                eng.wait_ge(sem("sel3"), l + 1)
                for k in range(3):
                    for t in range(TT):
                        at = k * T + t * P
                        ins = nc.tensor.transpose(st[:, 2 + at // 512, at % 512:at % 512 + P],
                                                  sel3[:, k, t * P:(t + 1) * P], ident)
                ins.then_inc(sem("sel_psum"), 1)
                stage(eng, ST[f"peer_a{l}"])

                def token_gates(half, g, i=None):
                    n = 2 * TURNS * l + TURNS * half + g
                    eng.wait_ge(sem("hot_l"), plus(i, 2, n + 1))
                    eng.wait_ge(sem("hot_r"), plus(i, 6, 3 * n + 3))
                    if n >= 2:
                        eng.wait_ge(sem("g_mult"), plus(i, 2, n - 1))
                    for k in range(GROUP):
                        for part_ in range(3):
                            ins = mm(st[:, 2 + g % 2, k * HALF:(k + 1) * HALF], hot_l[:, k, :],
                                     hot_r[part_][:, k, :], start=part_ == 0, stop=part_ == 2)
                    ins.then_inc(sem("g_psum"), 1)

                def turns(half, unit):
                    unit(0)
                    unit(1)
                    with eng.Fori(0, TURNS // 2 - 1) as i:
                        for g in range(2):
                            unit(2 + 2 * g, i)
                            token_gates(half, g, i)
                            unit(3 + 2 * g, i)
                    unit(HALF - 2)
                    token_gates(half, TURNS - 2)
                    unit(HALF - 1)
                    token_gates(half, TURNS - 1)

                def v_unit(n, i=None):
                    eng.wait_ge(sem("gated_lo"), plus(i, 4, n_key + n + 1))
                    accumulate(base + NKEYS + n, n % 2, i, 4, last=n == NKEYS - 1)

                turns(0, lambda n, i=None: u_tile(HALF + n, i))
                stage(eng, ST[f"peer_b{l}"])
                clear_acc()
                turns(1, v_unit)
                stage(eng, ST[f"peer_c{l}"])
                with eng.Fori(0, HALF // 4 - 1) as i:
                    for k in range(4):
                        v_unit(HALF + k, i)
                for n in range(NKEYS - 4, NKEYS):
                    v_unit(n)
                squares(6 + 2 * l)
                stage(eng, ST[f"peer_d{l}"])


def _columns(a):
    return np.asarray(a).reshape(-1, P).T


def _out_tiles(w):
    return w.reshape(8, P, -1, P).transpose(2, 1, 0, 3).reshape(-1, P, UNIT)


def _row_tiles(w):
    return w.reshape(-1, P, UNIT)


def _ada_weights(a):
    mats = [a["ada_w"][0]] + [a["w_ada_2"][l] for l in range(LAYERS)]
    return np.concatenate([w.reshape(8, P, -1, UNIT).transpose(2, 0, 1, 3).reshape(-1, P, UNIT) for w in mats])


def _constants():
    f = np.arange(P)
    tok = np.arange(T)
    dist = tok[:, None] - tok[None, :]
    dist = np.where(dist >= 0, dist, -NEG).astype(np.float32).reshape(TT, P, T).transpose(1, 0, 2).reshape(P, -1)
    onecol = np.zeros((P, 31), np.float32)
    onecol[:, 15] = 1
    is_q = (f < HEADS)[:, None]
    one = np.ones((P, 1), np.float32)
    parts = dict(ident=np.eye(P), ones=np.ones((P, P)), iota=np.tile(f, (P, 1)), dist=dist, onecol=onecol,
                 iota16=np.tile(np.arange(16), (P, 1)), eps=one * 1e-6, qk_scale=np.where(is_q, 128.0, 1.0),
                 qk_eps=np.where(is_q, 128e-6, 1e-6))
    k1 = np.concatenate([parts[n] for n in _K1], 1).astype(np.float32)
    j, i = f[:, None], f[None, :]
    levels = [((j // (2 * b) == i // (2 * b)) & (j % (2 * b) < b) & (i % (2 * b) >= b)) for b in
              (1 << lv for lv in range(LEVELS))]
    inv = np.concatenate([1.0 / np.minimum(tok + 1, w) for w in POOL_WINDOWS])
    select = np.zeros((P, 16, P))
    for h in range(16):
        select[h, h] = 1
    parts = dict(upto=j <= i, future=np.where(j <= i, 0, NEG), levels=np.concatenate(levels, 1),
                 inv_count=np.tile(inv, (P, 1)), select=select.reshape(P, -1))
    k2 = np.concatenate([parts[n] for n in _K2], 1).astype(np.float32)
    return k1, k2


def _weights(a):
    w = np.empty((N_UNITS, P, UNIT), np.float32)

    def put(at, units):
        w[at:at + len(units)] = units

    for base, w_in, w_out in ((U_FFN1, "ffn1_w_in", "ffn1_w_out"), (U_FFN2, "ffn2_w_in", "ffn2_w_out")):
        up = _out_tiles(a[w_in][0])
        down = _row_tiles(a[w_out][0])
        w[base] = up[0]
        w[base + 1] = up[FT]
        w[base + 2:base + N_FFN - 1:3] = up[1:FT]
        w[base + 3:base + N_FFN - 1:3] = up[FT + 1:]
        w[base + 4:base + N_FFN - 1:3] = down[:FT - 1]
        w[base + N_FFN - 1] = down[FT - 1]
    m = a["mix_w_in"][0]
    ba = 512 + 4 * D
    put(U_MIX, _out_tiles(m[:, :ba]))
    put(U_MIX + 36, _out_tiles(m[:, ba + 16:]))
    small_ba = m[:, ba:ba + 16].reshape(8, P, 16).transpose(1, 0, 2).reshape(P, -1)
    pool_w = a["pool_w"][0].transpose(1, 0, 2).reshape(P, -1)
    put(U_POOLP, _row_tiles(a["pool_proj"][0]))
    put(U_DNP, _row_tiles(a["dn_proj"][0]))
    put(U_MIXO, _row_tiles(a["mix_w_out"][0]))
    for l in range(LAYERS):
        U = U_L2 + l * N_L2
        tiles = _out_tiles(a["w_in_2"][l])
        put(U + O_QK, tiles[0:8])
        put(U + O_V, tiles[8:12])
        put(U + O_REST, tiles[12:])
        put(U + O_AP, _row_tiles(a["w_attn_proj_2"][l]))
        put(U + O_CP, _row_tiles(a["w_conv_proj_2"][l]))
        put(U + O_OUT, _row_tiles(a["w_out_2"][l]))
        put(U + O_WQ, _out_tiles(a["w_query_2"][l]))
        keys = a["sub_keys_2"][l].reshape(16, NKEYS, P).transpose(2, 0, 1).reshape(P, 2, UNIT)
        put(U + O_SK, keys.transpose(1, 0, 2))
        u = a["expert_u_2"][l].reshape(NKEYS, NKEYS, 8, P).transpose(1, 3, 2, 0)
        v = a["expert_v_2"][l].reshape(NKEYS, NKEYS, D).transpose(1, 0, 2)
        base = U + O_PEER
        put(base, u.reshape(NKEYS, P, UNIT))
        put(base + NKEYS, v)
    return w, np.concatenate([small_ba, pool_w], 1)


def kernel(**inputs):
    import concourse.bacc as bacc
    from concourse.bass_utils import run_bass_kernel_spmd

    a = {n: np.asarray(x) for n, x in inputs.items()}
    weights, smallw = _weights(a)

    def row(name):
        return np.broadcast_to(a[name].reshape(1, -1), (P, a[name].size))

    cols = dict(c=_columns(a["c"]), c2=_columns(a["c_2"]), ada_b=_columns(a["ada_b"]), b_ada2=_columns(a["b_ada_2"]),
                norm_g=_columns(a["norm_g"]), final_g=_columns(a["final_g"]), conv_w=_columns(a["conv_w"]),
                pool_scale=_columns(a["pool_scale"]), dn_g=_columns(a["dn_norm_g"]), a_log=row("a_log"),
                dt_bias=row("dt_bias"), n1g2=_columns(a["norm1_g_2"]), n2g2=_columns(a["norm2_g_2"]),
                conv_w2=_columns(a["conv_w_2"]), final_g2=_columns(a["final_g_2"]))
    x = a["x"][0].reshape(T, DT, P).transpose(2, 1, 0).reshape(P, -1)
    params = np.concatenate([cols[n] for n in _COLS] + [x], 1)
    k1, k2 = _constants()
    arrays = {"weights": weights, "ada_weights": _ada_weights(a), "params": params, "const1": k1, "const2": k2, "smallw": smallw}
    arrays = {n: np.ascontiguousarray(v, dtype=np.float32) for n, v in arrays.items()}

    nc = bacc.Bacc("TRN2", target_bir_lowering=False, num_devices=1)
    args = [nc.dram_tensor(n, v.shape, F32, kind="ExternalInput").ap() for n, v in arrays.items()]
    out = nc.dram_tensor("out", (P, DT * T), F32, kind="ExternalOutput").ap()
    build(nc, *args, out)
    r = run_bass_kernel_spmd(nc, [arrays], core_ids=[0])
    y = np.asarray(r.results[0]["out"])
    return y.reshape(P, DT, T).transpose(2, 1, 0).reshape(1, T, D)
```
